# Optimizing a Trainium2 kernel written in Bass

```python
import math
import jax, jax.numpy as jnp
from jax import lax
import numpy as np

D_MODEL = 1024
BATCH = 1
SEQ = 512
DEPTH = 2

D_MIX = D_MODEL
N_MIXERS = 4
GROUP_W = D_MIX // N_MIXERS
Q_BLOCK = 128
EPS = 1e-6

MOBA_HEADS = 4
MOBA_HD = GROUP_W // MOBA_HEADS
MOBA_BLOCK = 256
MOBA_TOPK = 3

SSM_HEADS = 4
SSM_HD = GROUP_W // SSM_HEADS
SSM_STATE = 128
SSM_GROUPS = 2
SSM_CONV = 4
SSM_CHUNK = 128
SSM_XBC = GROUP_W + 2 * SSM_GROUPS * SSM_STATE

MLSTM_HEADS = 4
MLSTM_HD = GROUP_W // MLSTM_HEADS
MLSTM_CONV = 4
MLSTM_CHUNK = 128

MLA_HEADS = 4
MLA_Q_LORA = 256
MLA_KV_LORA = 128
MLA_NOPE = 64
MLA_ROPE = 32
MLA_V = GROUP_W // MLA_HEADS
ROPE_THETA = 10000.0

N_EXPERT_GROUPS = 4
EXPERTS_PER_GROUP = 4
N_EXPERTS = N_EXPERT_GROUPS * EXPERTS_PER_GROUP
TOP_K_IN_GROUP = 2
D_EXPERT = 256

IN_SIZES = (3 * GROUP_W,
            GROUP_W,
            SSM_XBC,
            SSM_HEADS,
            2 * GROUP_W,
            GROUP_W,
            MLSTM_HEADS,
            MLSTM_HEADS,
            GROUP_W,
            MLA_Q_LORA,
            MLA_KV_LORA,
            MLA_ROPE)
N_IN = sum(IN_SIZES)

kernel_name = 'hybrid_moba_ssd_mlstm_mla_hmoe'

F32 = jnp.float32

def rms_norm(x, g):
    xf = x.astype(F32)
    y = xf * lax.rsqrt(jnp.mean(xf * xf, axis=-1, keepdims=True) + EPS)
    return (y * g.astype(F32)).astype(x.dtype)

def causal_conv(x, w, b):
    k = w.shape[0]
    y = lax.conv_general_dilated(x, w[:, None, :].astype(x.dtype), window_strides=(1,),
                                 padding=[(k - 1, 0)], dimension_numbers=('NWC', 'WIO', 'NWC'),
                                 feature_group_count=x.shape[-1])
    return y + b.astype(x.dtype)

def rope_tables(positions):
    inv = ROPE_THETA ** (-jnp.arange(0, MLA_ROPE, 2, dtype=F32) / MLA_ROPE)
    ang = positions.astype(F32)[..., None] * inv
    return jnp.cos(ang), jnp.sin(ang)

def apply_rope(x, cos, sin):
    half = x.shape[-1] // 2
    x1 = x[..., :half].astype(F32)
    x2 = x[..., half:].astype(F32)
    return jnp.concatenate([x1 * cos - x2 * sin, x2 * cos + x1 * sin], axis=-1).astype(x.dtype)

def moba_attention(q, k, v):
    bsz, s, h, dh = q.shape
    nb = -(-s // MOBA_BLOCK)
    pad = nb * MOBA_BLOCK - s
    topk = min(MOBA_TOPK, nb)
    nq = s // Q_BLOCK
    scale = dh ** -0.5
    kb = jnp.pad(k, ((0, 0), (0, pad), (0, 0), (0, 0))).reshape(bsz, nb, MOBA_BLOCK, h, dh).transpose(0, 3, 1, 2, 4)
    vb = jnp.pad(v, ((0, 0), (0, pad), (0, 0), (0, 0))).reshape(bsz, nb, MOBA_BLOCK, h, dh).transpose(0, 3, 1, 2, 4)
    k_mean = jnp.mean(kb.astype(F32), axis=3)
    q_blocks = q.reshape(bsz, nq, Q_BLOCK, h, dh).transpose(1, 0, 3, 2, 4)
    take_blocks = jax.vmap(jax.vmap(lambda blocks, idx: blocks[idx]))

    def one_block(args):
        ci, qi = args
        q_pos = ci * Q_BLOCK + jnp.arange(Q_BLOCK)
        cur = (ci * Q_BLOCK) // MOBA_BLOCK
        gate = jnp.einsum('bhqd,bhnd->bhqn', qi.astype(F32), k_mean)
        gate = jnp.where(jnp.arange(nb) < cur, gate, -jnp.inf)
        _, sel = lax.top_k(gate, topk)
        valid = sel < cur
        k_sel = take_blocks(kb, sel)
        v_sel = take_blocks(vb, sel)
        s_sel = jnp.einsum('bhqd,bhqnjd->bhqnj', qi, k_sel).astype(F32) * scale
        s_sel = jnp.where(valid[..., None], s_sel, -jnp.inf).reshape(bsz, h, Q_BLOCK, topk * MOBA_BLOCK)
        k_own = lax.dynamic_index_in_dim(kb, cur, axis=2, keepdims=False)
        v_own = lax.dynamic_index_in_dim(vb, cur, axis=2, keepdims=False)
        k_pos = cur * MOBA_BLOCK + jnp.arange(MOBA_BLOCK)
        s_own = jnp.einsum('bhqd,bhjd->bhqj', qi, k_own).astype(F32) * scale
        s_own = jnp.where(k_pos[None, :] <= q_pos[:, None], s_own, -jnp.inf)
        p = jax.nn.softmax(jnp.concatenate([s_sel, s_own], axis=-1), axis=-1).astype(v.dtype)
        p_sel = p[..., :topk * MOBA_BLOCK].reshape(bsz, h, Q_BLOCK, topk, MOBA_BLOCK)
        p_own = p[..., topk * MOBA_BLOCK:]
        return (jnp.einsum('bhqnj,bhqnjd->bhqd', p_sel, v_sel)
                + jnp.einsum('bhqj,bhjd->bhqd', p_own, v_own))

    out = lax.map(one_block, (jnp.arange(nq), q_blocks))
    return out.transpose(1, 0, 3, 2, 4).reshape(bsz, s, h * dh)

def mamba2_ssd(z, xbc, dt_raw, conv_w, conv_b, dt_bias, a_log, d_skip, norm_g):
    bsz, s, _ = xbc.shape
    hh, pp, nn, ll = SSM_HEADS, SSM_HD, SSM_STATE, SSM_CHUNK
    nc = s // ll
    xbc = jax.nn.silu(causal_conv(xbc, conv_w, conv_b)).astype(F32)
    x = xbc[..., :GROUP_W].reshape(bsz, s, hh, pp)
    rep = hh // SSM_GROUPS
    bm = jnp.repeat(xbc[..., GROUP_W:GROUP_W + SSM_GROUPS * nn].reshape(bsz, s, SSM_GROUPS, nn), rep, axis=2)
    cm = jnp.repeat(xbc[..., GROUP_W + SSM_GROUPS * nn:].reshape(bsz, s, SSM_GROUPS, nn), rep, axis=2)
    dt = jax.nn.softplus(dt_raw.astype(F32) + dt_bias.astype(F32))
    a = -jnp.exp(a_log.astype(F32))
    xc = x.reshape(bsz, nc, ll, hh, pp)
    bc = bm.reshape(bsz, nc, ll, hh, nn)
    cc = cm.reshape(bsz, nc, ll, hh, nn)
    dtc = dt.reshape(bsz, nc, ll, hh)
    a_cum = jnp.cumsum(dtc * a, axis=2)
    causal = jnp.tril(jnp.ones((ll, ll), dtype=bool))
    seg = a_cum[:, :, :, None, :] - a_cum[:, :, None, :, :]
    decay_in = jnp.exp(jnp.where(causal[None, None, :, :, None], seg, -jnp.inf))
    xdt = xc * dtc[..., None]
    scores = jnp.einsum('bclhn,bcshn->bclsh', cc, bc) * decay_in
    y_diag = jnp.einsum('bclsh,bcshp->bclhp', scores, xdt)
    decay_out = jnp.exp(a_cum[:, :, -1:, :] - a_cum)
    chunk_states = jnp.einsum('bclhn,bclh,bclhp->bchpn', bc, decay_out, xdt)
    chunk_decay = jnp.exp(a_cum[:, :, -1, :])

    def carry_state(state, inp):
        st, dec = inp
        return state * dec[:, :, None, None] + st, state

    _, prev = lax.scan(carry_state, jnp.zeros((bsz, hh, pp, nn), F32),
                       (jnp.moveaxis(chunk_states, 1, 0), jnp.moveaxis(chunk_decay, 1, 0)))
    prev = jnp.moveaxis(prev, 0, 1)
    y_off = jnp.einsum('bclhn,bchpn,bclh->bclhp', cc, prev, jnp.exp(a_cum))
    y = (y_diag + y_off).reshape(bsz, s, hh, pp) + x * d_skip.astype(F32)[:, None]
    y = y.reshape(bsz, s, GROUP_W) * jax.nn.silu(z.astype(F32))
    gsz = GROUP_W // SSM_GROUPS
    y = rms_norm(y.reshape(bsz, s, SSM_GROUPS, gsz), norm_g.reshape(SSM_GROUPS, gsz))
    return y.reshape(bsz, s, GROUP_W).astype(z.dtype)

def mlstm_mixer(qk, v, i_pre, f_pre, o_pre, conv_w, conv_b, ig_bias, fg_bias, norm_g):
    bsz, s, _ = v.shape
    hh, dd, ll = MLSTM_HEADS, MLSTM_HD, MLSTM_CHUNK
    nc = s // ll
    qk = jax.nn.silu(causal_conv(qk, conv_w, conv_b)).astype(F32)
    q = qk[..., :GROUP_W]
    k = qk[..., GROUP_W:] * (dd ** -0.5)

    def heads(t):
        return t.reshape(bsz, nc, ll, hh, dd).transpose(1, 0, 3, 2, 4)

    def gates(t):
        return t.reshape(bsz, nc, ll, hh).transpose(1, 0, 3, 2)

    qc, kc, vc = heads(q), heads(k), heads(v.astype(F32))
    igc = gates(i_pre.astype(F32) + ig_bias.astype(F32))
    lfc = gates(jax.nn.log_sigmoid(f_pre.astype(F32) + fg_bias.astype(F32)))
    causal = jnp.tril(jnp.ones((ll, ll), dtype=bool))

    def chunk_step(carry, inp):
        c_st, n_st, m_st = carry
        qb, kb, vb, ig, lf = inp
        b = jnp.cumsum(lf, axis=-1)
        dmat = jnp.where(causal, b[..., :, None] - b[..., None, :] + ig[..., None, :], -jnp.inf)
        inter = b + m_st[..., None]
        m_t = jnp.maximum(inter, jnp.max(dmat, axis=-1))
        sc = jnp.einsum('bhld,bhsd->bhls', qb, kb) * jnp.exp(dmat - m_t[..., None])
        w_inter = jnp.exp(inter - m_t)
        num = jnp.einsum('bhls,bhse->bhle', sc, vb) + w_inter[..., None] * jnp.einsum('bhld,bhde->bhle', qb, c_st)
        den = jnp.sum(sc, axis=-1) + w_inter * jnp.einsum('bhld,bhd->bhl', qb, n_st)
        h = num / jnp.maximum(jnp.abs(den), jnp.exp(-m_t))[..., None]
        g = b[..., -1:] - b + ig
        m_new = jnp.maximum(b[..., -1] + m_st, jnp.max(g, axis=-1))
        w_state = jnp.exp(g - m_new[..., None])
        keep = jnp.exp(b[..., -1] + m_st - m_new)
        c_new = keep[..., None, None] * c_st + jnp.einsum('bhs,bhsd,bhse->bhde', w_state, kb, vb)
        n_new = keep[..., None] * n_st + jnp.einsum('bhs,bhsd->bhd', w_state, kb)
        return (c_new, n_new, m_new), h

    init = (jnp.zeros((bsz, hh, dd, dd), F32), jnp.zeros((bsz, hh, dd), F32), jnp.zeros((bsz, hh), F32))
    _, hs = lax.scan(chunk_step, init, (qc, kc, vc, igc, lfc))
    h = hs.transpose(1, 0, 3, 2, 4).reshape(bsz, s, hh, dd)
    h = jax.nn.sigmoid(o_pre.astype(F32)).reshape(bsz, s, hh, dd) * h
    h = rms_norm(h, norm_g.reshape(hh, dd))
    return h.reshape(bsz, s, GROUP_W).astype(v.dtype)

def mla_attention(c_q, c_kv, k_rope, cos, sin, q_norm_g, w_uq, kv_norm_g, w_ukv):
    bsz, s, _ = c_q.shape
    nq = s // Q_BLOCK
    hh = MLA_HEADS
    q = (rms_norm(c_q, q_norm_g) @ w_uq).reshape(bsz, s, hh, MLA_NOPE + MLA_ROPE)
    kv = (rms_norm(c_kv, kv_norm_g) @ w_ukv).reshape(bsz, s, hh, MLA_NOPE + MLA_V)
    q_nope = q[..., :MLA_NOPE]
    q_pe = apply_rope(q[..., MLA_NOPE:], cos[:, :, None, :], sin[:, :, None, :])
    k_nope = kv[..., :MLA_NOPE].transpose(0, 2, 1, 3)
    v = kv[..., MLA_NOPE:].transpose(0, 2, 1, 3)
    k_pe = apply_rope(k_rope, cos, sin)
    qn_b = q_nope.reshape(bsz, nq, Q_BLOCK, hh, MLA_NOPE).transpose(1, 0, 3, 2, 4)
    qp_b = q_pe.reshape(bsz, nq, Q_BLOCK, hh, MLA_ROPE).transpose(1, 0, 3, 2, 4)
    scale = (MLA_NOPE + MLA_ROPE) ** -0.5
    k_pos = jnp.arange(s)

    def one_block(args):
        ci, qn, qp = args
        q_pos = ci * Q_BLOCK + jnp.arange(Q_BLOCK)
        sc = (jnp.einsum('bhqd,bhkd->bhqk', qn, k_nope)
              + jnp.einsum('bhqr,bkr->bhqk', qp, k_pe)).astype(F32) * scale
        sc = jnp.where(k_pos[None, :] <= q_pos[:, None], sc, -jnp.inf)
        p = jax.nn.softmax(sc, axis=-1).astype(v.dtype)
        return jnp.einsum('bhqk,bhkd->bhqd', p, v)

    out = lax.map(one_block, (jnp.arange(nq), qn_b, qp_b))
    return out.transpose(1, 0, 3, 2, 4).reshape(bsz, s, hh * MLA_V)

def hier_moe(x, w_group, b_group, w_router, b_router, w_gate, w_up, w_down):
    bsz, s, d = x.shape
    t = x.reshape(bsz * s, d)
    n_tok = t.shape[0]
    g_prob = jax.nn.softmax((t @ w_group).astype(F32) + b_group.astype(F32), axis=-1)
    g_w, g_idx = lax.top_k(g_prob, 1)
    e_logits = ((t @ w_router).astype(F32) + b_router.astype(F32)).reshape(n_tok, N_EXPERT_GROUPS, EXPERTS_PER_GROUP)
    idx = jnp.broadcast_to(g_idx[:, :, None], (n_tok, 1, EXPERTS_PER_GROUP))
    e_logits = jnp.take_along_axis(e_logits, idx, axis=1)[:, 0]
    e_w, e_idx = lax.top_k(jax.nn.softmax(e_logits, axis=-1), TOP_K_IN_GROUP)
    e_w = e_w / jnp.sum(e_w, axis=-1, keepdims=True)
    expert_id = g_idx * EXPERTS_PER_GROUP + e_idx
    combine = jnp.sum(jax.nn.one_hot(expert_id, N_EXPERTS, dtype=F32) * (g_w * e_w)[..., None], axis=1)
    hid = jax.nn.silu(jnp.einsum('td,edf->tef', t, w_gate)) * jnp.einsum('td,edf->tef', t, w_up)
    hid = hid * combine[:, :, None].astype(hid.dtype)
    return jnp.einsum('tef,efd->td', hid, w_down).reshape(bsz, s, d)

def setup_inputs(seed: int = 0) -> dict:
    key = jax.random.key(seed)
    ks = jax.random.split(key, 32)
    L = DEPTH

    def normal(k, shape, scale):
        return jax.random.normal(k, shape, F32) * scale

    def gain(k, shape):
        return 1.0 + 0.01 * jax.random.normal(k, shape, F32)

    x = normal(ks[0], (BATCH, SEQ, D_MODEL), 1.0)
    start = jax.random.randint(ks[1], (BATCH, 1), 0, 1024, dtype=jnp.int32)
    positions = (start + jnp.arange(SEQ, dtype=jnp.int32)[None, :]).astype(jnp.int32)
    dt0 = jnp.exp(jax.random.uniform(ks[6], (L, SSM_HEADS), F32, math.log(1e-3), math.log(1e-1)))
    return {
        'x': x,
        'positions': positions,
        'norm_mix_g': gain(ks[2], (L, D_MODEL)),
        'w_in': normal(ks[3], (L, D_MODEL, N_IN), D_MODEL ** -0.5),
        'ssm_conv_w': normal(ks[4], (L, SSM_CONV, SSM_XBC), SSM_CONV ** -0.5),
        'ssm_conv_b': normal(ks[5], (L, SSM_XBC), 0.01),
        'ssm_dt_bias': dt0 + jnp.log(-jnp.expm1(-dt0)),
        'ssm_a_log': jnp.log(jax.random.uniform(ks[7], (L, SSM_HEADS), F32, 1.0, 16.0)),
        'ssm_d': gain(ks[8], (L, SSM_HEADS)),
        'ssm_norm_g': gain(ks[9], (L, GROUP_W)),
        'ml_conv_w': normal(ks[10], (L, MLSTM_CONV, 2 * GROUP_W), MLSTM_CONV ** -0.5),
        'ml_conv_b': normal(ks[11], (L, 2 * GROUP_W), 0.01),
        'ml_ig_bias': normal(ks[12], (L, MLSTM_HEADS), 0.1),
        'ml_fg_bias': 3.0 + 3.0 * jax.random.uniform(ks[13], (L, MLSTM_HEADS), F32),
        'ml_norm_g': gain(ks[14], (L, GROUP_W)),
        'mla_q_norm_g': gain(ks[15], (L, MLA_Q_LORA)),
        'mla_w_uq': normal(ks[16], (L, MLA_Q_LORA, MLA_HEADS * (MLA_NOPE + MLA_ROPE)), MLA_Q_LORA ** -0.5),
        'mla_kv_norm_g': gain(ks[17], (L, MLA_KV_LORA)),
        'mla_w_ukv': normal(ks[18], (L, MLA_KV_LORA, MLA_HEADS * (MLA_NOPE + MLA_V)), MLA_KV_LORA ** -0.5),
        'w_out': normal(ks[19], (L, D_MIX, D_MODEL), D_MIX ** -0.5),
        'norm_ffn_g': gain(ks[20], (L, D_MODEL)),
        'moe_w_group': normal(ks[21], (L, D_MODEL, N_EXPERT_GROUPS), D_MODEL ** -0.5),
        'moe_b_group': normal(ks[22], (L, N_EXPERT_GROUPS), 0.01),
        'moe_w_router': normal(ks[23], (L, D_MODEL, N_EXPERTS), D_MODEL ** -0.5),
        'moe_b_router': normal(ks[24], (L, N_EXPERTS), 0.01),
        'moe_w_gate': normal(ks[25], (L, N_EXPERTS, D_MODEL, D_EXPERT), D_MODEL ** -0.5),
        'moe_w_up': normal(ks[26], (L, N_EXPERTS, D_MODEL, D_EXPERT), D_MODEL ** -0.5),
        'moe_w_down': normal(ks[27], (L, N_EXPERTS, D_EXPERT, D_MODEL), D_EXPERT ** -0.5),
        'final_norm_g': gain(ks[28], (D_MODEL,)),
    }

def reference(x, positions, norm_mix_g, w_in, ssm_conv_w, ssm_conv_b, ssm_dt_bias, ssm_a_log, ssm_d,
              ssm_norm_g, ml_conv_w, ml_conv_b, ml_ig_bias, ml_fg_bias, ml_norm_g, mla_q_norm_g, mla_w_uq,
              mla_kv_norm_g, mla_w_ukv, w_out, norm_ffn_g, moe_w_group, moe_b_group, moe_w_router,
              moe_b_router, moe_w_gate, moe_w_up, moe_w_down, final_norm_g):
    bsz, s, _ = x.shape
    cos, sin = rope_tables(positions)
    split_at = [int(i) for i in np.cumsum(IN_SIZES)[:-1]]
    for l in range(DEPTH):
        h = rms_norm(x, norm_mix_g[l])
        proj = h @ w_in[l]
        (a_qkv, s_z, s_xbc, s_dt, m_qk, m_v, m_i, m_f, m_o,
         d_cq, d_ckv, d_kr) = jnp.split(proj, split_at, axis=-1)
        aq, ak, av = jnp.split(a_qkv.reshape(bsz, s, 3, MOBA_HEADS, MOBA_HD), 3, axis=2)
        y_a = moba_attention(aq[:, :, 0], ak[:, :, 0], av[:, :, 0]).astype(x.dtype)
        y_b = mamba2_ssd(s_z, s_xbc, s_dt, ssm_conv_w[l], ssm_conv_b[l], ssm_dt_bias[l],
                         ssm_a_log[l], ssm_d[l], ssm_norm_g[l]).astype(x.dtype)
        y_c = mlstm_mixer(m_qk, m_v, m_i, m_f, m_o, ml_conv_w[l], ml_conv_b[l], ml_ig_bias[l],
                          ml_fg_bias[l], ml_norm_g[l]).astype(x.dtype)
        y_d = mla_attention(d_cq, d_ckv, d_kr, cos, sin, mla_q_norm_g[l], mla_w_uq[l],
                            mla_kv_norm_g[l], mla_w_ukv[l]).astype(x.dtype)
        x = x + jnp.concatenate([y_a, y_b, y_c, y_d], axis=-1) @ w_out[l]
        h2 = rms_norm(x, norm_ffn_g[l])
        x = x + hier_moe(h2, moe_w_group[l], moe_b_group[l], moe_w_router[l], moe_b_router[l],
                         moe_w_gate[l], moe_w_up[l], moe_w_down[l]).astype(x.dtype)
    return rms_norm(x, final_norm_g)


_drawn_inputs = setup_inputs


def setup_inputs(seed=0):
    import zlib

    import numpy as np

    out = dict(_drawn_inputs(seed))
    spreads = {}
    factors = {'ssm_conv_b': 3.125,
     'ssm_d': 7.24,
     'ssm_norm_g': 3.121,
     'ml_conv_b': 2.695,
     'ml_ig_bias': 64.0,
     'ml_norm_g': 4.052,
     'mla_q_norm_g': 8.0,
     'mla_kv_norm_g': 8.0,
     'norm_ffn_g': 3.162,
     'moe_b_group': 2.785,
     'moe_b_router': 3.91,
     'final_norm_g': 30.047}
    for name, (base, spread) in spreads.items():
        noise = np.random.default_rng([zlib.crc32(name.encode()), seed]).standard_normal(out[name].shape)
        drawn = base * np.exp(spread * noise) if base else spread * noise
        out[name] = __import__('jax').numpy.asarray(drawn.astype(out[name].dtype))
    for name, factor in factors.items():
        out[name] = (out[name] * factor).astype(out[name].dtype)
    return out
```

```python
from contextlib import ExitStack

import concourse.bass as bass
import numpy as np
from concourse import mybir

F32 = mybir.dt.float32
BF16 = mybir.dt.bfloat16
I32 = mybir.dt.int32
U32 = mybir.dt.uint32
ALU = mybir.AluOpType
ACT = mybir.ActivationFunctionType
AX = mybir.AxisListType

P = 128
D = 1024
KD = D // P
T = 512
NT = T // P
L = 2
H = 4
HD = 64
GW = H * HD
NE = 16
NG = 4
EG = NE // NG
DE = 256
EPS = 1e-6
NEG = -1e30
MLA_SCALE = float(96) ** -0.5
HEAD_SCALE = float(HD) ** -0.5

SLOTS = ["x", "B", "C", "mq", "mk", "mv", "aq", "ak", "av", "cq", "ckv", "z", "mo"]
W_IN_AT = {"aq": 0, "ak": 256, "av": 512, "z": 768, "x": 1024, "B": 1280, "C": 1536,
           "mq": 1796, "mk": 2052, "mv": 2308, "mo": 2572, "cq": 2828, "ckv": 3084}
W_DT, W_IG, W_FG, W_KR = 1792, 2564, 2568, 3212

PARAMS = {}


def _param(name, n):
    PARAMS[name] = sum(w for _, w in PARAMS.values()), n


for _name, _n in (("g_mix", KD), ("g_ffn", KD), ("conv_w", 40), ("conv_b", 10), ("gate_b", 1), ("a_log", 1),
                  ("d_skip", 2), ("ssm_g", 2), ("ml_g", 2), ("q_g", 2), ("kv_g", 1), ("router_b", NG + NE)):
    _param(_name, _n)
NPAR = sum(w for _, w in PARAMS.values())
CONV_TILES = ["x0", "x1", "B0", "B1", "C0", "C1", "mq0", "mq1", "mk0", "mk1"]

CONSTS = ["ident", "neg_row", "neg_col", "avg128", "avg256", "avg64", "swap", "before", "ones", "iota"]
COLS = {"freq": (0, 1), "sign": (1, 1), "token": (2, 2 * NT), "rank": (2 + 2 * NT, EG), "first_row": (2 + 2 * NT + EG, NE)}
NCOLS = 2 + 2 * NT + EG + NE
NR = NG + NE
CAP = P
SPARE = 2 * T // (CAP + 1) + T // CAP - 1
Q_DT, Q_IG, Q_FG, Q_KR = 0, 32, 64, 96

BANK_OF = {0: (0, 0), 1: (1, 0), 3: (1, 384), 2: (2, 0)}
PACK = {i: 512 * b + at for i, (b, at) in BANK_OF.items()}
PACKED = 1280


class Steps:

    def __init__(self, nc, ctx, known, block, engine):
        self.done = ctx.enter_context(nc.semaphore(f"{block}_{engine}_done"))
        self.known, self.prefix, self.n, self.seen = known, f"{block}/{engine}:", 0, {}

    def step(self, name=None):
        self.n += 1
        if name is not None:
            assert self.prefix + name not in self.seen, name
            self.seen[self.prefix + name] = self.n
        return 1

    def at(self, name):
        return 1 if self.known is None else self.known[self.prefix + name]


def engine_steps(nc, ctx, known, block):
    return [Steps(nc, ctx, known, block, e) for e in ("tensor", "scalar", "vector", "gpsimd")]


def schedule():
    s = [("norm", None)]
    s += [("proj", "small"), ("gates", None)]
    s += [("proj", "x0"), ("proj", "x1"), ("silu", "x0"), ("proj", "B0"), ("silu", "x1"), ("gate_cols", None),
          ("proj", "B1"), ("silu", "B0"), ("proj", "C0"), ("silu", "B1"), ("xdt", None), ("proj", "C1"),
          ("silu", "C0"), ("proj", "mq0"), ("silu", "C1"), ("proj", "mq1"), ("silu", "mq0"), ("proj", "mk0"),
          ("silu", "mq1"), ("proj", "mk1"), ("silu", "mk0"), ("projT", "mv"), ("silu", "mk1")]
    fill = [("proj", "aq0"), ("proj", "aq1"), ("proj", "ak0"), ("proj", "ak1"), ("projT", "av"),
            ("proj", "cq0"), ("proj", "cq1"), ("proj", "ckv"), ("proj", "z0"), ("proj", "z1"),
            ("proj", "mo0"), ("proj", "mo1")]
    for h in range(H):
        s += [("ssd_a", h), fill.pop(0)]
        s += [("ssd_b", h)]
    for h in range(H):
        s += [("ml_a", h), fill.pop(0)]
        s += [("ml_b", h)]
    s += [("mla_norm", None)]
    s += [("att_a", ("moba", 0)), fill.pop(0), ("att_b", ("moba", 0))]
    s += [("att_a", ("moba", 1)), ("mla_up", None), ("att_c", ("moba", 0)), ("att_b", ("moba", 1))]
    s += [("att_a", ("moba", 2)), fill.pop(0), ("att_c", ("moba", 1)), ("att_b", ("moba", 2))]
    s += [("att_a", ("moba", 3)), fill.pop(0), ("att_c", ("moba", 2)), ("att_b", ("moba", 3))]
    s += [("att_a", ("mla", 0)), fill.pop(0), ("att_c", ("moba", 3)), ("att_b", ("mla", 0))]
    s += [("att_a", ("mla", 1)), ("fin_a", None), ("att_c", ("mla", 0)), ("att_b", ("mla", 1))]
    s += [("att_a", ("mla", 2)), ("fin_b", None), ("att_c", ("mla", 1)), ("att_b", ("mla", 2))]
    s += [("att_a", ("mla", 3)), ("att_c", ("mla", 2)), ("att_b", ("mla", 3)), ("att_c", ("mla", 3))]
    s += [("out", None)]
    assert not fill
    return s


def build(nc, A, known):
    seen = {}
    top = ExitStack()
    with top:
        def sb(ctx, name, shape, dt=F32):
            return ctx.enter_context(nc.sbuf_tensor(name, shape, dt))

        bank = [top.enter_context(nc.psum_tensor(f"bank{i}", [P, 512], F32)) for i in range(8)]
        const = sb(top, "const", [P, len(CONSTS), P])
        C = {n: const[:, i, :] for i, n in enumerate(CONSTS)}
        ident_bf = sb(top, "ident_bf", [P, P], BF16)
        neg_bf = sb(top, "neg_bf", [P, P], BF16)
        ccols = sb(top, "ccols", [P, NCOLS])
        token_bf = sb(top, "token_bf", [P, NT, 2], BF16)
        hT = sb(top, "hT", [P, KD, T])
        x2 = hT[:, :, :].rearrange("p k t -> p (k t)").rearrange("p (i d) -> p i d", i=NT)
        cos_t = sb(top, "cos_t", [P, T])
        sin_t = sb(top, "sin_t", [P, T])
        rows1 = sb(top, "rows1", [P, T])
        rows2 = sb(top, "rows2", [P, T])
        par = sb(top, "par", [P, NPAR])
        arena = sb(top, "arena", [P, 8192])
        x_tm = arena[:, 0:4096].rearrange("p (i d) -> p i d", i=NT)
        h_tm = arena[:, 4096:8192].rearrange("p (i d) -> p i d", i=NT)
        ms = sb(top, "ms", [P, 3 * NT])
        eps = sb(top, "eps", [P, 1])
        spare_zeroed = top.enter_context(nc.semaphore("spare_zeroed"))

        def pcol(name, i=0):
            return par[:, PARAMS[name][0] + i:PARAMS[name][0] + i + 1]

        setup(nc, A, known, seen, C, const, ident_bf, neg_bf, ccols, token_bf, cos_t, sin_t, rows1, rows2, x_tm, h_tm, ms, eps, spare_zeroed)
        with nc.Fori(0, L) as layer:
            mixers(nc, A, known, seen, layer, bank, C, ident_bf, neg_bf, cos_t, sin_t, rows1, rows2, par, pcol, hT, x2,
                   arena, x_tm, h_tm, ms, eps)
            moe(nc, A, known, seen, layer, bank, C, ccols, token_bf, par, pcol, x2, x_tm, h_tm, ms, eps, spare_zeroed)
        final_norm(nc, A, known, seen, h_tm)
    return seen


def clear(nc, steps, sems):
    nums = [s.num for s in [e.done for e in steps] + list(sems)]
    assert max(nums) - min(nums) == len(nums) - 1
    nc.all_engine_barrier(sems_to_clear=range(min(nums), max(nums) + 1))


def record(seen, steps):
    for e in steps:
        seen.update(e.seen)


def forget(pool, *sems):
    pool.dma_reset(range(min(s.num for s in sems), max(s.num for s in sems) + 1))


def root_mean_square(act, scalar, x, scratch, ms, eps, i):
    act.activation(scratch, x, ACT.Square, accum_out=ms[:, i:i + 1]).then_inc(scalar.done, scalar.step())
    act.wait_ge(scalar.done, scalar.n)
    act.activation(ms[:, NT + i:NT + i + 1], ms[:, i:i + 1], ACT.Sqrt, scale=1.0 / D, bias=eps[:, :]).then_inc(scalar.done, scalar.step(f"rms{i}"))


def normalise(dve, scalar, vector, x, out, ms, i):
    dve.wait_ge(scalar.done, scalar.at(f"rms{i}"))
    dve.reciprocal(ms[:, 2 * NT + i:2 * NT + i + 1], ms[:, NT + i:NT + i + 1]).then_inc(vector.done, vector.step())
    dve.wait_ge(vector.done, vector.n)
    dve.tensor_scalar(out, x, ms[:, 2 * NT + i:2 * NT + i + 1], None, ALU.mult).then_inc(vector.done, vector.step(f"h{i}"))


def setup(nc, A, known, seen, C, const, ident_bf, neg_bf, ccols, token_bf, cos_t, sin_t, rows1, rows2, x_tm, h_tm, ms, eps, spare_zeroed):
    with ExitStack() as ctx:
        tensor, scalar, vector, gpsimd = steps = engine_steps(nc, ctx, known, "setup")
        loaded = ctx.enter_context(nc.semaphore("setup_loaded"))
        constants_in = ctx.enter_context(nc.semaphore("constants_in"))
        x_in = [ctx.enter_context(nc.semaphore(f"x_in{i}")) for i in range(NT)]
        pos = ctx.enter_context(nc.sbuf_tensor("pos", [P, T], I32))
        zeros = ctx.enter_context(nc.sbuf_tensor("zeros", [P, D], F32))
        ang = ctx.enter_context(nc.sbuf_tensor("ang", [P, T], F32))
        turn = ctx.enter_context(nc.sbuf_tensor("turn", [P, T], F32))
        with nc.Block() as block:
            @block.sync
            def _(sp):
                sp.dma_start(ccols[:, :], A["ccols"]).then_inc(loaded, 16)
                sp.dma_start(pos[:, :], A["positions"].partition_broadcast(P).rearrange("p o t -> p (o t)")
                             if len(A["positions"].shape) == 2 else A["positions"]).then_inc(loaded, 16)
                for i in range(NT):
                    sp.dma_start(x_tm[:, i, :], A["x"][i * P:(i + 1) * P, :]).then_inc(x_in[i], 16)
                sp.dma_start(const[:, :, :], A["const"]).then_inc(constants_in, 16)
                sp.wait_ge(gpsimd.done, gpsimd.at("zeros"))
                for n in range(SPARE):
                    sp.dma_start(A["y"][(NE + n) * CAP:(NE + n + 1) * CAP, :], zeros[:, :]).then_inc(spare_zeroed, 16)

            @block.gpsimd
            def _(pool):
                pool.memset(eps[:, :], EPS).then_inc(gpsimd.done, gpsimd.step("eps"))
                pool.memset(zeros[:, :], 0.0).then_inc(gpsimd.done, gpsimd.step("zeros"))
                pool.memset(rows1[:, :], 0.0).then_inc(gpsimd.done, gpsimd.step())
                pool.memset(rows2[:, :], 0.0).then_inc(gpsimd.done, gpsimd.step())

            @block.vector
            def _(dve):
                dve.wait_ge(loaded, 32)
                def then(ins, name=None):
                    ins.then_inc(vector.done, vector.step(name))
                    dve.wait_ge(vector.done, vector.n)
                then(dve.tensor_copy(ang[:, :], pos[:, :]))
                then(dve.tensor_scalar(ang[:, :], ang[:, :], ccols[:, 0:1], None, ALU.mult))
                then(dve.tensor_scalar(turn[:, :], ang[:, :], float(1 / (2 * np.pi)), 12582912.0, ALU.mult, ALU.add))
                then(dve.tensor_scalar(turn[:, :], turn[:, :], -12582912.0, None, ALU.add))
                for part in (6.28125, 0.0019350051879882812, float(2 * np.pi - 6.28125 - 0.0019350051879882812)):
                    then(dve.scalar_tensor_tensor(ang[:, :], turn[:, :], -part, ang[:, :], ALU.mult, ALU.add))
                then(dve.tensor_scalar(ang[:, :], ang[:, :], 3.1415925, -3.1415925, ALU.min, ALU.max))
                then(dve.scalar_tensor_tensor(turn[:, :], ang[:, :], -1.0, ang[:, :], ALU.mult, ALU.max))
                then(dve.tensor_scalar(turn[:, :], turn[:, :], -1.0, float(np.pi / 2), ALU.mult, ALU.add), "angles")
                for i in range(NT):
                    normalise(dve, scalar, vector, x_tm[:, i, :], h_tm[:, i, :], ms, i)
                dve.wait_ge(constants_in, 16)
                dve.tensor_copy(ident_bf[:, :], C["ident"]).then_inc(vector.done, vector.step())
                dve.tensor_copy(neg_bf[:, :], C["neg_row"]).then_inc(vector.done, vector.step())
                dve.tensor_copy(token_bf[:, :, :], ccols[:, 2:2 + 2 * NT].rearrange("p (i c) -> p i c", i=NT)).then_inc(vector.done, vector.step())
                dve.wait_ge(scalar.done, scalar.at("sines"))
                dve.tensor_scalar(sin_t[:, :], sin_t[:, :], ccols[:, 1:2], None, ALU.mult).then_inc(vector.done, vector.step())

            @block.scalar
            def _(act):
                act.wait_ge(gpsimd.done, gpsimd.at("eps"))
                for i in range(NT):
                    act.wait_ge(x_in[i], 16)
                    root_mean_square(act, scalar, x_tm[:, i, :], h_tm[:, i, :], ms, eps, i)
                act.wait_ge(vector.done, vector.at("angles"))
                act.activation(cos_t[:, :], turn[:, :], ACT.Sin).then_inc(scalar.done, scalar.step())
                act.activation(sin_t[:, :], ang[:, :], ACT.Sin).then_inc(scalar.done, scalar.step("sines"))
        clear(nc, steps, [loaded, constants_in, *x_in])
        record(seen, steps)


def mixers(nc, A, known, seen, layer, bank, C, ident_bf, neg_bf, cos_t, sin_t, rows1, rows2, par, pcol, hT, x2,
           arena, x_tm, h_tm, ms, eps):
    NS = 4
    plan = schedule()
    with ExitStack() as ctx:
        def sb(name, shape, dt=F32):
            return ctx.enter_context(nc.sbuf_tensor(name, shape, dt))

        tensor, scalar, vector, gpsimd = steps = engine_steps(nc, ctx, known, "mix")
        sem = lambda n: ctx.enter_context(nc.semaphore(n))
        par_in, small_in, up_in, x_kept, x_again = (sem(n) for n in ("par_in", "small_in", "up_in", "x_kept", "x_again"))
        slot_in = [sem(f"slot_in{i}") for i in range(NS)]
        sems = [par_in, small_in, up_in, x_kept, x_again, *slot_in]

        ring = sb("ring", [P, NS, KD, 256])
        mixed = sb("mixed", [P, KD, T])
        w_small = sb("w_small", [P, KD, P])
        w_uq = sb("w_uq", [P, 2, 384])
        w_ukv = sb("w_ukv", [P, 512])
        q_mla = arena[:, 0:2048].rearrange("p (h t) -> p h t", h=H)
        k_mla = arena[:, 2048:4096].rearrange("p (h t) -> p h t", h=H)
        v_moba = arena[:, 4096:5120].rearrange("p (i d) -> p i d", i=NT)
        v_mla = arena[:, 5120:6144].rearrange("p (i d) -> p i d", i=NT)
        probT = arena[:, 6144:8192].rearrange("p (j t) -> p j t", j=NT)
        raw = sb("raw", [P, 2, 3 + T])
        conv = sb("conv", [P, 10, T])
        cv = {n: conv[:, i, :] for i, n in enumerate(CONV_TILES)}
        u = sb("u", [P, T])
        au = sb("au", [P, T])
        tmp = sb("tmp", [P, T])
        cols = sb("cols", [P, NT, P])
        neg_a = sb("neg_a", [P, NT, H])
        a_col = sb("a_col", [P, 1])
        xdt = sb("xdt", [P, NT, GW])
        v_aug = sb("v_aug", [P, NT, H, P])
        qT = sb("qT", [P, 2, T])
        kT = sb("kT", [P, 2, T])
        tri = sb("tri", [P, 2, PACKED])
        diag = sb("diag", [P, NT, P])
        ckv = sb("ckv", [P, T])
        rstd = sb("rstd", [P, T])
        absden = sb("absden", [P, T])
        mx = sb("mx", [P, 2, 4 * NT])
        zero = sb("zero", [P, 1])
        cq = mixed[:, 6:8, :]
        zs = mixed[:, 2:4, :]
        os_ = mixed[:, 4:6, :]

        slot_of = {n: (i % NS, i // NS) for i, n in enumerate(SLOTS)}
        NSL = len(SLOTS)
        slot_of.update({f"out{j}": ((NSL + j) % NS, (NSL + j) // NS) for j in range(4)})

        def last_use(name):
            return "ckv" if name == "ckv" else f"{name}1"

        ssd_y, ml_h = [cv["x0"], cv["x1"]], [cv["mq0"], cv["mq1"]]
        cq_sq = ssd_sq = [cv["B0"], cv["B1"]]
        ckv_sq, ml_sq = cv["C0"], [cv["C0"], cv["C1"]]
        q_pe, q_cos = cv["mk0"], cv["mk1"]
        rstds = [rstd, absden]
        units = ([f"ssd_y{h}" for h in range(H)] + [f"ml_y{h}" for h in range(H)]
                 + [f"att_t2{(k, h)}" for k in ("moba", "mla") for h in range(H)])
        unit_at = {"ssd": 0, "ml": H, "moba": 2 * H, "mla": 3 * H}

        with nc.Block() as block:
            @block.sync
            def _(sp):
                sp.dma_start(par[:, :], A["params"][bass.ds(layer, 1), :, :].rearrange("o p n -> (o p) n")).then_inc(par_in, 16)
                sp.dma_start(w_small[:, :, :], A["w_small"][bass.ds(layer, 1), :, :, :].rearrange("o p k n -> (o p) k n")).then_inc(small_in, 16)
                order = SLOTS + [f"out{j}" for j in range(4)]
                for n, name in enumerate(order):
                    if n == 2:
                        sp.dma_start(A["residual"].rearrange("(i p) d -> p i d", p=P), x_tm).then_inc(x_kept, 16)
                    if n == 4:
                        sp.dma_start(w_uq[:, :, :], A["w_uq"][bass.ds(layer, 1), :, :, :].rearrange("o p k n -> (o p) k n")).then_inc(up_in, 16)
                        sp.dma_start(w_ukv[:, :], A["w_ukv"][bass.ds(layer, 1), :, :].rearrange("o p n -> (o p) n")).then_inc(up_in, 16)
                    if n >= NS:
                        sp.wait_ge(tensor.done, tensor.at(last_use(order[n - NS])))
                    slot = slot_of[name][0]
                    if n < NSL:
                        sp.dma_start(ring[:, slot, :, :], A["w_in"][bass.ds(layer, 1), n, :, :, :].rearrange("o p k n -> (o p) k n")).then_inc(slot_in[slot], 16)
                    else:
                        sp.dma_start(ring[:, slot, :, :], A["w_out"][bass.ds(layer, 1), n - NSL, :, :, :].rearrange("o p k n -> (o p) k n")).then_inc(slot_in[slot], 16)
                sp.wait_ge(x_kept, 16)
                sp.wait_ge(tensor.done, tensor.at("mo1"))
                sp.dma_start(x2, A["residual"].rearrange("(i p) d -> p i d", p=P)).then_inc(x_again, 16)

            @block.tensor
            def _(pe):
                free = {}

                def claim(b, engine, reader):
                    if b in free:
                        last_engine, last_reader = free[b]
                        pe.wait_ge(last_engine.done, last_engine.at(last_reader))
                    free[b] = engine, reader

                def mm(out, lhsT, rhs, start, stop):
                    return pe.matmul(out, lhsT, rhs, start=start, stop=stop, skip_group_check=True)

                turn = [0]

                def pj():
                    turn[0] += 1
                    return turn[0] % 2

                def norm(_):
                    for k in range(KD):
                        for i in range(NT):
                            m = pe.transpose(bank[k][:, i * P:(i + 1) * P], h_tm[:, i, k * P:(k + 1) * P], C["ident"])
                        m.then_inc(tensor.done, tensor.step(f"hT{k}"))
                        free[k] = (scalar, vector)[k % 2], f"hT{k}"
                    pe.wait_ge(scalar.done, scalar.at(f"hT{KD - 2}"))
                    pe.wait_ge(vector.done, vector.at(f"hT{KD - 1}"))

                def proj(name):
                    b = pj()
                    claim(b, scalar, name)
                    if name == "small":
                        pe.wait_ge(small_in, 16)
                        w = w_small[:, :, :]
                    else:
                        slot, times = slot_of[name.rstrip("01")]
                        pe.wait_ge(slot_in[slot], 16 * (times + 1))
                        at = P if name[-1] == "1" else 0
                        w = ring[:, slot, :, at:at + P]
                    for k in range(KD):
                        m = mm(bank[b][:, :], w[:, k, :], hT[:, k, :], k == 0, k == KD - 1)
                    m.then_inc(tensor.done, tensor.step(name))

                def projT(name):
                    slot, times = slot_of[name]
                    pe.wait_ge(slot_in[slot], 16 * (times + 1))
                    for half in range(2):
                        b = pj()
                        claim(b, scalar, f"{name}{half}")
                        for i in range(2):
                            for k in range(KD):
                                tile = 2 * half + i
                                m = mm(bank[b][:, i * GW:(i + 1) * GW], hT[:, k, tile * P:(tile + 1) * P],
                                       ring[:, slot, k, :], k == 0, k == KD - 1)
                        m.then_inc(tensor.done, tensor.step(f"{name}{half}"))

                def gate_cols(_):
                    claim(7, scalar, "cols")
                    pe.wait_ge(vector.done, vector.at("rows1"))
                    for i in range(NT):
                        m = pe.transpose(bank[7][:, i * P:(i + 1) * P], rows1[:, i * P:(i + 1) * P], C["ident"])
                    m.then_inc(tensor.done, tensor.step("cols"))

                def xdt_(_):
                    for half in range(2):
                        claim(2 + half, vector, f"xdt{half}")
                        for i in range(2):
                            for j in range(2):
                                pe.wait_ge(scalar.done, scalar.at(f"silu_x{j}"))
                                tile = 2 * half + i
                                m = pe.transpose(bank[2 + half][:, i * GW + j * P:i * GW + (j + 1) * P],
                                                 cv[f"x{j}"][:, tile * P:(tile + 1) * P], C["ident"])
                        m.then_inc(tensor.done, tensor.step(f"xdt{half}"))

                def pair_scores(keys, queries, at, n, reader):
                    for b in range(3):
                        claim(2 + b, vector, reader)
                    for i in (0, 1, 3, 2):
                        b, off = BANK_OF[i]
                        m = mm(bank[2 + b][:, off:off + T - i * P], keys[at:at + n, i * P:(i + 1) * P],
                               queries[at:at + n, i * P:T], True, True)
                    return m

                def spread(b, row, rows, engine, reader):
                    claim(b, engine, reader)
                    return mm(bank[b][:, :], C["ident"][:, row:row + 1].to_broadcast([P, P]), rows[:, :], True, True)

                def ssd_a(h):
                    if h % 2 == 0:
                        pe.wait_ge(scalar.done, scalar.at(f"silu_B{h // 2}"))
                        pe.wait_ge(scalar.done, scalar.at(f"silu_C{h // 2}"))
                        pair_scores(cv[f"B{h // 2}"], cv[f"C{h // 2}"], 0, P, f"ssd_w{h + 1}").then_inc(tensor.done, tensor.step(f"ssd_s{h}"))
                    pe.wait_ge(vector.done, vector.at("rows1"))
                    spread(5, Q_DT + h, rows1, scalar, f"ssd_e{h}").then_inc(tensor.done, tensor.step(f"ssd_r{h}"))

                def triangle(out, weight, h):
                    for i in range(NT):
                        m = mm(out[:, i * P:T], weight(i), tri[:, h % 2, PACK[i]:PACK[i] + T - i * P], i == 0, i == NT - 1)
                    return m

                def ssd_b(h):
                    if h % 2 == 0:
                        claim(6, vector, f"ssd_y{h // 2}")
                    pe.wait_ge(vector.done, vector.at(f"ssd_w{h}"))
                    pe.wait_ge(vector.done, vector.at("xdt1"))
                    lo = HD * (h % 2)
                    triangle(bank[6][lo:lo + HD, :], lambda i: xdt[:, i, HD * h:HD * (h + 1)], h).then_inc(tensor.done, tensor.step(f"ssd_y{h}"))

                def ml_a(h):
                    pe.wait_ge(scalar.done, scalar.at(f"silu_mq{h // 2}"))
                    pe.wait_ge(scalar.done, scalar.at(f"silu_mk{h // 2}"))
                    lo = HD * (h % 2)
                    pair_scores(cv[f"mk{h // 2}"], cv[f"mq{h // 2}"], lo, HD, f"ml_w{h}").then_inc(tensor.done, tensor.step(f"ml_s{h}"))
                    spread(5, Q_KR + h, rows1, scalar, f"ml_e{h}").then_inc(tensor.done, tensor.step(f"ml_r{h}"))
                    pe.wait_ge(scalar.done, scalar.at("rows2"))
                    spread(7, Q_FG + h, rows2, vector, f"ml_d{h}").then_inc(tensor.done, tensor.step(f"ml_f{h}"))

                def ml_b(h):
                    claim(6, vector, f"ml_y{h}")
                    pe.wait_ge(vector.done, vector.at(f"ml_w{h}"))
                    pe.wait_ge(scalar.done, scalar.at("mv1"))
                    pe.wait_ge(gpsimd.done, gpsimd.at("ones"))
                    triangle(bank[6][:, :], lambda i: v_aug[:, i, h, :], h).then_inc(tensor.done, tensor.step(f"ml_y{h}"))

                def att_a(a):
                    kind, h = a
                    if kind == "moba":
                        pe.wait_ge(scalar.done, scalar.at(f"aq{h // 2}"))
                        pe.wait_ge(scalar.done, scalar.at(f"ak{h // 2}"))
                        lo, n, q, k = HD * (h % 2), HD, qT[:, h // 2, :], kT[:, h // 2, :]
                    else:
                        pe.wait_ge(vector.done, vector.at(f"mla_q{h}"))
                        pe.wait_ge(vector.done, vector.at(f"mla_k{h}"))
                        pe.wait_ge(scalar.done, scalar.at("k_up1"))
                        lo, n, q, k = 0, 96, q_mla[:, h, :], k_mla[:, h, :]
                    for b in range(3):
                        claim(2 + b, scalar, f"att_e{a}")
                    for r in (0, 1, 3, 2):
                        i = NT - 1 - r
                        b, off = BANK_OF[r]
                        mm(bank[2 + b][:, off:off + (i + 1) * P], q[lo:lo + n, i * P:(i + 1) * P], k[lo:lo + n, 0:(i + 1) * P], True, False)
                        m = mm(bank[2 + b][:, off + i * P:off + (i + 1) * P], ident_bf[:, :], neg_bf[:, :], False, True)
                    m.then_inc(tensor.done, tensor.step(f"att_s{a}"))

                def att_b(a):
                    for n, (b, tiles) in enumerate(((5, [3]), (7, [2, 0]), (5, [1]))):
                        claim(b, (scalar, vector, scalar)[n], f"att_t{n}{a}")
                        for i in tiles:
                            off = 384 if i == 0 else 0
                            pe.wait_ge(vector.done, vector.at(f"att_p{i}{a}"))
                            for j in range(i + 1):
                                m = pe.transpose(bank[b][:, off + j * P:off + (j + 1) * P],
                                                 tri[:, a[1] % 2, PACK[NT - 1 - i] + j * P:PACK[NT - 1 - i] + (j + 1) * P], C["ident"])
                        m.then_inc(tensor.done, tensor.step(f"att_t{n}{a}"))

                def att_c(a):
                    kind, h = a
                    v = v_moba if kind == "moba" else v_mla
                    pe.wait_ge(scalar.done, scalar.at("av1" if kind == "moba" else "mla_v1"))
                    pe.wait_ge(vector.done, vector.at(f"att_t1{a}"))
                    pe.wait_ge(scalar.done, scalar.at(f"att_t0{a}"))
                    pe.wait_ge(scalar.done, scalar.at(f"att_t2{a}"))
                    if h % 2 == 0:
                        claim(6, scalar, f"att_y{(kind, h // 2)}")
                    lo = HD * (h % 2)
                    for j in range(NT):
                        m = mm(bank[6][lo:lo + HD, j * P:T], v[:, j, HD * h:HD * (h + 1)], probT[:, j, j * P:T], j == 0, j == NT - 1)
                    m.then_inc(tensor.done, tensor.step(f"att_y{a}"))

                def mla_norm(_):
                    claim(7, scalar, "cq_ln")
                    pe.wait_ge(vector.done, vector.at("cq_sq0"))
                    pe.wait_ge(vector.done, vector.at("cq_sq1"))
                    mm(bank[7][:, :], C["avg256"], cq_sq[0], True, False)
                    mm(bank[7][:, :], C["avg256"], cq_sq[1], False, True).then_inc(tensor.done, tensor.step("cq_ms"))

                def kv_norm():
                    claim(7, scalar, "ckv_ln")
                    pe.wait_ge(vector.done, vector.at("ckv_sq"))
                    mm(bank[7][:, :], C["avg128"], ckv_sq, True, True).then_inc(tensor.done, tensor.step("ckv_ms"))

                def mla_up(_):
                    kv_norm()
                    pe.wait_ge(up_in, 32)
                    pe.wait_ge(vector.done, vector.at("cq_n1"))
                    for n in range(3):
                        b = pj()
                        claim(b, scalar, f"q_up{n}")
                        for k in range(2):
                            m = mm(bank[b][:, :], w_uq[:, k, n * P:(n + 1) * P], cq[:, k, :], k == 0, k == 1)
                        m.then_inc(tensor.done, tensor.step(f"q_up{n}"))
                    claim(7, vector, "k_rot")
                    mm(bank[7][:, :], C["swap"], u[:, :], True, True).then_inc(tensor.done, tensor.step("k_swap"))
                    pe.wait_ge(vector.done, vector.at("ckv_n"))
                    for n in range(2):
                        b = pj()
                        claim(b, scalar, f"k_up{n}")
                        mm(bank[b][:, :], w_ukv[:, n * P:(n + 1) * P], ckv[:, :], True, True).then_inc(tensor.done, tensor.step(f"k_up{n}"))
                    for half in range(2):
                        b = pj()
                        claim(b, scalar, f"mla_v{half}")
                        for i in range(2):
                            tile = 2 * half + i
                            m = mm(bank[b][:, i * GW:(i + 1) * GW], ckv[:, tile * P:(tile + 1) * P], w_ukv[:, GW:2 * GW], True, True)
                        m.then_inc(tensor.done, tensor.step(f"mla_v{half}"))
                    pe.wait_ge(scalar.done, scalar.at("q_up2"))
                    claim(7, vector, "q_rot")
                    mm(bank[7][:, :], C["swap"], q_pe, True, True).then_inc(tensor.done, tensor.step("q_swap"))

                def fin_a(_):
                    for j in range(2):
                        b = pj()
                        claim(b, scalar, f"ssd_ln{j}")
                        pe.wait_ge(vector.done, vector.at(f"ssd_sq{j}"))
                        mm(bank[b][:, :], C["avg128"], ssd_sq[j], True, True).then_inc(tensor.done, tensor.step(f"ssd_ms{j}"))

                def fin_b(_):
                    for j in range(2):
                        b = pj()
                        claim(b, scalar, f"ml_ln{j}")
                        pe.wait_ge(vector.done, vector.at(f"ml_sq{j}"))
                        mm(bank[b][:, :], C["avg64"], ml_sq[j], True, True).then_inc(tensor.done, tensor.step(f"ml_ms{j}"))

                def out(_):
                    for b in range(8):
                        claim(b, vector, f"x{b // 2}")
                    pe.wait_ge(vector.done, vector.at("ssd_n1"))
                    pe.wait_ge(vector.done, vector.at("ml_n1"))
                    pe.wait_ge(scalar.done, scalar.at("att_y('moba', 1)"))
                    pe.wait_ge(scalar.done, scalar.at("att_y('mla', 1)"))
                    for j in range(4):
                        slot, times = slot_of[f"out{j}"]
                        pe.wait_ge(slot_in[slot], 16 * (times + 1))
                    for i in range(NT):
                        for half in range(2):
                            for k in range(KD):
                                w = ring[:, slot_of[f"out{k // 2}"][0], :, :].rearrange("p k n -> p (k n)")
                                at = (k % 2) * D + half * 512
                                m = mm(bank[2 * i + half][:, :], mixed[:, k, i * P:(i + 1) * P], w[:, at:at + 512], k == 0, k == KD - 1)
                        m.then_inc(tensor.done, tensor.step(f"out{i}"))

                do = dict(norm=norm, proj=proj, projT=projT, gate_cols=gate_cols, xdt=xdt_, ssd_a=ssd_a, ssd_b=ssd_b,
                          ml_a=ml_a, ml_b=ml_b, att_a=att_a, att_b=att_b, att_c=att_c, mla_norm=mla_norm, mla_up=mla_up,
                          fin_a=fin_a, fin_b=fin_b, out=out)
                for op, arg in plan:
                    if op in do:
                        do[op](arg)

            @block.scalar
            def _(act):

                def act_to(out, src, func=ACT.Copy, name=None, **kw):
                    act.activation(out, src, func, **kw).then_inc(scalar.done, scalar.step(name))

                def norm(_):
                    act.wait_ge(par_in, 16)
                    for k in range(0, KD, 2):
                        act.wait_ge(tensor.done, tensor.at(f"hT{k}"))
                        act_to(hT[:, k, :], bank[k][:, :], ACT.Identity, f"hT{k}", scale=pcol("g_mix", k))

                turn = [0]

                def pj():
                    turn[0] += 1
                    return bank[turn[0] % 2]

                def proj(name):
                    b = pj()
                    act.wait_ge(tensor.done, tensor.at(name))
                    if name == "small":
                        act_to(u[:, :], b[:, :], ACT.Identity, name, bias=pcol("gate_b"))
                    elif name in CONV_TILES:
                        n = CONV_TILES.index(name)
                        if n >= 2:
                            act.wait_ge(vector.done, vector.at(f"conv_{CONV_TILES[n - 2]}"))
                        act_to(raw[:, n % 2, 3:3 + T], b[:, :], name=name)
                    else:
                        j = int(name[-1]) if name[-1] in "01" else 0
                        out = {"aq": qT, "ak": kT, "cq": cq, "z": zs, "mo": os_}.get(name.rstrip("01"))
                        act_to(ckv[:, :] if out is None else out[:, j, :], b[:, :], name=name)

                def projT(name):
                    for half in range(2):
                        b = pj()
                        act.wait_ge(tensor.done, tensor.at(f"{name}{half}"))
                        tiles = slice(2 * half, 2 * half + 2)
                        if name == "av":
                            act_to(v_moba[:, tiles, :], b[:, :].rearrange("p (i d) -> p i d", i=2), name=f"{name}{half}")
                        else:
                            for i in range(2):
                                act_to(v_aug[:, 2 * half + i, :, 0:HD],
                                       b[:, i * GW:(i + 1) * GW].rearrange("p (h d) -> p h d", h=H), name=f"{name}{half}" if i else None)

                def gates(_):
                    act_to(a_col[0:H, :], pcol("a_log")[0:H, :], ACT.Exp, "a_col")
                    act.wait_ge(vector.done, vector.at("au"))
                    act.activation(au[0:68, :], au[0:68, :], ACT.Exp, scale=-1.0).then_inc(scalar.done, scalar.step())
                    act.wait_ge(scalar.done, scalar.n)
                    act_to(au[0:68, :], au[0:68, :], ACT.Ln, "softplus", bias=1.0)
                    act.wait_ge(vector.done, vector.at("rows2"))
                    act_to(rows2[Q_FG:Q_FG + H, :], rows2[Q_FG:Q_FG + H, :], ACT.Exp, "rows2", scale=-1.0)

                def silu(name):
                    act.wait_ge(vector.done, vector.at(f"conv_{name}"))
                    act_to(cv[name], cv[name], ACT.Silu, f"silu_{name}")

                def gate_cols(_):
                    act.wait_ge(tensor.done, tensor.at("cols"))
                    act_to(cols[:, :, :], bank[7][:, :].rearrange("p (i c) -> p i c", i=NT), name="cols")

                def decays(h, kind, col):
                    n = unit_at[kind] + h
                    if n >= 2:
                        act.wait_ge(tensor.done, tensor.at(units[n - 2]))
                    act.wait_ge(tensor.done, tensor.at(f"{kind}_r{h}"))
                    act.wait_ge(vector.done, vector.at(f"{kind}_x{h}"))
                    for i in range(NT):
                        at = PACK[i]
                        m = act.activation(tri[:, h % 2, at:at + P], diag[:, i, :], ACT.Exp, bias=col(i))
                        if i < NT - 1:
                            m = act.activation(tri[:, h % 2, at + P:at + T - i * P], bank[5][:, (i + 1) * P:T], ACT.Exp, bias=col(i))
                    m.then_inc(scalar.done, scalar.step(f"{kind}_e{h}"))

                def ssd_a(h):
                    act.wait_ge(vector.done, vector.at("neg_a"))
                    decays(h, "ssd", lambda i: neg_a[:, i, h:h + 1])

                def ml_a(h):
                    decays(h, "ml", lambda i: cols[:, i, Q_FG + h:Q_FG + h + 1])

                def ml_b(h):
                    act.wait_ge(tensor.done, tensor.at(f"ml_y{h}"))
                    if h:
                        act.wait_ge(vector.done, vector.at(f"ml_y{h - 1}"))
                    act_to(absden[HD:P, :], bank[6][HD:P, :], ACT.Abs, f"ml_abs{h}")

                def rms(src, out, name):
                    act.activation(out, src, ACT.Ln, bias=eps[:, :]).then_inc(scalar.done, scalar.step(f"{name.replace('@', '_ln')}"))
                    act.wait_ge(scalar.done, scalar.n)
                    act.activation(out, out, ACT.Exp, scale=-0.5).then_inc(scalar.done, scalar.step(f"{name.replace('@', '_rstd')}"))

                def mla_norm(_):
                    act.wait_ge(tensor.done, tensor.at("cq_ms"))
                    rms(bank[7][:, :], rstd[:, :], "cq@")

                def mla_up(_):
                    act.wait_ge(x_kept, 16)
                    act.wait_ge(tensor.done, tensor.at("ckv_ms"))
                    act.wait_ge(vector.done, vector.at("cq_n1"))
                    rms(bank[7][:, :], rstd[:, :], "ckv@")
                    for n in range(3):
                        b = pj()
                        act.wait_ge(tensor.done, tensor.at(f"q_up{n}"))
                        if n == 2:
                            act_to(q_pe, b[:, :], name="q_up2")
                        else:
                            act_to(q_mla[0:HD, 2 * n, :], b[0:HD, :])
                            act_to(q_mla[0:HD, 2 * n + 1, :], b[HD:P, :], name=f"q_up{n}")
                    for n in range(2):
                        b = pj()
                        act.wait_ge(tensor.done, tensor.at(f"k_up{n}"))
                        act_to(k_mla[0:HD, 2 * n, :], b[0:HD, :])
                        act_to(k_mla[0:HD, 2 * n + 1, :], b[HD:P, :], name=f"k_up{n}")
                    for half in range(2):
                        b = pj()
                        act.wait_ge(tensor.done, tensor.at(f"mla_v{half}"))
                        act_to(v_mla[:, 2 * half:2 * half + 2, :], b[:, :].rearrange("p (i d) -> p i d", i=2), name=f"mla_v{half}")

                def att_a(a):
                    kind, h = a
                    scale = HEAD_SCALE if kind == "moba" else MLA_SCALE
                    act.wait_ge(tensor.done, tensor.at(units[unit_at[kind] + h - 2]))
                    act.wait_ge(vector.done, vector.at(f"att_m{a}"))
                    for i in (3, 2, 1, 0):
                        b, off = BANK_OF[NT - 1 - i]
                        at, n = PACK[NT - 1 - i], (i + 1) * P
                        act.activation(tri[:, h % 2, at:at + n], bank[2 + b][:, off:off + n], ACT.Exp,
                                              bias=mx[:, h % 2, NT + i:NT + i + 1], scale=scale,
                                              accum_out=mx[:, h % 2, 2 * NT + i:2 * NT + i + 1]).then_inc(scalar.done, scalar.step(f"att_e{a}" if i == 0 else f"att_e{i}{a}"))

                def att_b(a):
                    n = unit_at[a[0]] + a[1] - 1 - 2 * H
                    if n >= 0:
                        act.wait_ge(tensor.done, tensor.at(f"att_y{(('moba', 'mla')[n // H], n % H)}"))
                    act.wait_ge(tensor.done, tensor.at(f"att_t0{a}"))
                    act_to(probT[:, :, 3 * P:T], bank[5][:, :].rearrange("p (j t) -> p j t", j=NT), name=f"att_t0{a}")
                    act.wait_ge(tensor.done, tensor.at(f"att_t2{a}"))
                    act_to(probT[:, 0:2, P:2 * P], bank[5][:, 0:2 * P].rearrange("p (j t) -> p j t", j=2), name=f"att_t2{a}")

                def att_c(a):
                    kind, h = a
                    if h % 2:
                        act.wait_ge(tensor.done, tensor.at(f"att_y{a}"))
                        act_to(mixed[:, (0 if kind == "moba" else 6) + h // 2, :], bank[6][:, :], name=f"att_y{(kind, h // 2)}")

                def fin_a(_):
                    act_to(zs, zs, ACT.Silu, "silu_z")
                    for j in range(2):
                        b = pj()
                        act.wait_ge(tensor.done, tensor.at(f"ssd_ms{j}"))
                        rms(b[:, :], rstds[j][:, :], f"ssd@{j}")

                def fin_b(_):
                    act_to(os_, os_, ACT.Sigmoid, "sig_o")
                    for j in range(2):
                        b = pj()
                        act.wait_ge(tensor.done, tensor.at(f"ml_ms{j}"))
                        act.wait_ge(vector.done, vector.at(f"ssd_n{j}"))
                        rms(b[:, :], rstds[j][:, :], f"ml@{j}")

                def out(_):
                    for i in range(NT):
                        act.wait_ge(vector.done, vector.at(f"x{i}"))
                        root_mean_square(act, scalar, x2[:, i, :], h_tm[:, i, :], ms, eps, i)

                do = dict(norm=norm, proj=proj, projT=projT, gates=gates, silu=silu, gate_cols=gate_cols, ssd_a=ssd_a,
                          ml_a=ml_a, ml_b=ml_b, att_a=att_a, att_b=att_b, att_c=att_c, mla_norm=mla_norm, mla_up=mla_up,
                          fin_a=fin_a, fin_b=fin_b, out=out)
                for op, arg in plan:
                    if op in do:
                        do[op](arg)

            @block.vector
            def _(dve):

                def norm(_):
                    dve.wait_ge(par_in, 16)
                    for k in range(1, KD, 2):
                        dve.wait_ge(tensor.done, tensor.at(f"hT{k}"))
                        dve.tensor_scalar(hT[:, k, :], bank[k][:, :], pcol("g_mix", k), None, ALU.mult).then_inc(vector.done, vector.step(f"hT{k}"))

                def proj(name):
                    if name not in CONV_TILES:
                        return
                    n = CONV_TILES.index(name)
                    dve.wait_ge(gpsimd.done, gpsimd.at("pads"))
                    dve.wait_ge(scalar.done, scalar.at(name))
                    src = lambda j: raw[:, n % 2, j:j + T]
                    dve.tensor_scalar(cv[name], src(0), pcol("conv_w", 4 * n), pcol("conv_b", n), ALU.mult, ALU.add).then_inc(vector.done, vector.step())
                    dve.wait_ge(vector.done, vector.n)
                    for j in (1, 2, 3):
                        ins = dve.scalar_tensor_tensor(cv[name], src(j), pcol("conv_w", 4 * n + j), cv[name], ALU.mult, ALU.add)
                        ins.then_inc(vector.done, vector.step(f"conv_{name}" if j == 3 else None))
                        dve.wait_ge(vector.done, vector.n)

                def gates(_):
                    dt, ig, fg = slice(Q_DT, Q_DT + H), slice(Q_IG, Q_IG + H), slice(Q_FG, Q_FG + H)
                    none = zero[:, :].to_broadcast([P, T])
                    dve.wait_ge(scalar.done, scalar.at("small"))
                    dve.wait_ge(gpsimd.done, gpsimd.at("zero"))
                    dve.scalar_tensor_tensor(au[0:68, :], u[0:68, :], -1.0, u[0:68, :], ALU.mult, ALU.max).then_inc(vector.done, vector.step("au"))
                    dve.tensor_copy(tmp[fg, :], u[ig, :]).then_inc(vector.done, vector.step())
                    dve.wait_ge(scalar.done, scalar.at("softplus"))
                    dve.wait_ge(scalar.done, scalar.at("a_col"))
                    dve.scalar_tensor_tensor(rows1[Q_IG:Q_IG + H, :], u[dt, :], 0.0, au[dt, :], ALU.max, ALU.add).then_inc(vector.done, vector.step())
                    dve.scalar_tensor_tensor(tmp[dt, :], u[dt, :], 0.0, au[dt, :], ALU.max, ALU.add).then_inc(vector.done, vector.step())
                    dve.wait_ge(vector.done, vector.n)
                    dve.tensor_scalar(tmp[dt, :], tmp[dt, :], a_col[0:H, :], -1.0, ALU.mult, ALU.mult).then_inc(vector.done, vector.step())
                    dve.wait_ge(vector.done, vector.n)
                    dve.tensor_tensor_scan(rows1[dt, :], tmp[dt, :], none[dt, :], 0.0, ALU.add, ALU.add).then_inc(vector.done, vector.step())
                    dve.scalar_tensor_tensor(au[fg, :], u[fg, :], 0.0, au[fg, :], ALU.min, ALU.subtract).then_inc(vector.done, vector.step())
                    dve.wait_ge(vector.done, vector.n)
                    dve.tensor_tensor_scan(rows2[fg, :], au[fg, :], none[fg, :], 0.0, ALU.add, ALU.add).then_inc(vector.done, vector.step())
                    dve.wait_ge(vector.done, vector.n)
                    dve.tensor_tensor(rows1[fg, :], tmp[fg, :], rows2[fg, :], ALU.subtract).then_inc(vector.done, vector.step())
                    dve.wait_ge(vector.done, vector.n)
                    dve.tensor_tensor_scan(tmp[fg, :], rows1[fg, :], rows1[fg, :], 0.0, ALU.max, ALU.max).then_inc(vector.done, vector.step())
                    dve.wait_ge(vector.done, vector.n)
                    dve.tensor_tensor(rows2[fg, :], rows2[fg, :], tmp[fg, :], ALU.add).then_inc(vector.done, vector.step("rows2"))
                    dve.tensor_scalar(rows1[Q_KR:Q_KR + H, :], tmp[fg, :], -1.0, None, ALU.mult).then_inc(vector.done, vector.step("rows1"))

                def gate_cols(_):
                    dve.wait_ge(scalar.done, scalar.at("cols"))
                    dve.tensor_scalar(neg_a[:, :, :], cols[:, :, Q_DT:Q_DT + H], -1.0, None, ALU.mult).then_inc(vector.done, vector.step("neg_a"))

                def xdt_(_):
                    for half in range(2):
                        dve.wait_ge(tensor.done, tensor.at(f"xdt{half}"))
                        for i in range(2):
                            tile = 2 * half + i
                            dt = cols[:, tile, Q_IG:Q_IG + H].rearrange("p (h o) -> p h o", o=1).to_broadcast([P, H, HD])
                            m = dve.tensor_tensor(xdt[:, tile, :].rearrange("p (h d) -> p h d", h=H),
                                                  bank[2 + half][:, i * GW:(i + 1) * GW].rearrange("p (h d) -> p h d", h=H), dt, ALU.mult)
                        m.then_inc(vector.done, vector.step(f"xdt{half}"))

                def decayed(h, kind, scores, scale):
                    dve.wait_ge(tensor.done, tensor.at(f"{kind}_r{h}"))
                    before = f"{kind}_e{h - 1}" if h else ("ssd_e3" if kind == "ml" else None)
                    if before:
                        dve.wait_ge(scalar.done, scalar.at(before))
                    mask = C["neg_col"].rearrange("p (o t) -> p o t", o=1).to_broadcast([P, NT, P])
                    dve.tensor_tensor(diag[:, :, :], bank[5][:, :].rearrange("p (i t) -> p i t", i=NT), mask, ALU.add).then_inc(vector.done, vector.step(f"{kind}_x{h}"))
                    dve.wait_ge(scalar.done, scalar.at(f"{kind}_e{h}"))
                    dve.wait_ge(tensor.done, tensor.at(scores))
                    for b, n in enumerate((512, 512, 256)):
                        part = tri[:, h % 2, 512 * b:512 * b + n]
                        m = dve.scalar_tensor_tensor(part, bank[2 + b][:, 0:n], scale, part, ALU.mult, ALU.mult)
                    m.then_inc(vector.done, vector.step(f"{kind}_w{h}"))

                def ssd_a(h):
                    decayed(h, "ssd", f"ssd_s{h - h % 2}", 1.0)

                def ssd_b(h):
                    if h % 2:
                        j = h // 2
                        dve.wait_ge(tensor.done, tensor.at(f"ssd_y{h}"))
                        dve.wait_ge(tensor.done, tensor.at("xdt1"))
                        dve.scalar_tensor_tensor(ssd_y[j], cv[f"x{j}"], pcol("d_skip", j), bank[6][:, :], ALU.mult, ALU.add).then_inc(vector.done, vector.step(f"ssd_y{j}"))

                def ml_a(h):
                    decayed(h, "ml", f"ml_s{h}", HEAD_SCALE)

                def ml_b(h):
                    lo, hi = HD * (h % 2), HD * (h % 2) + HD
                    dve.wait_ge(scalar.done, scalar.at(f"ml_abs{h}"))
                    dve.wait_ge(tensor.done, tensor.at(f"ml_f{h}"))
                    dve.tensor_tensor(absden[HD:P, :], absden[HD:P, :], bank[7][HD:P, :], ALU.max).then_inc(vector.done, vector.step(f"ml_d{h}"))
                    dve.wait_ge(vector.done, vector.n)
                    dve.reciprocal(absden[HD:P, :], absden[HD:P, :]).then_inc(vector.done, vector.step())
                    dve.wait_ge(vector.done, vector.n)
                    dve.tensor_tensor(ml_h[h // 2][lo:hi, :], bank[6][0:HD, :], absden[HD:P, :], ALU.mult).then_inc(vector.done, vector.step(f"ml_y{h}"))

                def mla_norm(_):
                    for j in range(2):
                        dve.wait_ge(scalar.done, scalar.at(f"cq{j}"))
                        dve.tensor_tensor(cq_sq[j], cq[:, j, :], cq[:, j, :], ALU.mult).then_inc(vector.done, vector.step(f"cq_sq{j}"))
                    dve.wait_ge(scalar.done, scalar.at("cq_rstd"))
                    for j in range(2):
                        dve.scalar_tensor_tensor(cq[:, j, :], cq[:, j, :], pcol("q_g", j), rstd[:, :], ALU.mult, ALU.mult).then_inc(vector.done, vector.step(f"cq_n{j}"))
                    dve.wait_ge(scalar.done, scalar.at("ckv"))
                    dve.tensor_tensor(ckv_sq, ckv[:, :], ckv[:, :], ALU.mult).then_inc(vector.done, vector.step("ckv_sq"))

                def mla_up(_):
                    dve.wait_ge(scalar.done, scalar.at("ckv_rstd"))
                    dve.scalar_tensor_tensor(ckv[:, :], ckv[:, :], pcol("kv_g"), rstd[:, :], ALU.mult, ALU.mult).then_inc(vector.done, vector.step("ckv_n"))
                    kr = slice(Q_KR, P)
                    dve.tensor_tensor(tmp[kr, :], u[kr, :], cos_t[kr, :], ALU.mult).then_inc(vector.done, vector.step())
                    dve.wait_ge(x_kept, 16)
                    dve.wait_ge(tensor.done, tensor.at("k_swap"))
                    dve.tensor_tensor(au[kr, :], bank[7][kr, :], sin_t[kr, :], ALU.mult).then_inc(vector.done, vector.step("k_rot"))
                    dve.wait_ge(vector.done, vector.n)
                    for h in range(H):
                        dve.tensor_tensor(k_mla[HD:96, h, :], tmp[kr, :], au[kr, :], ALU.add).then_inc(vector.done, vector.step(f"mla_k{h}"))
                        dve.wait_ge(vector.done, vector.n)
                    dve.wait_ge(scalar.done, scalar.at("q_up2"))
                    dve.tensor_tensor(q_cos, q_pe, cos_t[:, :], ALU.mult).then_inc(vector.done, vector.step())
                    dve.wait_ge(tensor.done, tensor.at("q_swap"))
                    dve.tensor_tensor(tmp[:, :], bank[7][:, :], sin_t[:, :], ALU.mult).then_inc(vector.done, vector.step("q_rot"))
                    dve.wait_ge(vector.done, vector.n)
                    for h in range(H):
                        r = slice(32 * h, 32 * h + 32)
                        dve.tensor_tensor(q_mla[HD:96, h, :], q_cos[r, :], tmp[r, :], ALU.add).then_inc(vector.done, vector.step(f"mla_q{h}"))

                def att_a(a):
                    kind, h = a
                    scale = HEAD_SCALE if kind == "moba" else MLA_SCALE
                    dve.wait_ge(tensor.done, tensor.at(f"att_s{a}"))
                    m = mx[:, h % 2, :]
                    for i in range(NT):
                        b, off = BANK_OF[NT - 1 - i]
                        ins = dve.reduce_max(m[:, i:i + 1], bank[2 + b][:, off:off + (i + 1) * P], AX.X)
                        ins.then_inc(vector.done, vector.step())
                    dve.wait_ge(vector.done, vector.n)
                    dve.tensor_scalar(m[:, NT:2 * NT], m[:, 0:NT], -scale, None, ALU.mult).then_inc(vector.done, vector.step(f"att_m{a}"))
                    dve.wait_ge(scalar.done, scalar.at(f"att_e{a}"))
                    dve.reciprocal(m[:, 3 * NT:4 * NT], m[:, 2 * NT:3 * NT]).then_inc(vector.done, vector.step())
                    dve.wait_ge(vector.done, vector.n)
                    for i in (3, 2, 0, 1):
                        at, n = PACK[NT - 1 - i], (i + 1) * P
                        part = tri[:, h % 2, at:at + n]
                        dve.tensor_scalar(part, part, m[:, 3 * NT + i:3 * NT + i + 1], None, ALU.mult).then_inc(vector.done, vector.step(f"att_p{i}{a}"))

                def att_b(a):
                    n = unit_at[a[0]] + a[1] - 1 - 2 * H
                    if n >= 0:
                        dve.wait_ge(tensor.done, tensor.at(f"att_y{(('moba', 'mla')[n // H], n % H)}"))
                    dve.wait_ge(tensor.done, tensor.at(f"att_t1{a}"))
                    dve.tensor_copy(probT[:, 0:3, 2 * P:3 * P], bank[7][:, 0:3 * P].rearrange("p (j t) -> p j t", j=3)).then_inc(vector.done, vector.step())
                    dve.tensor_copy(probT[:, 0, 0:P], bank[7][:, 3 * P:T]).then_inc(vector.done, vector.step(f"att_t1{a}"))

                def gated(kind, y, gate, ready, sq, g, out):
                    dve.wait_ge(scalar.done, scalar.at(ready))
                    for j in range(2):
                        dve.tensor_tensor(y[j], y[j], gate[:, j, :], ALU.mult).then_inc(vector.done, vector.step())
                        dve.wait_ge(vector.done, vector.n)
                        dve.tensor_tensor(sq[j], y[j], y[j], ALU.mult).then_inc(vector.done, vector.step(f"{kind}_sq{j}"))
                    for j in range(2):
                        dve.wait_ge(scalar.done, scalar.at(f"{kind}_rstd{j}"))
                        dve.scalar_tensor_tensor(mixed[:, out + j, :], y[j], pcol(g, j), rstds[j][:, :], ALU.mult, ALU.mult).then_inc(vector.done, vector.step(f"{kind}_n{j}"))

                def fin_a(_):
                    gated("ssd", ssd_y, zs, "silu_z", ssd_sq, "ssm_g", 2)

                def fin_b(_):
                    gated("ml", ml_h, os_, "sig_o", ml_sq, "ml_g", 4)

                def out(_):
                    dve.wait_ge(x_again, 16)
                    for i in range(NT):
                        dve.wait_ge(tensor.done, tensor.at(f"out{i}"))
                        for half in range(2):
                            part = x2[:, i, half * 512:(half + 1) * 512]
                            m = dve.tensor_tensor(part, part, bank[2 * i + half][:, :], ALU.add)
                        m.then_inc(vector.done, vector.step(f"x{i}"))
                        normalise(dve, scalar, vector, x2[:, i, :], h_tm[:, i, :], ms, i)

                do = dict(norm=norm, proj=proj, gates=gates, gate_cols=gate_cols, xdt=xdt_, ssd_a=ssd_a, ssd_b=ssd_b,
                          ml_a=ml_a, ml_b=ml_b, att_a=att_a, att_b=att_b, mla_norm=mla_norm, mla_up=mla_up,
                          fin_a=fin_a, fin_b=fin_b, out=out)
                for op, arg in plan:
                    if op in do:
                        do[op](arg)

            @block.gpsimd
            def _(pool):
                pool.memset(zero[:, :], 0.0).then_inc(gpsimd.done, gpsimd.step("zero"))
                pool.memset(raw[:, :, 0:3], 0.0).then_inc(gpsimd.done, gpsimd.step("pads"))
                pool.memset(v_aug[:, :, :, HD:P], 1.0).then_inc(gpsimd.done, gpsimd.step("ones"))
        clear(nc, steps, sems)
        record(seen, steps)


def moe(nc, A, known, seen, layer, bank, C, ccols, token_bf, par, pcol, x2, x_tm, h_tm, ms, eps, spare_zeroed):
    with ExitStack() as ctx:
        def sb(name, shape, dt=F32):
            return ctx.enter_context(nc.sbuf_tensor(name, shape, dt))

        h2T = sb("h2T", [P, KD, T])
        wring = sb("wring", [P, 2, 3, 2048])
        xe = sb("xe", [P, 2, D])
        xeT = sb("xeT", [P, 2, KD, P])
        act_g = sb("act_g", [P, 2, DE])
        hid = sb("hid", [P, 2, DE])
        hidT = sb("hidT", [P, 2, 2, P])
        ye = sb("ye", [P, 2, D])
        w_rt = sb("w_rt", [P, KD, NR])
        lg = sb("lg", [P, NT, NR])
        sm = sb("sm", [P, 24, NT])
        oh_g = sb("oh_g", [P, NT, NG])
        oh_e = sb("oh_e", [P, 2, NT, EG])
        el = sb("el", [P, NT, EG])
        tmp4 = sb("tmp4", [P, NT, NG])
        tmp16 = sb("tmp16", [P, NT, NE])
        chosen = sb("chosen", [P, 3, NT, NE])
        place = sb("place", [P, NT, NE])
        match = sb("match", [P, 2, NT, P], BF16)
        idx1 = sb("idx1", [P, 2], U32)
        rows_of = sb("rows_of", [P, 2, NT], U32)
        counts = sb("counts", [P, 2 * NE + 1], I32)
        cf = sb("cf", [P, 4, NE])
        weight = lambda c: sm[:, 8 + c, :]

        route_and_experts(nc, A, known, seen, layer, bank, C, ccols, token_bf, par, pcol, locals())
        most = nc.values_load(counts[0:1, NE:NE + 1], min_val=0, max_val=T)
        with nc.If(most > CAP):
            with nc.Fori(1, T // CAP) as again:
                with nc.Fori(0, NE) as e:
                    n = nc.values_load(counts[0:1, bass.ds(e, 1)], min_val=0, max_val=T)
                    base = nc.values_load(counts[0:1, bass.ds(e + NE + 1, 1)], min_val=NE, max_val=NE + SPARE - T // CAP + 1)
                    with nc.If(n > again * CAP):
                        one_pass(nc, A, known, seen, layer, e, again, base, bank, C, token_bf, pcol, locals())
                    nc.all_engine_barrier()
            nc.all_engine_barrier()
        nc.all_engine_barrier()
        combine(nc, A, known, seen, x2, rows_of, weight, xe, ye, h2T, x_tm, h_tm, ms, eps, spare_zeroed)


def route_and_experts(nc, A, known, seen, layer, bank, C, ccols, token_bf, par, pcol, B):
    h_tm, h2T, wring, xe, xeT, act_g, hid, hidT, ye = (B[n] for n in ("h_tm", "h2T", "wring", "xe", "xeT", "act_g", "hid", "hidT", "ye"))
    w_rt, lg, sm, oh_g, oh_e, el, tmp4, tmp16, chosen, place = (B[n] for n in ("w_rt", "lg", "sm", "oh_g", "oh_e", "el", "tmp4", "tmp16", "chosen", "place"))
    match, idx1, rows_of, counts, weight = (B[n] for n in ("match", "idx1", "rows_of", "counts", "weight"))
    cf = B["cf"]
    rank = ccols[:, COLS["rank"][0]:COLS["rank"][0] + EG].rearrange("p (o e) -> p o e", o=1).to_broadcast([P, NT, EG])
    first_row1 = ccols[:, COLS["first_row"][0]:COLS["first_row"][0] + NE]
    first_row = first_row1.rearrange("p (o e) -> p o e", o=1).to_broadcast([P, NT, NE])
    S_ = lambda i: sm[:, i, :]
    places = bank[6][:, 0:(NT + 1) * NE]

    def each(v, n):
        return v.rearrange("p (i o) -> p i o", o=1).to_broadcast([P, NT, n])

    with ExitStack() as ctx:
        tensor, scalar, vector, gpsimd = steps = engine_steps(nc, ctx, known, "moe")
        names = ("router_in", "h_stored", "matched", "found", "turned", "turned_out", "gu", "gated", "hidden", "hid_turned", "hid_out",
                 "down", "y_low", "y_high", "idx_at", "xe_in0", "xe_in1", "y_stored0", "y_stored1",
                 "w_in00", "w_in01", "w_in02", "w_in10", "w_in11", "w_in12")
        Q = {n: ctx.enter_context(nc.semaphore(n)) for n in names}

        def wait(eng, name, n):
            if isinstance(n, int) and n <= 0:
                return
            eng.wait_ge(Q[name], n)

        with nc.allow_low_precision(reason="counts below 2 ** 24 are exact in float32 and as integers"), nc.Block() as block:
            @block.sync
            def _(sp):
                sp.dma_start(w_rt[:, :, :], A["w_router"][bass.ds(layer, 1), :, :, :].rearrange("o p k n -> (o p) k n")).then_inc(Q["router_in"], 16)

                def load(e, two, parts):
                    for part in parts:
                        src = A["w_moe"][bass.ds(layer * NE + e, 1), part, :, :].rearrange("o p n -> (o p) n")
                        sp.dma_start(wring[:, two, part, :], src).then_inc(Q[f"w_in{two}{part}"], 16)

                sp.dma_start(A["h2"].rearrange("(i p) d -> p i d", p=P), h_tm).then_inc(Q["h_stored"], 16)
                load(0, 0, (0, 1, 2))
                load(1, 1, (0, 1, 2))

                def step(e, two, before):
                    static_last = isinstance(e, int) and e + 2 >= NE
                    if not static_last:
                        wait(sp, "gu", e + 1)
                        load(e + 2, two, (0, 1))
                        wait(sp, "down", e + 1)
                        load(e + 2, two, (2,))
                    wait(sp, "y_low", e + 1)
                    wait(sp, "y_high", e + 1)
                    sp.dma_start(A["y"][bass.ds(e * CAP, CAP), :], ye[:, two, :]).then_inc(Q[f"y_stored{two}"], 16)

                step(0, 0, 0)
                with sp.Fori(0, NE // 2 - 2) as n:
                    step(2 * n + 1, 1, n)
                    step(2 * n + 2, 0, n + 1)
                step(NE - 3, 1, NE // 2 - 2)
                step(NE - 2, 0, NE // 2 - 1)
                step(NE - 1, 1, NE // 2 - 1)
                for two in range(2):
                    sp.wait_ge(Q[f"y_stored{two}"], 16 * (NE // 2))
                sp.wait_ge(Q["h_stored"], 16)

            @block.gpsimd
            def _(pool):
                pool.memset(cf[:, 3, :], 0.0).then_inc(gpsimd.done, gpsimd.step("zeros"))

                pool.wait_ge(Q["h_stored"], 16)
                for e in range(NE):
                    wait(pool, "idx_at", e + 1)
                    pool.indirect_dma_start(xe[:, e % 2, :], None, A["h2"], bass.IndirectOffsetOnAxis(ap=idx1[:, e % 2:e % 2 + 1], axis=0))\
                        .then_inc(Q[f"xe_in{e % 2}"], 16)
                for two in range(2):
                    pool.wait_ge(Q[f"xe_in{two}"], 16 * (NE // 2))
                forget(pool, Q["xe_in0"], Q["xe_in1"])

            @block.tensor
            def _(pe):

                def mm(out, lhsT, rhs, start, stop):
                    return pe.matmul(out, lhsT, rhs, start=start, stop=stop, skip_group_check=True)

                for k in range(KD):
                    for i in range(NT):
                        m = pe.transpose(bank[k][:, i * P:(i + 1) * P], h_tm[:, i, k * P:(k + 1) * P], C["ident"])
                    m.then_inc(tensor.done, tensor.step(f"hT{k}"))
                pe.wait_ge(Q["router_in"], 16)
                pe.wait_ge(scalar.done, scalar.at(f"hT{KD - 2}"))
                pe.wait_ge(vector.done, vector.at(f"hT{KD - 1}"))
                for i in range(NT):
                    for k in range(KD):
                        m = mm(bank[0][:, i * NR:(i + 1) * NR], h2T[:, k, i * P:(i + 1) * P], w_rt[:, k, :], k == 0, k == KD - 1)
                m.then_inc(tensor.done, tensor.step("logits"))
                pe.wait_ge(vector.done, vector.at("chosen"))
                for i in range(NT):
                    for j in range(i + 1):
                        mm(places[:, i * NE:(i + 1) * NE], C["before"] if j == i else C["ones"], chosen[:, 2, j, :], j == 0, j == i)
                for j in range(NT):
                    m = mm(places[:, NT * NE:NT * NE + NE], C["ones"], chosen[:, 2, j, :], j == 0, j == NT - 1)
                m.then_inc(tensor.done, tensor.step("places"))

                def find(e, two):
                    wait(pe, "matched", e + 1)
                    wait(pe, "idx_at", e)
                    for i in range(NT):
                        m = mm(bank[7][:, 2 * two:2 * two + 2], match[:, two, i, :], token_bf[:, i, :], i == 0, i == NT - 1)
                    m.then_inc(Q["found"], 1)

                def turn(e, two, times):
                    pe.wait_ge(Q[f"xe_in{two}"], 16 * (times + 1))
                    wait(pe, "turned_out", e)
                    for k in range(KD):
                        m = pe.transpose(bank[k // 4][:, (k % 4) * P:(k % 4 + 1) * P], xe[:, two, k * P:(k + 1) * P], C["ident"])
                    m.then_inc(Q["turned"], 1)

                def gate_up(e, two, times):
                    wait(pe, "turned_out", e + 1)
                    wait(pe, "hidden", e - 1)
                    for part in range(2):
                        pe.wait_ge(Q[f"w_in{two}{part}"], 16 * (times + 1))
                        for j in range(4):
                            m = mm(bank[2 + two][:, :], xeT[:, two, 4 * part + j, :], wring[:, two, part, j * 512:(j + 1) * 512],
                                   part + j == 0, part * j == 3)
                    m.then_inc(Q["gu"], 1)

                def down(e, two, times):
                    wait(pe, "hid_out", e + 1)
                    pe.wait_ge(Q[f"w_in{two}2"], 16 * (times + 1))
                    wait(pe, "y_low", e)
                    wait(pe, "y_high", e)
                    for half in range(2):
                        for f in range(2):
                            m = mm(bank[5 + half][:, :], hidT[:, two, f, :], wring[:, two, 2, f * D + half * 512:f * D + half * 512 + 512], f == 0, f == 1)
                    m.then_inc(Q["down"], 1)

                def turn_hidden(e, two, times):
                    wait(pe, "hidden", e + 1)
                    wait(pe, "hid_out", e)
                    for f in range(2):
                        m = pe.transpose(bank[4][:, f * P:(f + 1) * P], hid[:, two, f * P:(f + 1) * P], C["ident"])
                    m.then_inc(Q["hid_turned"], 1)

                find(0, 0)
                find(1, 1)
                turn(0, 0, 0)
                gate_up(0, 0, 0)
                turn(1, 1, 0)
                turn_hidden(0, 0, 0)

                def step(e, two, times, last=False):
                    gate_up(e, two, times)
                    if not last:
                        turn(e + 1, 1 - two, times + two)
                    down(e - 1, 1 - two, times - (1 - two))
                    if not (isinstance(e, int) and e + 2 >= NE):
                        find(e + 2, two)
                    turn_hidden(e, two, times)

                find(2, 0)
                step(1, 1, 0)
                step(2, 0, 1)
                with pe.Fori(1, NE // 2 - 2) as n:
                    step(2 * n + 1, 1, n)
                    step(2 * n + 2, 0, n + 1)
                step(NE - 3, 1, NE // 2 - 2)
                step(NE - 2, 0, NE // 2 - 1)
                step(NE - 1, 1, NE // 2 - 1, True)
                down(NE - 1, 1, NE // 2 - 1)

            @block.scalar
            def _(act):
                for k in range(0, KD, 2):
                    act.wait_ge(tensor.done, tensor.at(f"hT{k}"))
                    act.activation(h2T[:, k, :], bank[k][:, :], ACT.Identity, scale=pcol("g_ffn", k)).then_inc(scalar.done, scalar.step(f"hT{k}"))
                act.wait_ge(vector.done, vector.at("group_less_max"))
                act.activation(tmp4[:, :, :], tmp4[:, :, :], ACT.Exp).then_inc(scalar.done, scalar.step("group_exp"))
                act.wait_ge(vector.done, vector.at("second_less_first"))
                act.activation(S_(4), S_(4), ACT.Exp).then_inc(scalar.done, scalar.step("second_exp"))

                def gate(e, two, times):
                    wait(act, "gu", e + 1)
                    wait(act, "hidden", e - 1)
                    act.activation(act_g[:, two, :], bank[2 + two][:, 0:DE], ACT.Silu).then_inc(Q["gated"], 1)

                def hidden_out(e, two, times):
                    wait(act, "hid_turned", e + 1)
                    wait(act, "down", e - 1)
                    act.activation(hidT[:, two, :, :], bank[4][:, 0:DE].rearrange("p (f s) -> p f s", f=2), ACT.Copy).then_inc(Q["hid_out"], 1)

                def y_out(e, two, times):
                    wait(act, "down", e + 1)
                    if not (isinstance(e, int) and e < 2):
                        act.wait_ge(Q[f"y_stored{two}"], 16 * times)
                    act.activation(ye[:, two, 0:512], bank[5][:, :], ACT.Copy).then_inc(Q["y_low"], 1)

                gate(0, 0, 0)
                hidden_out(0, 0, 0)
                gate(1, 1, 0)
                y_out(0, 0, 0)
                hidden_out(1, 1, 0)
                gate(2, 0, 1)
                y_out(1, 1, 0)
                hidden_out(2, 0, 1)

                def step(e, two, times):
                    gate(e, two, times)
                    y_out(e - 1, 1 - two, times - (1 - two))
                    hidden_out(e, two, times)
                with act.Fori(1, NE // 2 - 1) as n:
                    step(2 * n + 1, 1, n)
                    step(2 * n + 2, 0, n + 1)
                step(NE - 1, 1, NE // 2 - 1)
                y_out(NE - 1, 1, NE // 2 - 1)

            @block.vector
            def _(dve):
                tt, ts, stt = dve.tensor_tensor, dve.tensor_scalar, dve.scalar_tensor_tensor
                for k in range(1, KD, 2):
                    dve.wait_ge(tensor.done, tensor.at(f"hT{k}"))
                    ts(h2T[:, k, :], bank[k][:, :], pcol("g_ffn", k), None, ALU.mult).then_inc(vector.done, vector.step(f"hT{k}"))
                dve.wait_ge(tensor.done, tensor.at("logits"))
                bias = par[:, PARAMS["router_b"][0]:PARAMS["router_b"][0] + NR].rearrange("p (o n) -> p o n", o=1).to_broadcast([P, NT, NR])
                tt(lg[:, :, :], bank[0][:, 0:NT * NR].rearrange("p (i n) -> p i n", i=NT), bias, ALU.add).then_inc(vector.done, vector.step())
                dve.wait_ge(vector.done, vector.n)

                def first_max(values, best, onehot):
                    dve.tensor_reduce(best, values, AX.X, ALU.max).then_inc(vector.done, vector.step())
                    dve.wait_ge(vector.done, vector.n)
                    tt(onehot, values, each(best, EG), ALU.is_equal).then_inc(vector.done, vector.step())
                    dve.wait_ge(vector.done, vector.n)
                    tt(onehot, onehot, rank, ALU.mult).then_inc(vector.done, vector.step())
                    dve.wait_ge(vector.done, vector.n)
                    dve.tensor_reduce(S_(1), onehot, AX.X, ALU.max).then_inc(vector.done, vector.step())
                    dve.wait_ge(vector.done, vector.n)
                    tt(onehot, onehot, each(S_(1), EG), ALU.is_equal).then_inc(vector.done, vector.step())
                    dve.wait_ge(vector.done, vector.n)

                first_max(lg[:, :, 0:NG], S_(0), oh_g[:, :, :])
                tt(tmp4[:, :, :], lg[:, :, 0:NG], each(S_(0), NG), ALU.subtract).then_inc(vector.done, vector.step("group_less_max"))
                for g_ in range(NG):
                    lg_g = lg[:, :, NG + g_ * EG:NG + (g_ + 1) * EG]
                    one = oh_g[:, :, g_:g_ + 1].to_broadcast([P, NT, EG])
                    if g_ == 0:
                        tt(el[:, :, :], lg_g, one, ALU.mult).then_inc(vector.done, vector.step())
                        dve.wait_ge(vector.done, vector.n)
                    else:
                        tt(oh_e[:, 0, :, :], lg_g, one, ALU.mult).then_inc(vector.done, vector.step())
                        dve.wait_ge(vector.done, vector.n)
                        tt(el[:, :, :], el[:, :, :], oh_e[:, 0, :, :], ALU.add).then_inc(vector.done, vector.step())
                        dve.wait_ge(vector.done, vector.n)
                first_max(el[:, :, :], S_(2), oh_e[:, 0, :, :])
                stt(el[:, :, :], oh_e[:, 0, :, :], NEG, el[:, :, :], ALU.mult, ALU.add).then_inc(vector.done, vector.step())
                dve.wait_ge(vector.done, vector.n)
                first_max(el[:, :, :], S_(3), oh_e[:, 1, :, :])
                tt(S_(4), S_(3), S_(2), ALU.subtract).then_inc(vector.done, vector.step("second_less_first"))
                for c in range(2):
                    for g_ in range(NG):
                        m = tt(chosen[:, c, :, g_ * EG:(g_ + 1) * EG], oh_e[:, c, :, :], oh_g[:, :, g_:g_ + 1].to_broadcast([P, NT, EG]), ALU.mult)
                        m.then_inc(vector.done, vector.step())
                dve.wait_ge(vector.done, vector.n)
                tt(chosen[:, 2, :, :], chosen[:, 0, :, :], chosen[:, 1, :, :], ALU.add).then_inc(vector.done, vector.step("chosen"))
                dve.wait_ge(vector.done, vector.n)
                dve.wait_ge(tensor.done, tensor.at("places"))
                pos = places[:, 0:NT * NE].rearrange("p (i e) -> p i e", i=NT)
                stt(place[:, :, :], pos, 1.0, chosen[:, 2, :, :], ALU.add, ALU.mult).then_inc(vector.done, vector.step())
                dve.wait_ge(vector.done, vector.n)
                ts(place[:, :, :], place[:, :, :], -1.0, None, ALU.add).then_inc(vector.done, vector.step("place"))
                dve.wait_ge(vector.done, vector.n)
                def match_tokens(e, two):
                    wait(dve, "found", e - 1)
                    iota = C["iota"].rearrange("p (o s) -> p o s", o=1).to_broadcast([P, NT, P])
                    at = place[:, :, e:e + 1] if isinstance(e, int) else place[:, :, bass.ds(e, 1)]
                    tt(match[:, two, :, :], iota, at.to_broadcast([P, NT, P]), ALU.is_equal).then_inc(Q["matched"], 1)

                def index(e, two, times):
                    wait(dve, "found", e + 1)
                    if not (isinstance(e, int) and e < 2):
                        dve.wait_ge(Q[f"xe_in{two}"], 16 * times)
                    dve.tensor_reduce(idx1[:, two:two + 1], bank[7][:, 2 * two:2 * two + 2], AX.X, ALU.add).then_inc(Q["idx_at"], 1)

                match_tokens(0, 0)
                match_tokens(1, 1)
                index(0, 0, 0)
                index(1, 1, 0)
                dve.wait_ge(scalar.done, scalar.at("group_exp"))
                dve.reduce_sum(S_(5), tmp4[:, :, :], AX.X).then_inc(vector.done, vector.step())
                dve.wait_ge(vector.done, vector.n)
                dve.wait_ge(scalar.done, scalar.at("second_exp"))
                ts(S_(6), S_(4), 1.0, None, ALU.add).then_inc(vector.done, vector.step())
                dve.wait_ge(vector.done, vector.n)
                tt(S_(6), S_(6), S_(5), ALU.mult).then_inc(vector.done, vector.step())
                dve.wait_ge(vector.done, vector.n)
                dve.reciprocal(weight(0), S_(6)).then_inc(vector.done, vector.step())
                dve.wait_ge(vector.done, vector.n)
                tt(weight(1), weight(0), S_(4), ALU.mult).then_inc(vector.done, vector.step())
                dve.wait_ge(vector.done, vector.n)
                dve.tensor_copy(counts[:, 0:NE], places[:, NT * NE:NT * NE + NE]).then_inc(vector.done, vector.step())
                dve.reduce_max(counts[:, NE:NE + 1], places[:, NT * NE:NT * NE + NE], AX.X).then_inc(vector.done, vector.step())
                dve.wait_ge(vector.done, vector.n)
                dve.wait_ge(gpsimd.done, gpsimd.at("zeros"))
                dve.tensor_copy(cf[:, 0, :], counts[:, 0:NE]).then_inc(vector.done, vector.step())
                dve.wait_ge(vector.done, vector.n)
                ts(cf[:, 1, :], cf[:, 0, :], float(CAP), None, ALU.is_gt).then_inc(vector.done, vector.step())
                dve.wait_ge(vector.done, vector.n)
                for again in range(2, T // CAP):
                    stt(cf[:, 1, :], cf[:, 0, :], float(again * CAP), cf[:, 1, :], ALU.is_gt, ALU.add).then_inc(vector.done, vector.step())
                    dve.wait_ge(vector.done, vector.n)
                dve.tensor_tensor_scan(cf[:, 2, :], cf[:, 1, :], cf[:, 3, :], float(NE), ALU.add, ALU.add).then_inc(vector.done, vector.step())
                dve.wait_ge(vector.done, vector.n)
                tt(cf[:, 2, :], cf[:, 2, :], cf[:, 1, :], ALU.subtract).then_inc(vector.done, vector.step())
                dve.wait_ge(vector.done, vector.n)
                dve.tensor_copy(counts[:, NE + 1:2 * NE + 1], cf[:, 2, :]).then_inc(vector.done, vector.step())
                dve.wait_ge(vector.done, vector.n)
                ts(cf[:, 2, :], cf[:, 2, :], float(CAP), -float(CAP), ALU.mult, ALU.add).then_inc(vector.done, vector.step())
                dve.wait_ge(vector.done, vector.n)
                tt(cf[:, 2, :], cf[:, 2, :], first_row1, ALU.subtract).then_inc(vector.done, vector.step())
                dve.wait_ge(vector.done, vector.n)
                further = cf[:, 2, :].rearrange("p (o e) -> p o e", o=1).to_broadcast([P, NT, NE])
                stt(tmp16[:, :, :], place[:, :, :], float(CAP), further, ALU.is_ge, ALU.mult).then_inc(vector.done, vector.step())
                dve.wait_ge(vector.done, vector.n)
                tt(tmp16[:, :, :], tmp16[:, :, :], place[:, :, :], ALU.add).then_inc(vector.done, vector.step())
                dve.wait_ge(vector.done, vector.n)
                tt(tmp16[:, :, :], tmp16[:, :, :], first_row, ALU.add).then_inc(vector.done, vector.step())
                dve.wait_ge(vector.done, vector.n)
                for c in range(2):
                    tt(chosen[:, c, :, :], chosen[:, c, :, :], tmp16[:, :, :], ALU.mult).then_inc(vector.done, vector.step())
                    dve.wait_ge(vector.done, vector.n)
                    dve.tensor_reduce(rows_of[:, c, :], chosen[:, c, :, :], AX.X, ALU.add).then_inc(vector.done, vector.step())

                def turned_out(e, two, times):
                    wait(dve, "turned", e + 1)
                    wait(dve, "gu", e - 1)
                    for half in range(2):
                        gain = par[:, PARAMS["g_ffn"][0] + 4 * half:PARAMS["g_ffn"][0] + 4 * half + 4].rearrange("p (k o) -> p k o", o=1)
                        m = tt(xeT[:, two, 4 * half:4 * half + 4, :], bank[half][:, :].rearrange("p (k s) -> p k s", k=4),
                               gain.to_broadcast([P, 4, P]), ALU.mult)
                    m.then_inc(Q["turned_out"], 1)

                def hidden(e, two, times):
                    wait(dve, "gated", e + 1)
                    wait(dve, "hid_turned", e - 1)
                    tt(hid[:, two, :], bank[2 + two][:, DE:2 * DE], act_g[:, two, :], ALU.mult).then_inc(Q["hidden"], 1)

                def y_out(e, two, times):
                    wait(dve, "down", e + 1)
                    if not (isinstance(e, int) and e < 2):
                        dve.wait_ge(Q[f"y_stored{two}"], 16 * times)
                    dve.tensor_copy(ye[:, two, 512:D], bank[6][:, :]).then_inc(Q["y_high"], 1)

                def step(e, two, times, ahead=True):
                    if ahead:
                        turned_out(e + 1, 1 - two, times + two)
                    more = not (isinstance(e, int) and e + 2 >= NE)
                    if more:
                        match_tokens(e + 2, two)
                    hidden(e, two, times)
                    if more:
                        index(e + 2, two, times + 1)
                    if not (isinstance(e, int) and e == 0):
                        y_out(e - 1, 1 - two, times - (1 - two))

                turned_out(0, 0, 0)
                step(0, 0, 0)
                step(1, 1, 0)
                step(2, 0, 1)
                with dve.Fori(1, NE // 2 - 2) as n:
                    step(2 * n + 1, 1, n)
                    step(2 * n + 2, 0, n + 1)
                step(NE - 3, 1, NE // 2 - 2)
                step(NE - 2, 0, NE // 2 - 1)
                step(NE - 1, 1, NE // 2 - 1, False)
                y_out(NE - 1, 1, NE // 2 - 1)
        clear(nc, steps, Q.values())
        record(seen, steps)


def one_pass(nc, A, known, seen, layer, e, again, base, bank, C, token_bf, pcol, B):
    wring, xe, xeT, act_g, hid, hidT, ye, place, match, idx1, par = (
        B[n] for n in ("wring", "xe", "xeT", "act_g", "hid", "hidT", "ye", "place", "match", "idx1", "par"))
    with ExitStack() as ctx:
        tensor, scalar, vector, gpsimd = steps = engine_steps(nc, ctx, known, "pass")
        loaded, gathered, stored = (ctx.enter_context(nc.semaphore(n)) for n in ("pass_loaded", "pass_gathered", "pass_stored"))
        with nc.allow_low_precision(reason="token numbers are exact in float32 and as integers"), nc.Block() as block:
            @block.sync
            def _(sp):
                for part in range(3):
                    sp.dma_start(wring[:, 0, part, :], A["w_moe"][bass.ds(layer * NE + e, 1), part, :, :].rearrange("o p n -> (o p) n")).then_inc(loaded, 16)
                sp.wait_ge(vector.done, vector.at("y"))
                sp.dma_start(A["y"][bass.ds((base + again - 1) * CAP, CAP), :], ye[:, 0, :]).then_inc(stored, 16)
                sp.wait_ge(stored, 16)

            @block.gpsimd
            def _(pool):
                pool.wait_ge(vector.done, vector.at("idx"))
                pool.indirect_dma_start(xe[:, 0, :], None, A["h2"], bass.IndirectOffsetOnAxis(ap=idx1[:, 0:1], axis=0)).then_inc(gathered, 16)
                pool.wait_ge(gathered, 16)
                forget(pool, gathered)

            @block.tensor
            def _(pe):

                def mm(out, lhsT, rhs, start, stop):
                    return pe.matmul(out, lhsT, rhs, start=start, stop=stop, skip_group_check=True)
                pe.wait_ge(vector.done, vector.at("match"))
                for i in range(NT):
                    m = mm(bank[7][:, 0:2], match[:, 0, i, :], token_bf[:, i, :], i == 0, i == NT - 1)
                m.then_inc(tensor.done, tensor.step("idx"))
                pe.wait_ge(gathered, 16)
                for k in range(KD):
                    m = pe.transpose(bank[k // 4][:, (k % 4) * P:(k % 4 + 1) * P], xe[:, 0, k * P:(k + 1) * P], C["ident"])
                m.then_inc(tensor.done, tensor.step("turned"))
                pe.wait_ge(loaded, 48)
                pe.wait_ge(vector.done, vector.at("turned"))
                for k in range(KD):
                    m = mm(bank[2][:, :], xeT[:, 0, k, :], wring[:, 0, k // 4, (k % 4) * 512:(k % 4 + 1) * 512], k == 0, k == KD - 1)
                m.then_inc(tensor.done, tensor.step("gu"))
                pe.wait_ge(vector.done, vector.at("hid"))
                for f in range(2):
                    m = pe.transpose(bank[4][:, f * P:(f + 1) * P], hid[:, 0, f * P:(f + 1) * P], C["ident"])
                m.then_inc(tensor.done, tensor.step("hid"))
                pe.wait_ge(vector.done, vector.at("hidT"))
                for half in range(2):
                    for f in range(2):
                        m = mm(bank[5 + half][:, :], hidT[:, 0, f, :], wring[:, 0, 2, f * D + half * 512:f * D + half * 512 + 512], f == 0, f == 1)
                m.then_inc(tensor.done, tensor.step("down"))

            @block.scalar
            def _(act):
                act.wait_ge(tensor.done, tensor.at("gu"))
                act.activation(act_g[:, 0, :], bank[2][:, 0:DE], ACT.Silu).then_inc(scalar.done, scalar.step("gate"))

            @block.vector
            def _(dve):
                iota = C["iota"].rearrange("p (o s) -> p o s", o=1).to_broadcast([P, NT, P])
                dve.tensor_scalar(B["tmp16"][:, :, 0:1], place[:, :, bass.ds(e, 1)], -float(CAP), None, ALU.add).then_inc(vector.done, vector.step())
                dve.wait_ge(vector.done, vector.n)
                dve.tensor_copy(place[:, :, bass.ds(e, 1)], B["tmp16"][:, :, 0:1]).then_inc(vector.done, vector.step())
                dve.wait_ge(vector.done, vector.n)
                dve.tensor_tensor(match[:, 0, :, :], iota, B["tmp16"][:, :, 0:1].to_broadcast([P, NT, P]), ALU.is_equal).then_inc(vector.done, vector.step("match"))
                dve.wait_ge(tensor.done, tensor.at("idx"))
                dve.tensor_reduce(idx1[:, 0:1], bank[7][:, 0:2], AX.X, ALU.add).then_inc(vector.done, vector.step("idx"))
                dve.wait_ge(tensor.done, tensor.at("turned"))
                for half in range(2):
                    gain = par[:, PARAMS["g_ffn"][0] + 4 * half:PARAMS["g_ffn"][0] + 4 * half + 4].rearrange("p (k o) -> p k o", o=1)
                    m = dve.tensor_tensor(xeT[:, 0, 4 * half:4 * half + 4, :], bank[half][:, :].rearrange("p (k s) -> p k s", k=4),
                                          gain.to_broadcast([P, 4, P]), ALU.mult)
                m.then_inc(vector.done, vector.step("turned"))
                dve.wait_ge(scalar.done, scalar.at("gate"))
                dve.tensor_tensor(hid[:, 0, :], bank[2][:, DE:2 * DE], act_g[:, 0, :], ALU.mult).then_inc(vector.done, vector.step("hid"))
                dve.wait_ge(tensor.done, tensor.at("hid"))
                dve.tensor_copy(hidT[:, 0, :, :], bank[4][:, 0:DE].rearrange("p (f s) -> p f s", f=2)).then_inc(vector.done, vector.step("hidT"))
                dve.wait_ge(tensor.done, tensor.at("down"))
                dve.tensor_copy(ye[:, 0, 0:512], bank[5][:, :]).then_inc(vector.done, vector.step())
                dve.tensor_copy(ye[:, 0, 512:D], bank[6][:, :]).then_inc(vector.done, vector.step("y"))
        clear(nc, steps, [loaded, gathered, stored])
        record(seen, steps)


def combine(nc, A, known, seen, x2, rows_of, weight, xe, ye, h2T, x_tm, h_tm, ms, eps, spare_zeroed):
    spare = h2T[:, :, :].rearrange("p k t -> p (k t)").rearrange("p (n d) -> p n d", d=D)
    bufs = [xe[:, 0, :], xe[:, 1, :], ye[:, 0, :], ye[:, 1, :], *(spare[:, i, :] for i in range(4))]
    with ExitStack() as ctx:
        tensor, scalar, vector, gpsimd = steps = engine_steps(nc, ctx, known, "combine")
        got = [ctx.enter_context(nc.semaphore(f"result_in{n}")) for n in range(2 * NT)]
        with nc.Block() as block:
            @block.gpsimd
            def _(pool):
                pool.wait_ge(spare_zeroed, 16 * SPARE)
                for i in range(NT):
                    for c in range(2):
                        n = 2 * i + c
                        pool.indirect_dma_start(bufs[n], None, A["y"], bass.IndirectOffsetOnAxis(ap=rows_of[:, c, i:i + 1], axis=0)).then_inc(got[n], 16)
                for n in range(2 * NT):
                    pool.wait_ge(got[n], 16)
                forget(pool, *got)

            @block.vector
            def _(dve):
                for i in range(NT):
                    dve.wait_ge(got[2 * i], 16)
                    dve.scalar_tensor_tensor(x2[:, i, :], bufs[2 * i], weight(0)[:, i:i + 1], x2[:, i, :], ALU.mult, ALU.add).then_inc(vector.done, vector.step())
                    dve.wait_ge(vector.done, vector.n)
                    dve.wait_ge(got[2 * i + 1], 16)
                    dve.scalar_tensor_tensor(x_tm[:, i, :], bufs[2 * i + 1], weight(1)[:, i:i + 1], x2[:, i, :], ALU.mult, ALU.add).then_inc(vector.done, vector.step(f"x{i}"))
                    if i:
                        normalise(dve, scalar, vector, x_tm[:, i - 1, :], h_tm[:, i - 1, :], ms, i - 1)
                normalise(dve, scalar, vector, x_tm[:, NT - 1, :], h_tm[:, NT - 1, :], ms, NT - 1)

            @block.scalar
            def _(act):
                for i in range(NT):
                    act.wait_ge(vector.done, vector.at(f"x{i}"))
                    root_mean_square(act, scalar, x_tm[:, i, :], h_tm[:, i, :], ms, eps, i)
        clear(nc, steps, got)
        record(seen, steps)


def final_norm(nc, A, known, seen, h_tm):
    with ExitStack() as ctx:
        sb = lambda name, shape: ctx.enter_context(nc.sbuf_tensor(name, shape, F32))
        g_row, o = sb("g_row", [P, D]), sb("o", [P, NT, D])
        tensor, scalar, vector, gpsimd = steps = engine_steps(nc, ctx, known, "final")
        loaded, stored = (ctx.enter_context(nc.semaphore(n)) for n in ("g_loaded", "out_stored"))
        with nc.Block() as block:
            @block.sync
            def _(sp):
                sp.dma_start(g_row[:, :], A["final_norm_g"].partition_broadcast(P)).then_inc(loaded, 16)
                for i in range(NT):
                    sp.wait_ge(vector.done, vector.at(f"o{i}"))
                    sp.dma_start(A["out"][i * P:(i + 1) * P, :], o[:, i, :]).then_inc(stored, 16)
                sp.wait_ge(stored, 16 * NT)

            @block.vector
            def _(dve):
                dve.wait_ge(loaded, 16)
                for i in range(NT):
                    dve.tensor_tensor(o[:, i, :], h_tm[:, i, :], g_row[:, :], ALU.mult).then_inc(vector.done, vector.step(f"o{i}"))
        record(seen, steps)


def constants():
    r = np.arange(P)
    m = {
        "ident": np.eye(P), "neg_row": np.where(r[None, :] <= r[:, None], 0, NEG),
        "neg_col": np.where(r[None, :] >= r[:, None], 0, NEG),
        "avg128": np.full((P, P), 1 / 128), "avg256": np.full((P, P), 1 / 256),
        "avg64": (r[:, None] // HD == r[None, :] // HD) / HD, "swap": np.eye(P)[r ^ 16],
        "before": (r[:, None] < r[None, :]), "ones": np.ones((P, P)), "iota": np.broadcast_to(r[None, :], (P, P)),
    }
    const = np.stack([np.asarray(m[n], np.float32) for n in CONSTS], 1)
    inv = np.float32(10000.0) ** (-(np.arange(16, dtype=np.float32) * 2) / np.float32(32))
    cols = np.zeros((P, NCOLS), np.float32)
    cols[:, 0], cols[:, 1] = inv[r % 16], np.where(r % 32 < 16, -1, 1)
    token = np.stack([np.broadcast_to(P * np.arange(NT), (P, NT)), np.broadcast_to(r[:, None], (P, NT))], -1)
    for name, v in (("token", token.reshape(P, -1)), ("rank", EG - np.arange(EG)), ("first_row", CAP * np.arange(NE))):
        cols[:, COLS[name][0]:sum(COLS[name])] = v
    return np.ascontiguousarray(const), cols


def layout(i):
    a = {n: np.asarray(v) for n, v in i.items()}

    def tiles(w):
        return w.reshape(w.shape[0], -1, P, w.shape[-1]).transpose(0, 2, 1, 3)

    w_in = a["w_in"]
    slots = np.zeros((L, len(SLOTS), P, KD, 256), np.float32)
    for n, name in enumerate(SLOTS):
        width = 128 if name == "ckv" else 256
        slots[:, n, :, :, :width] = tiles(w_in[:, :, W_IN_AT[name]:W_IN_AT[name] + width])
    small = np.zeros((L, D, P), np.float32)
    for at, src, n in ((Q_DT, W_DT, H), (Q_IG, W_IG, H), (Q_FG, W_FG, H), (Q_KR, W_KR, 32)):
        small[:, :, at:at + n] = w_in[:, :, src:src + n]
    uq = a["mla_w_uq"].reshape(L, GW, H, 96)
    uq = np.concatenate([uq[..., :HD].reshape(L, GW, GW), uq[..., HD:].reshape(L, GW, P)], -1)
    ukv = a["mla_w_ukv"].reshape(L, P, H, P)
    ukv = np.concatenate([ukv[..., :HD].reshape(L, P, GW), ukv[..., HD:].reshape(L, P, GW)], -1)
    w_out = a["w_out"].reshape(L, 4, 2, P, D).transpose(0, 1, 3, 2, 4).reshape(L, 4, P, KD, 256)

    par = np.zeros((L, P, NPAR), np.float32)

    def put(name, cols):
        par[:, :, PARAMS[name][0]:PARAMS[name][0] + cols.shape[-1]] = cols

    columns = lambda v: v.reshape(L, -1, P).transpose(0, 2, 1)
    put("g_mix", columns(a["norm_mix_g"]))
    put("g_ffn", columns(a["norm_ffn_g"]))
    cw = np.concatenate([a["ssm_conv_w"], a["ml_conv_w"]], -1)
    put("conv_w", cw.reshape(L, 4, 10, P).transpose(0, 3, 2, 1).reshape(L, P, 40))
    put("conv_b", columns(np.concatenate([a["ssm_conv_b"], a["ml_conv_b"]], -1)))
    gate = np.zeros((L, P, 1), np.float32)
    for at, name in ((Q_DT, "ssm_dt_bias"), (Q_IG, "ml_ig_bias"), (Q_FG, "ml_fg_bias")):
        gate[:, at:at + H, 0] = a[name]
    put("gate_b", gate)
    log = np.zeros((L, P, 1), np.float32)
    log[:, 0:H, 0] = a["ssm_a_log"]
    put("a_log", log)
    put("d_skip", columns(np.repeat(a["ssm_d"], HD, -1)))
    put("ssm_g", columns(a["ssm_norm_g"]))
    put("ml_g", columns(a["ml_norm_g"]))
    put("q_g", columns(a["mla_q_norm_g"]))
    put("kv_g", columns(a["mla_kv_norm_g"]))
    rb = np.concatenate([a["moe_b_group"], a["moe_b_router"]], -1)
    put("router_b", np.broadcast_to(rb[:, None, :], (L, P, NG + NE)))
    router = np.concatenate([a["moe_w_group"], a["moe_w_router"]], -1)
    gu = np.concatenate([a["moe_w_gate"], a["moe_w_up"]], -1).reshape(L * NE, 2, 4, P, 2 * DE).transpose(0, 1, 3, 2, 4).reshape(L * NE, 2, P, 2048)
    dn = a["moe_w_down"].reshape(L * NE, 1, 2, P, D).transpose(0, 1, 3, 2, 4).reshape(L * NE, 1, P, 2048)
    const, ccols = constants()
    arrays = {"x": a["x"].reshape(T, D), "positions": a["positions"], "const": const, "ccols": ccols, "params": par,
              "w_router": tiles(router), "w_moe": np.concatenate([gu, dn], 1), "final_norm_g": a["final_norm_g"],
              "w_in": slots, "w_small": tiles(small), "w_uq": tiles(uq), "w_ukv": ukv, "w_out": w_out}
    return {n: np.ascontiguousarray(v) for n, v in arrays.items()}


def program(nc, arrays, known):
    A = {n: nc.dram_tensor(f"in_{n}", v.shape, mybir.dt.from_np(v.dtype), kind="ExternalInput").ap() for n, v in arrays.items()}
    for name, rows in (("residual", T), ("h2", T), ("y", (NE + SPARE) * CAP)):
        A[name] = nc.dram_tensor(name, (rows, D), F32, kind="Internal").ap()
    A["out"] = nc.dram_tensor("out_0_dram", (T, D), F32, kind="ExternalOutput").ap()
    return build(nc, A, known)


def kernel(**inputs):
    import concourse.bacc as bacc
    from concourse.bass_utils import run_bass_kernel_spmd

    arrays = layout(inputs)
    known = program(bacc.Bacc("TRN2", target_bir_lowering=False, num_devices=1), arrays, None)
    nc = bacc.Bacc("TRN2", target_bir_lowering=False, num_devices=1)
    program(nc, arrays, known)
    r = run_bass_kernel_spmd(nc, [{f"in_{n}": v for n, v in arrays.items()}], core_ids=[0])
    return r.results[0]["out_0_dram"].reshape(1, T, D)
```

```python
from contextlib import ExitStack

import concourse.bass as bass
import numpy as np
from concourse import mybir

F32 = mybir.dt.float32
F32R = mybir.dt.float32r
BF16 = mybir.dt.bfloat16
I32 = mybir.dt.int32
U32 = mybir.dt.uint32
ALU = mybir.AluOpType
ACT = mybir.ActivationFunctionType
AX = mybir.AxisListType

P = 128
D = 1024
KD = D // P
T = 512
NT = T // P
L = 2
H = 4
HD = 64
GW = H * HD
NE = 16
NG = 4
EG = NE // NG
DE = 256
EPS = 1e-6
NEG = -1e30
MLA_SCALE = float(96) ** -0.5
HEAD_SCALE = float(HD) ** -0.5

SLOTS = ["small", "x", "B", "C", "mq", "mk", "mv", "aq", "ak", "av", "cq", "ckv", "z", "mo"]
W_IN_AT = {"aq": 0, "ak": 256, "av": 512, "z": 768, "x": 1024, "B": 1280, "C": 1536,
           "mq": 1796, "mk": 2052, "mv": 2308, "mo": 2572, "cq": 2828, "ckv": 3084}
UNITS = [u for n in SLOTS for u in ([n] if n in ("small", "ckv") else [n + "0", n + "1"])]
W_DT, W_IG, W_FG, W_KR = 1792, 2564, 2568, 3212

PARAMS = {}


def _param(name, n):
    PARAMS[name] = sum(w for _, w in PARAMS.values()), n


for _name, _n in (("g_mix", KD), ("g_ffn", KD), ("conv_w", 40), ("conv_b", 10), ("gate_b", 1), ("a_log", 1),
                  ("d_skip", 2), ("ssm_g", 2), ("ml_g", 2), ("q_g", 2), ("kv_g", 1), ("router_b", NG + NE)):
    _param(_name, _n)
NPAR = sum(w for _, w in PARAMS.values())
CONV_TILES = ["x0", "x1", "B0", "B1", "C0", "C1", "mq0", "mq1", "mk0", "mk1"]

CONSTS = ["ident", "neg_row", "neg_col", "avg128", "avg256", "avg64", "swap", "before", "ones", "iota"]
COLS = {"freq": (0, 1), "sign": (1, 1), "token": (2, 2 * NT), "rank": (2 + 2 * NT, EG), "first_row": (2 + 2 * NT + EG, NE)}
NCOLS = 2 + 2 * NT + EG + NE
NR = NG + NE
CAP = P
SPARE = 2 * T // (CAP + 1) + T // CAP - 1
Q_DT, Q_IG, Q_FG, Q_KR = 0, 32, 64, 96

BANK_OF = {0: (0, 0), 1: (1, 0), 3: (1, 384), 2: (2, 0)}
PACK = {i: 512 * b + at for i, (b, at) in BANK_OF.items()}
PACKED = 1280


class Steps:

    def __init__(self, nc, ctx, known, block, engine):
        self.done = ctx.enter_context(nc.semaphore(f"{block}_{engine}_done"))
        self.known, self.prefix, self.n, self.seen = known, f"{block}/{engine}:", 0, {}

    def step(self, name=None):
        self.n += 1
        if name is not None:
            assert self.prefix + name not in self.seen, name
            self.seen[self.prefix + name] = self.n
        return 1

    def at(self, name):
        return 1 if self.known is None else self.known[self.prefix + name]


def engine_steps(nc, ctx, known, block):
    return [Steps(nc, ctx, known, block, e) for e in ("tensor", "scalar", "vector", "gpsimd")]


def schedule():
    s = [("norm", None)]
    s += [("proj", "small"), ("gates_a", None), ("proj", "x0"), ("gates_b", None), ("proj", "x1"), ("gates_c", None)]
    s += [("silu", "x0"), ("proj", "B0"), ("silu", "x1"), ("gate_cols", None),
          ("proj", "B1"), ("silu", "B0"), ("proj", "C0"), ("silu", "B1"), ("xdt", None), ("proj", "C1"),
          ("silu", "C0"), ("proj", "mq0"), ("silu", "C1"), ("proj", "mq1"), ("silu", "mq0"), ("proj", "mk0"),
          ("silu", "mq1"), ("proj", "mk1"), ("silu", "mk0"), ("projT", "mv0"), ("silu", "mk1"), ("projT", "mv1")]
    fill = [("proj", "aq0"), ("proj", "aq1"), ("proj", "ak0"), ("proj", "ak1"), ("projT", "av0"), ("projT", "av1"),
            ("proj", "cq0"), ("proj", "cq1"), ("proj", "ckv"), ("proj", "z0"), ("proj", "z1"),
            ("proj", "mo0"), ("proj", "mo1")]
    for h in range(H):
        s += [("ssd_a", h), fill.pop(0)]
        s += [("ssd_b", h)]
    for h in range(H):
        s += [("ml_a", h), fill.pop(0)]
        s += [("ml_b", h)]
    heads = [(kind, h) for kind in ("moba", "mla") for h in range(H)]
    s += [("att_a", heads[0]), fill.pop(0), ("att_e", heads[0]), fill.pop(0)]
    between = {0: [fill.pop(0), ("mla_norm", None)], 1: [("mla_up", None)], 2: [fill.pop(0)], 3: [fill.pop(0), ("fin_a", None)],
               4: [("out_high", 0)], 5: [("fin_b", None), ("out_high", 1)], 6: [("fin_c", None), ("out_split", 0)], 7: [("out_split", 1)]}
    for n, head in enumerate(heads):
        following = heads[n + 1:n + 2]
        s += [("att_a", a) for a in following] + [("att_b", head)] + [("att_e", a) for a in following]
        s += between.get(n, []) + [("att_c", head)]
        if ("fin_b", None) in between.get(n, []):
            s += [("fin_ms", None)]
    s += [("out", None)]
    assert not fill
    return s


def build(nc, A, known):
    seen = {}
    top = ExitStack()
    with top:
        def sb(ctx, name, shape, dt=F32):
            return ctx.enter_context(nc.sbuf_tensor(name, shape, dt))

        bank = [top.enter_context(nc.psum_tensor(f"bank{i}", [P, 512], F32)) for i in range(8)]
        const = sb(top, "const", [P, len(CONSTS), P])
        C = {n: const[:, i, :] for i, n in enumerate(CONSTS)}
        ident_bf = sb(top, "ident_bf", [P, P], BF16)
        neg_bf = sb(top, "neg_bf", [P, P], BF16)
        ccols = sb(top, "ccols", [P, NCOLS])
        token_bf = sb(top, "token_bf", [P, NT, 2], BF16)
        cos_t = sb(top, "cos_t", [P, T])
        sin_t = sb(top, "sin_t", [P, T])
        rows1 = sb(top, "rows1", [P, T])
        rows2 = sb(top, "rows2", [P, T])
        par = sb(top, "par", [P, NPAR])
        arena = sb(top, "arena", [P, 8192])
        x_tm = arena[:, 0:4096].rearrange("p (i d) -> p i d", i=NT)
        h_tm = arena[:, 4096:8192].rearrange("p (i d) -> p i d", i=NT)
        ms = sb(top, "ms", [P, 3 * NT])
        eps = sb(top, "eps", [P, 1])

        def pcol(name, i=0):
            return par[:, PARAMS[name][0] + i:PARAMS[name][0] + i + 1]

        setup(nc, A, known, seen, C, const, ident_bf, neg_bf, ccols, token_bf, cos_t, sin_t, rows1, rows2, x_tm, h_tm, ms, eps)
        with nc.Fori(0, L) as layer:
            mixers(nc, A, known, seen, layer, bank, C, ident_bf, neg_bf, cos_t, sin_t, rows1, rows2, par, pcol,
                   arena, x_tm, h_tm, ms, eps)
            moe(nc, A, known, seen, layer, bank, C, ccols, token_bf, par, pcol, x_tm, h_tm, ms, eps)
        final_norm(nc, A, known, seen, h_tm)
    return seen


def clear(nc, steps, sems):
    nums = [s.num for s in [e.done for e in steps] + list(sems)]
    assert max(nums) - min(nums) == len(nums) - 1
    nc.all_engine_barrier(sems_to_clear=range(min(nums), max(nums) + 1))


def record(seen, steps):
    for e in steps:
        seen.update(e.seen)


def forget(pool, *sems):
    pool.dma_reset(range(min(s.num for s in sems), max(s.num for s in sems) + 1))


def root_mean_square(act, scalar, x, scratch, ms, eps, i):
    act.activation(scratch, x, ACT.Square, accum_out=ms[:, i:i + 1]).then_inc(scalar.done, scalar.step())
    act.wait_ge(scalar.done, scalar.n)
    act.activation(ms[:, NT + i:NT + i + 1], ms[:, i:i + 1], ACT.Sqrt, scale=1.0 / D, bias=eps[:, :]).then_inc(scalar.done, scalar.step(f"rms{i}"))


def normalise(dve, scalar, vector, x, out, ms, i):
    dve.wait_ge(scalar.done, scalar.at(f"rms{i}"))
    dve.reciprocal(ms[:, 2 * NT + i:2 * NT + i + 1], ms[:, NT + i:NT + i + 1]).then_inc(vector.done, vector.step())
    dve.wait_ge(vector.done, vector.n)
    dve.tensor_scalar(out, x, ms[:, 2 * NT + i:2 * NT + i + 1], None, ALU.mult).then_inc(vector.done, vector.step(f"h{i}"))


def setup(nc, A, known, seen, C, const, ident_bf, neg_bf, ccols, token_bf, cos_t, sin_t, rows1, rows2, x_tm, h_tm, ms, eps):
    with ExitStack() as ctx:
        tensor, scalar, vector, gpsimd = steps = engine_steps(nc, ctx, known, "setup")
        loaded = ctx.enter_context(nc.semaphore("setup_loaded"))
        constants_in = ctx.enter_context(nc.semaphore("constants_in"))
        x_in = [ctx.enter_context(nc.semaphore(f"x_in{i}")) for i in range(NT)]
        pos = ctx.enter_context(nc.sbuf_tensor("pos", [P, T], I32))
        ang = ctx.enter_context(nc.sbuf_tensor("ang", [P, T], F32))
        turn = ctx.enter_context(nc.sbuf_tensor("turn", [P, T], F32))
        with nc.Block() as block:
            @block.sync
            def _(sp):
                sp.dma_start(ccols[:, :], A["ccols"]).then_inc(loaded, 16)
                sp.dma_start(pos[:, :], A["positions"].partition_broadcast(P).rearrange("p o t -> p (o t)")
                             if len(A["positions"].shape) == 2 else A["positions"]).then_inc(loaded, 16)
                for i in range(NT):
                    sp.dma_start(x_tm[:, i, :], A["x"][i * P:(i + 1) * P, :]).then_inc(x_in[i], 16)
                sp.dma_start(const[:, :, :], A["const"]).then_inc(constants_in, 16)

            @block.gpsimd
            def _(pool):
                pool.memset(eps[:, :], EPS).then_inc(gpsimd.done, gpsimd.step("eps"))
                pool.memset(rows1[:, :], 0.0).then_inc(gpsimd.done, gpsimd.step())
                pool.memset(rows2[:, :], 0.0).then_inc(gpsimd.done, gpsimd.step())

            @block.vector
            def _(dve):
                dve.wait_ge(loaded, 32)
                def then(ins, name=None):
                    ins.then_inc(vector.done, vector.step(name))
                    dve.wait_ge(vector.done, vector.n)
                then(dve.tensor_copy(ang[:, :], pos[:, :]))
                then(dve.tensor_scalar(ang[:, :], ang[:, :], ccols[:, 0:1], None, ALU.mult))
                then(dve.tensor_scalar(turn[:, :], ang[:, :], float(1 / (2 * np.pi)), 12582912.0, ALU.mult, ALU.add))
                then(dve.tensor_scalar(turn[:, :], turn[:, :], -12582912.0, None, ALU.add))
                for part in (6.28125, 0.0019350051879882812, float(2 * np.pi - 6.28125 - 0.0019350051879882812)):
                    then(dve.scalar_tensor_tensor(ang[:, :], turn[:, :], -part, ang[:, :], ALU.mult, ALU.add))
                then(dve.tensor_scalar(ang[:, :], ang[:, :], 3.1415925, -3.1415925, ALU.min, ALU.max))
                then(dve.scalar_tensor_tensor(turn[:, :], ang[:, :], -1.0, ang[:, :], ALU.mult, ALU.max))
                then(dve.tensor_scalar(turn[:, :], turn[:, :], -1.0, float(np.pi / 2), ALU.mult, ALU.add), "angles")
                for i in range(NT):
                    normalise(dve, scalar, vector, x_tm[:, i, :], h_tm[:, i, :], ms, i)
                dve.wait_ge(constants_in, 16)
                dve.tensor_copy(ident_bf[:, :], C["ident"]).then_inc(vector.done, vector.step())
                dve.tensor_copy(neg_bf[:, :], C["neg_row"]).then_inc(vector.done, vector.step())
                dve.tensor_copy(token_bf[:, :, :], ccols[:, 2:2 + 2 * NT].rearrange("p (i c) -> p i c", i=NT)).then_inc(vector.done, vector.step())
                dve.wait_ge(scalar.done, scalar.at("sines"))
                dve.tensor_scalar(sin_t[:, :], sin_t[:, :], ccols[:, 1:2], None, ALU.mult).then_inc(vector.done, vector.step())

            @block.scalar
            def _(act):
                act.wait_ge(gpsimd.done, gpsimd.at("eps"))
                for i in range(NT):
                    act.wait_ge(x_in[i], 16)
                    root_mean_square(act, scalar, x_tm[:, i, :], h_tm[:, i, :], ms, eps, i)
                act.wait_ge(vector.done, vector.at("angles"))
                act.activation(cos_t[:, :], turn[:, :], ACT.Sin).then_inc(scalar.done, scalar.step())
                act.activation(sin_t[:, :], ang[:, :], ACT.Sin).then_inc(scalar.done, scalar.step("sines"))
        clear(nc, steps, [loaded, constants_in, *x_in])
        record(seen, steps)


def mixers(nc, A, known, seen, layer, bank, C, ident_bf, neg_bf, cos_t, sin_t, rows1, rows2, par, pcol,
           arena, x_tm, h_tm, ms, eps):
    plan = schedule()
    with ExitStack() as ctx:
        def sb(name, shape, dt=F32):
            return ctx.enter_context(nc.sbuf_tensor(name, shape, dt))

        tensor, scalar, vector, gpsimd = steps = engine_steps(nc, ctx, known, "mix")
        sem = lambda n: ctx.enter_context(nc.semaphore(n))
        par_in, up_in, x_kept, x_again, spare_zeroed = (sem(n) for n in ("par_in", "up_in", "x_kept", "x_again", "spare_zeroed"))
        slot_in = [sem(f"slot_in{i}") for i in range(4)]
        sems = [par_in, up_in, x_kept, x_again, spare_zeroed, *slot_in]

        ring = sb("ring", [P, 2, KD, 256])
        w_hi = sb("w_hi", [P, 2, KD, P], F32R)
        w_lo = sb("w_lo", [P, 2, KD, P], F32R)
        hT_hi = sb("hT_hi", [P, KD, T], F32R)
        hT_lo = sb("hT_lo", [P, KD, T], F32R)
        mixed = sb("mixed", [P, KD, T])
        w_uq = sb("w_uq", [P, 2, 384])
        w_ukv = sb("w_ukv", [P, 512])
        q_mla = arena[:, 0:2048].rearrange("p (h t) -> p h t", h=H)
        k_mla = arena[:, 2048:4096].rearrange("p (h t) -> p h t", h=H)
        v_moba = arena[:, 4096:5120].rearrange("p (i d) -> p i d", i=NT)
        v_mla = arena[:, 5120:6144].rearrange("p (i d) -> p i d", i=NT)
        probT = arena[:, 6144:8192].rearrange("p (j t) -> p j t", j=NT)
        raw = sb("raw", [P, 2, 3 + T])
        conv = sb("conv", [P, 10, T])
        cv = {n: conv[:, i, :] for i, n in enumerate(CONV_TILES)}
        u = sb("u", [P, T])
        rs = sb("rs", [P, 4, T])
        rstd, absden, tmp, au = (rs[:, i, :] for i in range(4))
        cols = sb("cols", [P, NT, P])
        neg_a = sb("neg_a", [P, NT, H])
        a_col = sb("a_col", [P, 1])
        xdt = sb("xdt", [P, NT, GW])
        v_aug = sb("v_aug", [P, NT, H, P])
        qT = sb("qT", [P, 2, T])
        kT = sb("kT", [P, 2, T])
        tri = sb("tri", [P, 2, PACKED])
        diag = sb("diag", [P, NT, P])
        ckv = sb("ckv", [P, T])
        mx = sb("mx", [P, 2, 4 * NT])
        zero = sb("zero", [P, 1])
        zeros = sb("zeros", [P, 512])
        cq = mixed[:, 6:8, :]
        zs = mixed[:, 2:4, :]
        os_ = mixed[:, 4:6, :]
        sig_z = conv[:, 4:6, :]

        NSL = len(SLOTS)
        w_out_at = [ring[:, (NSL + j) % 2, :, :].rearrange("p k n -> p (k n)") for j in range(2)]
        w_out_at += [v_aug[:, :, :, :].rearrange("p i h d -> p (i h d)"), conv[:, 2:6, :].rearrange("p n t -> p (n t)")]
        w_out_in = [(slot_in[(NSL + j) % 2], 16 * ((NSL + j) // 2 + 1)) for j in range(2)] + [(slot_in[2], 16), (slot_in[3], 16)]

        out_hi, out_lo = (t[:, :, :].rearrange("p k t -> p (k t)").rearrange("p (k d) -> p k d", d=D) for t in (hT_hi, hT_lo))
        mixed_hi, mixed_lo = (t[:, :, :, :].rearrange("p a k n -> p (a k n)").rearrange("p (k t) -> p k t", t=T) for t in (w_hi, w_lo))

        def last_unit(slot):
            return UNITS.index(SLOTS[slot] if SLOTS[slot] in UNITS else SLOTS[slot] + "1")

        ssd_y, ml_h = conv[:, 0:2, :], conv[:, 6:8, :]
        cq_sq = ssd_sq = conv[:, 2:4, :]
        ckv_sq, ml_sq = cv["C0"], conv[:, 4:6, :]
        q_pe, q_cos = cv["mk0"], cv["mk1"]
        units = ([f"ssd_y{h}" for h in range(H)] + [f"ml_y{h}" for h in range(H)]
                 + [f"att_t2{(k, h)}" for k in ("moba", "mla") for h in range(H)])
        unit_at = {"ssd": 0, "ml": H, "moba": 2 * H, "mla": 3 * H}

        with nc.Block() as block:
            @block.sync
            def _(sp):
                sp.dma_start(par[:, :], A["params"][bass.ds(layer, 1), :, :].rearrange("o p n -> (o p) n")).then_inc(par_in, 16)
                for n in range(NSL + 2):
                    if n == 2:
                        sp.dma_start(A["residual"].rearrange("(i p) d -> p i d", p=P), x_tm).then_inc(x_kept, 16)
                    if n == 4:
                        sp.dma_start(w_uq[:, :, :], A["w_uq"][bass.ds(layer, 1), :, :, :].rearrange("o p k n -> (o p) k n")).then_inc(up_in, 16)
                        sp.dma_start(w_ukv[:, :], A["w_ukv"][bass.ds(layer, 1), :, :].rearrange("o p n -> (o p) n")).then_inc(up_in, 16)
                    if n == 8:
                        spare = A["y"][NE * CAP:(NE + SPARE) * CAP, :].rearrange("(p n) d -> p (n d)", p=P).rearrange("p (m d) -> p m d", d=512)
                        sp.wait_ge(gpsimd.done, gpsimd.at("zeros"))
                        sp.dma_start(spare, zeros[:, :].rearrange("p (o d) -> p o d", o=1).to_broadcast([P, 2 * SPARE, 512])).then_inc(spare_zeroed, 16)
                    if n >= 2:
                        sp.wait_ge(gpsimd.done, gpsimd.at(f"lo{last_unit(n - 2)}"))
                    if n < NSL:
                        width = P if SLOTS[n] in UNITS else 2 * P
                        sp.dma_start(ring[:, n % 2, :, 0:width], A["w_in"][bass.ds(layer, 1), n, :, :, 0:width].rearrange("o p k n -> (o p) k n")).then_inc(slot_in[n % 2], 16)
                    else:
                        sp.dma_start(w_out_at[n - NSL], A["w_out"][bass.ds(layer, 1), n - NSL, :, :].rearrange("o p n -> (o p) n")).then_inc(slot_in[n % 2], 16)
                for j, name in ((2, "ml_y3"), (3, "ms3")):
                    sp.wait_ge(tensor.done, tensor.at(name))
                    sp.dma_start(w_out_at[j], A["w_out"][bass.ds(layer, 1), j, :, :].rearrange("o p n -> (o p) n")).then_inc(slot_in[j], 16)
                sp.wait_ge(spare_zeroed, 16)
                sp.wait_ge(x_kept, 16)
                sp.wait_ge(tensor.done, tensor.at("att_s('mla', 3)"))
                sp.dma_start(x_tm, A["residual"].rearrange("(i p) d -> p i d", p=P)).then_inc(x_again, 16)

            @block.tensor
            def _(pe):
                free = {}

                def claim(b, engine, reader):
                    if b in free:
                        last_engine, last_reader = free[b]
                        pe.wait_ge(last_engine.done, last_engine.at(last_reader))
                    free[b] = engine, reader

                def mm(out, lhsT, rhs, start, stop):
                    return pe.matmul(out, lhsT, rhs, start=start, stop=stop, skip_group_check=True)

                turn = [0]

                def pj():
                    turn[0] += 1
                    return turn[0] % 2

                def norm(_):
                    for k in range(KD):
                        for i in range(NT):
                            m = pe.transpose(bank[k][:, i * P:(i + 1) * P], h_tm[:, i, k * P:(k + 1) * P], C["ident"])
                        m.then_inc(tensor.done, tensor.step(f"hT{k}"))
                        free[k] = vector, f"hT{k}"

                def proj(name):
                    b, n = pj(), UNITS.index(name)
                    claim(b, scalar, name)
                    pe.wait_ge(gpsimd.done, gpsimd.at(f"lo{n}"))
                    for k in range(KD):
                        if n == 0:
                            pe.wait_ge(vector.done, vector.at(f"hT{k}"))
                        mm(bank[b][:, :], w_hi[:, n % 2, k, :], hT_hi[:, k, :], k == 0, False)
                        mm(bank[b][:, :], w_hi[:, n % 2, k, :], hT_lo[:, k, :], False, False)
                        m = mm(bank[b][:, :], w_lo[:, n % 2, k, :], hT_hi[:, k, :], False, k == KD - 1)
                    m.then_inc(tensor.done, tensor.step(name))

                def projT(name):
                    b, n = pj(), UNITS.index(name)
                    claim(b, scalar, name)
                    pe.wait_ge(gpsimd.done, gpsimd.at(f"lo{n}"))
                    for i in range(NT):
                        out, tokens = bank[b][:, i * P:(i + 1) * P], slice(i * P, (i + 1) * P)
                        for k in range(KD):
                            mm(out, hT_hi[:, k, tokens], w_hi[:, n % 2, k, :], k == 0, False)
                            mm(out, hT_hi[:, k, tokens], w_lo[:, n % 2, k, :], False, False)
                            m = mm(out, hT_lo[:, k, tokens], w_hi[:, n % 2, k, :], False, k == KD - 1)
                    m.then_inc(tensor.done, tensor.step(name))

                def gate_cols(_):
                    claim(7, scalar, "cols")
                    pe.wait_ge(vector.done, vector.at("rows1"))
                    for i in range(NT):
                        m = pe.transpose(bank[7][:, i * P:(i + 1) * P], rows1[:, i * P:(i + 1) * P], C["ident"])
                    m.then_inc(tensor.done, tensor.step("cols"))

                def xdt_(_):
                    for half in range(2):
                        claim(2 + half, vector, f"xdt{half}")
                        for i in range(2):
                            for j in range(2):
                                pe.wait_ge(scalar.done, scalar.at(f"silu_x{j}"))
                                tile = 2 * half + i
                                m = pe.transpose(bank[2 + half][:, i * GW + j * P:i * GW + (j + 1) * P],
                                                 cv[f"x{j}"][:, tile * P:(tile + 1) * P], C["ident"])
                        m.then_inc(tensor.done, tensor.step(f"xdt{half}"))

                def pair_scores(keys, queries, at, n, reader):
                    for b in range(3):
                        claim(2 + b, vector, reader)
                    for i in (0, 1, 3, 2):
                        b, off = BANK_OF[i]
                        m = mm(bank[2 + b][:, off:off + T - i * P], keys[at:at + n, i * P:(i + 1) * P],
                               queries[at:at + n, i * P:T], True, True)
                    return m

                def spread(b, row, rows, engine, reader):
                    claim(b, engine, reader)
                    return mm(bank[b][:, :], C["ident"][:, row:row + 1].to_broadcast([P, P]), rows[:, :], True, True)

                def ssd_a(h):
                    if h % 2 == 0:
                        pe.wait_ge(scalar.done, scalar.at(f"silu_B{h // 2}"))
                        pe.wait_ge(scalar.done, scalar.at(f"silu_C{h // 2}"))
                        pair_scores(cv[f"B{h // 2}"], cv[f"C{h // 2}"], 0, P, f"ssd_w{h + 1}").then_inc(tensor.done, tensor.step(f"ssd_s{h}"))
                    pe.wait_ge(vector.done, vector.at("rows1"))
                    spread(5, Q_DT + h, rows1, scalar, f"ssd_e{h}").then_inc(tensor.done, tensor.step(f"ssd_r{h}"))

                def triangle(out, weight, h):
                    for i in range(NT):
                        m = mm(out[:, i * P:T], weight(i), tri[:, h % 2, PACK[i]:PACK[i] + T - i * P], i == 0, i == NT - 1)
                    return m

                def ssd_b(h):
                    if h % 2 == 0:
                        claim(6, vector, f"ssd_y{h // 2}")
                    pe.wait_ge(vector.done, vector.at(f"ssd_w{h}"))
                    pe.wait_ge(vector.done, vector.at("xdt1"))
                    lo = HD * (h % 2)
                    triangle(bank[6][lo:lo + HD, :], lambda i: xdt[:, i, HD * h:HD * (h + 1)], h).then_inc(tensor.done, tensor.step(f"ssd_y{h}"))

                def ml_a(h):
                    pe.wait_ge(scalar.done, scalar.at(f"silu_mq{h // 2}"))
                    pe.wait_ge(scalar.done, scalar.at(f"silu_mk{h // 2}"))
                    lo = HD * (h % 2)
                    pair_scores(cv[f"mk{h // 2}"], cv[f"mq{h // 2}"], lo, HD, f"ml_w{h}").then_inc(tensor.done, tensor.step(f"ml_s{h}"))
                    spread(5, Q_KR + h, rows1, scalar, f"ml_e{h}").then_inc(tensor.done, tensor.step(f"ml_r{h}"))
                    pe.wait_ge(scalar.done, scalar.at("rows2"))
                    spread(7, Q_FG + h, rows2, vector, f"ml_d{h}").then_inc(tensor.done, tensor.step(f"ml_f{h}"))

                def ml_b(h):
                    claim(6, vector, f"ml_y{h}")
                    pe.wait_ge(vector.done, vector.at(f"ml_w{h}"))
                    pe.wait_ge(scalar.done, scalar.at("mv1"))
                    pe.wait_ge(gpsimd.done, gpsimd.at("ones"))
                    triangle(bank[6][:, :], lambda i: v_aug[:, i, h, :], h).then_inc(tensor.done, tensor.step(f"ml_y{h}"))

                def att_a(a):
                    kind, h = a
                    if kind == "moba":
                        pe.wait_ge(scalar.done, scalar.at(f"aq{h // 2}"))
                        pe.wait_ge(scalar.done, scalar.at(f"ak{h // 2}"))
                        lo, n, q, k = HD * (h % 2), HD, qT[:, h // 2, :], kT[:, h // 2, :]
                    else:
                        pe.wait_ge(vector.done, vector.at(f"mla_q{h}"))
                        pe.wait_ge(vector.done, vector.at(f"mla_k{h}"))
                        pe.wait_ge(scalar.done, scalar.at("k_up1"))
                        lo, n, q, k = 0, 96, q_mla[:, h, :], k_mla[:, h, :]
                    for b in range(3):
                        claim(2 + b, scalar, f"att_e{a}")
                    for r in (0, 1, 3, 2):
                        i = NT - 1 - r
                        b, off = BANK_OF[r]
                        mm(bank[2 + b][:, off:off + (i + 1) * P], q[lo:lo + n, i * P:(i + 1) * P], k[lo:lo + n, 0:(i + 1) * P], True, False)
                        m = mm(bank[2 + b][:, off + i * P:off + (i + 1) * P], ident_bf[:, :], neg_bf[:, :], False, True)
                    m.then_inc(tensor.done, tensor.step(f"att_s{a}"))

                def att_b(a):
                    for n, (b, tiles) in enumerate(((5, [3]), (7, [2, 0]), (5, [1]))):
                        claim(b, (scalar, vector, scalar)[n], f"att_t{n}{a}")
                        for i in tiles:
                            off = 384 if i == 0 else 0
                            pe.wait_ge(vector.done, vector.at(f"att_p{i}{a}"))
                            for j in range(i + 1):
                                m = pe.transpose(bank[b][:, off + j * P:off + (j + 1) * P],
                                                 tri[:, a[1] % 2, PACK[NT - 1 - i] + j * P:PACK[NT - 1 - i] + (j + 1) * P], C["ident"])
                        m.then_inc(tensor.done, tensor.step(f"att_t{n}{a}"))

                def att_c(a):
                    kind, h = a
                    v = v_moba if kind == "moba" else v_mla
                    pe.wait_ge(scalar.done, scalar.at("av1" if kind == "moba" else "mla_v1"))
                    pe.wait_ge(vector.done, vector.at(f"att_t1{a}"))
                    pe.wait_ge(scalar.done, scalar.at(f"att_t0{a}"))
                    pe.wait_ge(scalar.done, scalar.at(f"att_t2{a}"))
                    if h % 2 == 0:
                        claim(6, scalar, f"att_y{(kind, h // 2)}")
                    lo = HD * (h % 2)
                    for j in range(NT):
                        m = mm(bank[6][lo:lo + HD, j * P:T], v[:, j, HD * h:HD * (h + 1)], probT[:, j, j * P:T], j == 0, j == NT - 1)
                    m.then_inc(tensor.done, tensor.step(f"att_y{a}"))

                def mla_norm(_):
                    claim(7, scalar, "cq_ln")
                    pe.wait_ge(gpsimd.done, gpsimd.at("cq_sq"))
                    mm(bank[7][:, :], C["avg256"], cq_sq[:, 0, :], True, False)
                    mm(bank[7][:, :], C["avg256"], cq_sq[:, 1, :], False, True).then_inc(tensor.done, tensor.step("cq_ms"))
                    b = pj()
                    claim(b, scalar, "ckv_ln")
                    pe.wait_ge(gpsimd.done, gpsimd.at("ckv_sq"))
                    mm(bank[b][:, :], C["avg128"], ckv_sq, True, True).then_inc(tensor.done, tensor.step("ckv_ms"))

                def mla_up(_):
                    pe.wait_ge(up_in, 32)
                    pe.wait_ge(vector.done, vector.at("cq_n1"))
                    for n in range(3):
                        b = pj()
                        claim(b, scalar, f"q_up{n}")
                        for k in range(2):
                            m = mm(bank[b][:, :], w_uq[:, k, n * P:(n + 1) * P], cq[:, k, :], k == 0, k == 1)
                        m.then_inc(tensor.done, tensor.step(f"q_up{n}"))
                    claim(7, vector, "k_rot")
                    mm(bank[7][:, :], C["swap"], u[:, :], True, True).then_inc(tensor.done, tensor.step("k_swap"))
                    pe.wait_ge(vector.done, vector.at("ckv_n"))
                    for n in range(2):
                        b = pj()
                        claim(b, scalar, f"k_up{n}")
                        mm(bank[b][:, :], w_ukv[:, n * P:(n + 1) * P], ckv[:, :], True, True).then_inc(tensor.done, tensor.step(f"k_up{n}"))
                    for half in range(2):
                        b = pj()
                        claim(b, scalar, f"mla_v{half}")
                        for i in range(2):
                            tile = 2 * half + i
                            m = mm(bank[b][:, i * GW:(i + 1) * GW], ckv[:, tile * P:(tile + 1) * P], w_ukv[:, GW:2 * GW], True, True)
                        m.then_inc(tensor.done, tensor.step(f"mla_v{half}"))
                    pe.wait_ge(scalar.done, scalar.at("q_up2"))
                    claim(7, vector, "q_rot")
                    mm(bank[7][:, :], C["swap"], q_pe, True, True).then_inc(tensor.done, tensor.step("q_swap"))

                def fin_b(_, tiles=(0, 1)):
                    for j in tiles:
                        b = pj()
                        claim(b, scalar, f"ln{j}")
                        pe.wait_ge(gpsimd.done, gpsimd.at("ssd_sq" if j < 2 else "ml_sq"))
                        average, squares = (C["avg128"], ssd_sq) if j < 2 else (C["avg64"], ml_sq)
                        mm(bank[b][:, :], average, squares[:, j % 2, :], True, True).then_inc(tensor.done, tensor.step(f"ms{j}"))

                def fin_ms(_):
                    fin_b(_, (2, 3))

                def out(_):
                    pe.wait_ge(vector.done, vector.at("n3"))
                    pe.wait_ge(vector.done, vector.at("mixed_lo1"))
                    pe.wait_ge(gpsimd.done, gpsimd.at("out_lo1"))
                    pe.wait_ge(scalar.done, scalar.at("att_y('moba', 1)"))
                    for arrived, count in w_out_in:
                        pe.wait_ge(arrived, count)
                    for i in range(NT):
                        claim(2 * i, vector, f"x{i}")
                        claim(2 * i + 1, vector, f"x{i}")
                        for half in range(2):
                            for k in range(KD):
                                if i + half == 0 and k == 6:
                                    pe.wait_ge(scalar.done, scalar.at("att_y('mla', 1)"))
                                at = (k % 2) * D + half * 512
                                out, tokens, cols = bank[2 * i + half][:, :], slice(i * P, (i + 1) * P), slice(half * 512, half * 512 + 512)
                                if k < KD // 2:
                                    mm(out, mixed_hi[:, k, tokens], out_hi[:, k, cols], k == 0, False)
                                    mm(out, mixed_hi[:, k, tokens], out_lo[:, k, cols], False, False)
                                    m = mm(out, mixed_lo[:, k, tokens], out_hi[:, k, cols], False, False)
                                else:
                                    m = mm(out, mixed[:, k, tokens], w_out_at[k // 2][:, at:at + 512], False, k == KD - 1)
                        m.then_inc(tensor.done, tensor.step(f"out{i}"))

                do = dict(norm=norm, proj=proj, projT=projT, gate_cols=gate_cols, xdt=xdt_, ssd_a=ssd_a, ssd_b=ssd_b,
                          ml_a=ml_a, ml_b=ml_b, att_a=att_a, att_b=att_b, att_c=att_c, mla_norm=mla_norm, mla_up=mla_up,
                          fin_b=fin_b, fin_ms=fin_ms, out=out)
                for op, arg in plan:
                    if op in do:
                        do[op](arg)

            @block.scalar
            def _(act):

                def act_to(out, src, func=ACT.Copy, name=None, **kw):
                    act.activation(out, src, func, **kw).then_inc(scalar.done, scalar.step(name))

                def norm(_):
                    act.wait_ge(par_in, 16)
                    for k in range(KD):
                        if k == KD // 2:
                            hi(0)
                        act.wait_ge(tensor.done, tensor.at(f"hT{k}"))
                        act_to(hT_hi[:, k, :], bank[k][:, :], ACT.Identity, f"hT{k}", scale=pcol("g_mix", k))
                    hi(1)

                def hi(n):
                    if n >= len(UNITS):
                        return
                    slot = SLOTS.index(UNITS[n].rstrip("01"))
                    act.wait_ge(slot_in[slot % 2], 16 * (slot // 2 + 1))
                    at = P if UNITS[n][-1] == "1" else 0
                    act_to(w_hi[:, n % 2, :, :], ring[:, slot % 2, :, at:at + P], name=f"hi{n}")

                turn = [0]

                def pj():
                    turn[0] += 1
                    return bank[turn[0] % 2]

                def proj(name):
                    b = pj()
                    act.wait_ge(tensor.done, tensor.at(name))
                    if name == "small":
                        act_to(u[:, :], b[:, :], ACT.Identity, name, bias=pcol("gate_b"))
                    elif name in CONV_TILES:
                        n = CONV_TILES.index(name)
                        if n >= 2:
                            act.wait_ge(vector.done, vector.at(f"conv_{CONV_TILES[n - 2]}"))
                        act_to(raw[:, n % 2, 3:3 + T], b[:, :], name=name)
                    else:
                        j = int(name[-1]) if name[-1] in "01" else 0
                        out = {"aq": qT, "ak": kT, "cq": cq, "z": zs, "mo": os_}.get(name.rstrip("01"))
                        act_to(ckv[:, :] if out is None else out[:, j, :], b[:, :], name=name)
                    hi(UNITS.index(name) + 2)

                def projT(name):
                    b, j = pj(), int(name[-1])
                    act.wait_ge(tensor.done, tensor.at(name))
                    if name[:2] == "av":
                        act_to(v_moba[:, :, j * P:(j + 1) * P], b[:, :].rearrange("p (i d) -> p i d", i=NT), name=name)
                    else:
                        for h in (2 * j, 2 * j + 1):
                            act_to(v_aug[:, :, h, 0:HD], b[:, :].rearrange("p (i d) -> p i d", i=NT)[:, :, (h % 2) * HD:(h % 2 + 1) * HD],
                                   name=name if h % 2 else None)
                    hi(UNITS.index(name) + 2)

                def gates_a(_):
                    act_to(a_col[0:H, :], pcol("a_log")[0:H, :], ACT.Exp, "a_col")

                def gates_b(_):
                    act.wait_ge(vector.done, vector.at("au"))
                    act.activation(au[0:68, :], au[0:68, :], ACT.Exp, scale=-1.0).then_inc(scalar.done, scalar.step())
                    act.wait_ge(scalar.done, scalar.n)
                    act_to(au[0:68, :], au[0:68, :], ACT.Ln, "softplus", bias=1.0)

                def gates_c(_):
                    act.wait_ge(vector.done, vector.at("rows2"))
                    act_to(rows2[Q_FG:Q_FG + H, :], rows2[Q_FG:Q_FG + H, :], ACT.Exp, "rows2", scale=-1.0)

                def silu(name):
                    act.wait_ge(vector.done, vector.at(f"conv_{name}"))
                    act_to(cv[name], cv[name], ACT.Silu, f"silu_{name}")

                def gate_cols(_):
                    act.wait_ge(tensor.done, tensor.at("cols"))
                    act_to(cols[:, :, :], bank[7][:, :].rearrange("p (i c) -> p i c", i=NT), name="cols")

                def decays(h, kind, col):
                    n = unit_at[kind] + h
                    if n >= 2:
                        act.wait_ge(tensor.done, tensor.at(units[n - 2]))
                    act.wait_ge(tensor.done, tensor.at(f"{kind}_r{h}"))
                    act.wait_ge(vector.done, vector.at(f"{kind}_x{h}"))
                    for i in range(NT):
                        at = PACK[i]
                        m = act.activation(tri[:, h % 2, at:at + P], diag[:, i, :], ACT.Exp, bias=col(i))
                        if i < NT - 1:
                            m = act.activation(tri[:, h % 2, at + P:at + T - i * P], bank[5][:, (i + 1) * P:T], ACT.Exp, bias=col(i))
                    m.then_inc(scalar.done, scalar.step(f"{kind}_e{h}"))

                def ssd_a(h):
                    act.wait_ge(vector.done, vector.at("neg_a"))
                    decays(h, "ssd", lambda i: neg_a[:, i, h:h + 1])

                def ml_a(h):
                    decays(h, "ml", lambda i: cols[:, i, Q_FG + h:Q_FG + h + 1])

                def ml_b(h):
                    act.wait_ge(tensor.done, tensor.at(f"ml_y{h}"))
                    if h:
                        act.wait_ge(vector.done, vector.at(f"ml_y{h - 1}"))
                    act_to(absden[HD:P, :], bank[6][HD:P, :], ACT.Abs, f"ml_abs{h}")

                def reciprocal_root(sources, out, names):
                    for j, (src, name) in enumerate(zip(sources, names)):
                        act.wait_ge(tensor.done, tensor.at(name))
                        act_to(out[:, j, :], src[:, :], ACT.Ln, name.replace("ms", "ln"), bias=eps[:, :])
                    act.wait_ge(scalar.done, scalar.n)
                    act.activation(out, out, ACT.Exp, scale=-0.5).then_inc(scalar.done, scalar.step("rstd_" + names[0]))

                def mla_norm(_):
                    act.wait_ge(vector.done, vector.at("ml_y3"))
                    reciprocal_root([bank[7], pj()], rs[:, 0:2, :], ["cq_ms", "ckv_ms"])

                def mla_up(_):
                    act.wait_ge(x_kept, 16)
                    for n in range(3):
                        b = pj()
                        act.wait_ge(tensor.done, tensor.at(f"q_up{n}"))
                        if n == 2:
                            act_to(q_pe, b[:, :], name="q_up2")
                        else:
                            act_to(q_mla[0:HD, 2 * n, :], b[0:HD, :])
                            act_to(q_mla[0:HD, 2 * n + 1, :], b[HD:P, :], name=f"q_up{n}")
                    for n in range(2):
                        b = pj()
                        act.wait_ge(tensor.done, tensor.at(f"k_up{n}"))
                        act_to(k_mla[0:HD, 2 * n, :], b[0:HD, :])
                        act_to(k_mla[0:HD, 2 * n + 1, :], b[HD:P, :], name=f"k_up{n}")
                    for half in range(2):
                        b = pj()
                        act.wait_ge(tensor.done, tensor.at(f"mla_v{half}"))
                        act_to(v_mla[:, 2 * half:2 * half + 2, :], b[:, :].rearrange("p (i d) -> p i d", i=2), name=f"mla_v{half}")

                def att_e(a):
                    kind, h = a
                    scale = HEAD_SCALE if kind == "moba" else MLA_SCALE
                    act.wait_ge(tensor.done, tensor.at(units[unit_at[kind] + h - 2]))
                    act.wait_ge(vector.done, vector.at(f"att_m{a}"))
                    for i in (3, 2, 1, 0):
                        b, off = BANK_OF[NT - 1 - i]
                        at, n = PACK[NT - 1 - i], (i + 1) * P
                        act.activation(tri[:, h % 2, at:at + n], bank[2 + b][:, off:off + n], ACT.Exp,
                                              bias=mx[:, h % 2, NT + i:NT + i + 1], scale=scale,
                                              accum_out=mx[:, h % 2, 2 * NT + i:2 * NT + i + 1]).then_inc(scalar.done, scalar.step(f"att_e{a}" if i == 0 else f"att_e{i}{a}"))

                def att_b(a):
                    n = unit_at[a[0]] + a[1] - 1 - 2 * H
                    if n >= 0:
                        act.wait_ge(tensor.done, tensor.at(f"att_y{(('moba', 'mla')[n // H], n % H)}"))
                    act.wait_ge(tensor.done, tensor.at(f"att_t0{a}"))
                    act_to(probT[:, :, 3 * P:T], bank[5][:, :].rearrange("p (j t) -> p j t", j=NT), name=f"att_t0{a}")
                    act.wait_ge(tensor.done, tensor.at(f"att_t2{a}"))
                    act_to(probT[:, 0:2, P:2 * P], bank[5][:, 0:2 * P].rearrange("p (j t) -> p j t", j=2), name=f"att_t2{a}")

                def att_c(a):
                    kind, h = a
                    if h % 2:
                        act.wait_ge(tensor.done, tensor.at(f"att_y{a}"))
                        act_to(mixed[:, (0 if kind == "moba" else 6) + h // 2, :], bank[6][:, :], name=f"att_y{(kind, h // 2)}")

                def fin_a(_):
                    act.wait_ge(scalar.done, scalar.n)
                    act_to(sig_z, zs, ACT.Sigmoid, "sig_z")
                    act_to(os_, os_, ACT.Sigmoid, "sig_o")

                def fin_b(_):
                    act.wait_ge(vector.done, vector.at("mla_q3"))
                    reciprocal_root([pj() for _ in range(4)], rs[:, :, :], [f"ms{j}" for j in range(4)])

                def out(_):
                    for i in range(NT):
                        act.wait_ge(vector.done, vector.at(f"x{i}"))
                        root_mean_square(act, scalar, x_tm[:, i, :], h_tm[:, i, :], ms, eps, i)

                do = dict(norm=norm, proj=proj, projT=projT, gates_a=gates_a, gates_b=gates_b, gates_c=gates_c, silu=silu, gate_cols=gate_cols, ssd_a=ssd_a,
                          ml_a=ml_a, ml_b=ml_b, att_e=att_e, att_b=att_b, att_c=att_c, mla_norm=mla_norm, mla_up=mla_up,
                          fin_a=fin_a, fin_b=fin_b, out=out)
                for op, arg in plan:
                    if op in do:
                        do[op](arg)

            @block.vector
            def _(dve):

                def norm(_):
                    dve.wait_ge(par_in, 16)
                    for k in range(KD):
                        dve.wait_ge(scalar.done, scalar.at(f"hT{k}"))
                        dve.scalar_tensor_tensor(hT_lo[:, k, :], bank[k][:, :], pcol("g_mix", k), hT_hi[:, k, :].bitcast(F32), ALU.mult, ALU.subtract)\
                            .then_inc(vector.done, vector.step(f"hT{k}"))

                def proj(name):
                    if name not in CONV_TILES:
                        return
                    n = CONV_TILES.index(name)
                    dve.wait_ge(gpsimd.done, gpsimd.at("pads"))
                    dve.wait_ge(scalar.done, scalar.at(name))
                    src = lambda j: raw[:, n % 2, j:j + T]
                    dve.tensor_scalar(cv[name], src(0), pcol("conv_w", 4 * n), pcol("conv_b", n), ALU.mult, ALU.add).then_inc(vector.done, vector.step())
                    dve.wait_ge(vector.done, vector.n)
                    for j in (1, 2, 3):
                        ins = dve.scalar_tensor_tensor(cv[name], src(j), pcol("conv_w", 4 * n + j), cv[name], ALU.mult, ALU.add)
                        ins.then_inc(vector.done, vector.step(f"conv_{name}" if j == 3 else None))
                        dve.wait_ge(vector.done, vector.n)

                dt, ig, fg = slice(Q_DT, Q_DT + H), slice(Q_IG, Q_IG + H), slice(Q_FG, Q_FG + H)

                def gates_a(_):
                    dve.wait_ge(scalar.done, scalar.at("small"))
                    dve.wait_ge(gpsimd.done, gpsimd.at("zero"))
                    dve.scalar_tensor_tensor(au[0:68, :], u[0:68, :], -1.0, u[0:68, :], ALU.mult, ALU.max).then_inc(vector.done, vector.step("au"))
                    dve.tensor_copy(tmp[fg, :], u[ig, :]).then_inc(vector.done, vector.step())

                def gates_b(_):
                    none = zero[:, :].to_broadcast([P, T])
                    dve.wait_ge(scalar.done, scalar.at("softplus"))
                    dve.wait_ge(scalar.done, scalar.at("a_col"))
                    dve.scalar_tensor_tensor(rows1[Q_IG:Q_IG + H, :], u[dt, :], 0.0, au[dt, :], ALU.max, ALU.add).then_inc(vector.done, vector.step())
                    dve.scalar_tensor_tensor(tmp[dt, :], u[dt, :], 0.0, au[dt, :], ALU.max, ALU.add).then_inc(vector.done, vector.step())
                    dve.wait_ge(vector.done, vector.n)
                    dve.tensor_scalar(tmp[dt, :], tmp[dt, :], a_col[0:H, :], -1.0, ALU.mult, ALU.mult).then_inc(vector.done, vector.step())
                    dve.wait_ge(vector.done, vector.n)
                    dve.tensor_tensor_scan(rows1[dt, :], tmp[dt, :], none[dt, :], 0.0, ALU.add, ALU.add).then_inc(vector.done, vector.step())
                    dve.scalar_tensor_tensor(au[fg, :], u[fg, :], 0.0, au[fg, :], ALU.min, ALU.subtract).then_inc(vector.done, vector.step())
                    dve.wait_ge(vector.done, vector.n)
                    dve.tensor_tensor_scan(rows2[fg, :], au[fg, :], none[fg, :], 0.0, ALU.add, ALU.add).then_inc(vector.done, vector.step())
                    dve.wait_ge(vector.done, vector.n)
                    dve.tensor_tensor(rows1[fg, :], tmp[fg, :], rows2[fg, :], ALU.subtract).then_inc(vector.done, vector.step())
                    dve.wait_ge(vector.done, vector.n)
                    dve.tensor_tensor_scan(tmp[fg, :], rows1[fg, :], rows1[fg, :], 0.0, ALU.max, ALU.max).then_inc(vector.done, vector.step())
                    dve.wait_ge(vector.done, vector.n)
                    dve.tensor_tensor(rows2[fg, :], rows2[fg, :], tmp[fg, :], ALU.add).then_inc(vector.done, vector.step("rows2"))
                    dve.tensor_scalar(rows1[Q_KR:Q_KR + H, :], tmp[fg, :], -1.0, None, ALU.mult).then_inc(vector.done, vector.step("rows1"))

                def gate_cols(_):
                    dve.wait_ge(scalar.done, scalar.at("cols"))
                    dve.tensor_scalar(neg_a[:, :, :], cols[:, :, Q_DT:Q_DT + H], -1.0, None, ALU.mult).then_inc(vector.done, vector.step("neg_a"))

                def xdt_(_):
                    for half in range(2):
                        dve.wait_ge(tensor.done, tensor.at(f"xdt{half}"))
                        for i in range(2):
                            tile = 2 * half + i
                            dt = cols[:, tile, Q_IG:Q_IG + H].rearrange("p (h o) -> p h o", o=1).to_broadcast([P, H, HD])
                            m = dve.tensor_tensor(xdt[:, tile, :].rearrange("p (h d) -> p h d", h=H),
                                                  bank[2 + half][:, i * GW:(i + 1) * GW].rearrange("p (h d) -> p h d", h=H), dt, ALU.mult)
                        m.then_inc(vector.done, vector.step(f"xdt{half}"))

                def decayed(h, kind, scores, scale):
                    dve.wait_ge(tensor.done, tensor.at(f"{kind}_r{h}"))
                    before = f"{kind}_e{h - 1}" if h else ("ssd_e3" if kind == "ml" else None)
                    if before:
                        dve.wait_ge(scalar.done, scalar.at(before))
                    mask = C["neg_col"].rearrange("p (o t) -> p o t", o=1).to_broadcast([P, NT, P])
                    dve.tensor_tensor(diag[:, :, :], bank[5][:, :].rearrange("p (i t) -> p i t", i=NT), mask, ALU.add).then_inc(vector.done, vector.step(f"{kind}_x{h}"))
                    dve.wait_ge(scalar.done, scalar.at(f"{kind}_e{h}"))
                    dve.wait_ge(tensor.done, tensor.at(scores))
                    for b, n in enumerate((512, 512, 256)):
                        part = tri[:, h % 2, 512 * b:512 * b + n]
                        m = dve.scalar_tensor_tensor(part, bank[2 + b][:, 0:n], scale, part, ALU.mult, ALU.mult)
                    m.then_inc(vector.done, vector.step(f"{kind}_w{h}"))

                def ssd_a(h):
                    decayed(h, "ssd", f"ssd_s{h - h % 2}", 1.0)

                def ssd_b(h):
                    if h % 2:
                        j = h // 2
                        dve.wait_ge(tensor.done, tensor.at(f"ssd_y{h}"))
                        dve.wait_ge(tensor.done, tensor.at("xdt1"))
                        dve.scalar_tensor_tensor(ssd_y[:, j, :], cv[f"x{j}"], pcol("d_skip", j), bank[6][:, :], ALU.mult, ALU.add).then_inc(vector.done, vector.step(f"ssd_y{j}"))

                def ml_a(h):
                    decayed(h, "ml", f"ml_s{h}", HEAD_SCALE)

                def ml_b(h):
                    lo, hi = HD * (h % 2), HD * (h % 2) + HD
                    dve.wait_ge(scalar.done, scalar.at(f"ml_abs{h}"))
                    dve.wait_ge(tensor.done, tensor.at(f"ml_f{h}"))
                    dve.tensor_tensor(absden[HD:P, :], absden[HD:P, :], bank[7][HD:P, :], ALU.max).then_inc(vector.done, vector.step(f"ml_d{h}"))
                    dve.wait_ge(vector.done, vector.n)
                    dve.reciprocal(absden[HD:P, :], absden[HD:P, :]).then_inc(vector.done, vector.step())
                    dve.wait_ge(vector.done, vector.n)
                    dve.tensor_tensor(ml_h[lo:hi, h // 2, :], bank[6][0:HD, :], absden[HD:P, :], ALU.mult).then_inc(vector.done, vector.step(f"ml_y{h}"))

                def mla_norm(_):
                    dve.wait_ge(scalar.done, scalar.at("rstd_cq_ms"))
                    for j in range(2):
                        dve.scalar_tensor_tensor(cq[:, j, :], cq[:, j, :], pcol("q_g", j), rstd, ALU.mult, ALU.mult).then_inc(vector.done, vector.step(f"cq_n{j}"))
                    dve.scalar_tensor_tensor(ckv[:, :], ckv[:, :], pcol("kv_g"), absden, ALU.mult, ALU.mult).then_inc(vector.done, vector.step("ckv_n"))

                def mla_up(_):
                    kr = slice(Q_KR, P)
                    dve.tensor_tensor(tmp[kr, :], u[kr, :], cos_t[kr, :], ALU.mult).then_inc(vector.done, vector.step())
                    dve.wait_ge(x_kept, 16)
                    dve.wait_ge(tensor.done, tensor.at("k_swap"))
                    dve.tensor_tensor(au[kr, :], bank[7][kr, :], sin_t[kr, :], ALU.mult).then_inc(vector.done, vector.step("k_rot"))
                    dve.wait_ge(vector.done, vector.n)
                    for h in range(H):
                        dve.tensor_tensor(k_mla[HD:96, h, :], tmp[kr, :], au[kr, :], ALU.add).then_inc(vector.done, vector.step(f"mla_k{h}"))
                        dve.wait_ge(vector.done, vector.n)
                    dve.wait_ge(scalar.done, scalar.at("q_up2"))
                    dve.tensor_tensor(q_cos, q_pe, cos_t[:, :], ALU.mult).then_inc(vector.done, vector.step())
                    dve.wait_ge(tensor.done, tensor.at("q_swap"))
                    dve.tensor_tensor(tmp[:, :], bank[7][:, :], sin_t[:, :], ALU.mult).then_inc(vector.done, vector.step("q_rot"))
                    dve.wait_ge(vector.done, vector.n)
                    for h in range(H):
                        r = slice(32 * h, 32 * h + 32)
                        dve.tensor_tensor(q_mla[HD:96, h, :], q_cos[r, :], tmp[r, :], ALU.add).then_inc(vector.done, vector.step(f"mla_q{h}"))

                def att_a(a):
                    kind, h = a
                    scale = HEAD_SCALE if kind == "moba" else MLA_SCALE
                    dve.wait_ge(tensor.done, tensor.at(f"att_s{a}"))
                    m = mx[:, h % 2, :]
                    for i in range(NT):
                        b, off = BANK_OF[NT - 1 - i]
                        ins = dve.reduce_max(m[:, i:i + 1], bank[2 + b][:, off:off + (i + 1) * P], AX.X)
                        ins.then_inc(vector.done, vector.step())
                    dve.wait_ge(vector.done, vector.n)
                    dve.tensor_scalar(m[:, NT:2 * NT], m[:, 0:NT], -scale, None, ALU.mult).then_inc(vector.done, vector.step(f"att_m{a}"))

                def att_e(a):
                    m, h = mx[:, a[1] % 2, :], a[1]
                    dve.wait_ge(scalar.done, scalar.at(f"att_e{a}"))
                    dve.reciprocal(m[:, 3 * NT:4 * NT], m[:, 2 * NT:3 * NT]).then_inc(vector.done, vector.step())
                    dve.wait_ge(vector.done, vector.n)
                    for i in (3, 2, 0, 1):
                        at, n = PACK[NT - 1 - i], (i + 1) * P
                        part = tri[:, h % 2, at:at + n]
                        dve.tensor_scalar(part, part, m[:, 3 * NT + i:3 * NT + i + 1], None, ALU.mult).then_inc(vector.done, vector.step(f"att_p{i}{a}"))

                def att_b(a):
                    n = unit_at[a[0]] + a[1] - 1 - 2 * H
                    if n >= 0:
                        dve.wait_ge(tensor.done, tensor.at(f"att_y{(('moba', 'mla')[n // H], n % H)}"))
                    dve.wait_ge(tensor.done, tensor.at(f"att_t1{a}"))
                    dve.tensor_copy(probT[:, 0:3, 2 * P:3 * P], bank[7][:, 0:3 * P].rearrange("p (j t) -> p j t", j=3)).then_inc(vector.done, vector.step())
                    dve.tensor_copy(probT[:, 0, 0:P], bank[7][:, 3 * P:T]).then_inc(vector.done, vector.step(f"att_t1{a}"))

                def out_high(n):
                    dve.wait_ge(tensor.done, tensor.at("mo1"))
                    dve.wait_ge(w_out_in[n][0], w_out_in[n][1])
                    dve.tensor_copy(out_hi[:, 2 * n:2 * n + 2, :], w_out_at[n].rearrange("p (k d) -> p k d", d=D)).then_inc(vector.done, vector.step(f"out_hi{n}"))

                def out_split(j):
                    dve.wait_ge(scalar.done, scalar.at("att_y('moba', 1)"))
                    dve.tensor_copy(mixed_hi[:, 2 * j:2 * j + 2, :], mixed[:, 2 * j:2 * j + 2, :]).then_inc(vector.done, vector.step())
                    dve.wait_ge(vector.done, vector.n)
                    dve.tensor_tensor(mixed_lo[:, 2 * j:2 * j + 2, :], mixed[:, 2 * j:2 * j + 2, :], mixed_hi[:, 2 * j:2 * j + 2, :].bitcast(F32), ALU.subtract)\
                        .then_inc(vector.done, vector.step(f"mixed_lo{j}"))

                def fin_c(_):
                    dve.wait_ge(scalar.done, scalar.at("rstd_ms0"))
                    dve.wait_ge(gpsimd.done, gpsimd.at("ml_sq"))
                    for j in range(4):
                        y, gain = (ssd_y, "ssm_g") if j < 2 else (ml_h, "ml_g")
                        dve.scalar_tensor_tensor(mixed[:, 2 + j, :], y[:, j % 2, :], pcol(gain, j % 2), rs[:, j, :], ALU.mult, ALU.mult).then_inc(vector.done, vector.step(f"n{j}"))

                def out(_):
                    dve.wait_ge(x_again, 16)
                    for i in range(NT):
                        dve.wait_ge(tensor.done, tensor.at(f"out{i}"))
                        for half in range(2):
                            part = x_tm[:, i, half * 512:(half + 1) * 512]
                            m = dve.tensor_tensor(part, part, bank[2 * i + half][:, :], ALU.add)
                        m.then_inc(vector.done, vector.step(f"x{i}"))
                        normalise(dve, scalar, vector, x_tm[:, i, :], h_tm[:, i, :], ms, i)

                do = dict(norm=norm, proj=proj, gates_a=gates_a, gates_b=gates_b, gate_cols=gate_cols, xdt=xdt_, ssd_a=ssd_a, ssd_b=ssd_b,
                          ml_a=ml_a, ml_b=ml_b, att_a=att_a, att_e=att_e, att_b=att_b, mla_norm=mla_norm, mla_up=mla_up,
                          fin_c=fin_c, out_high=out_high, out_split=out_split, out=out)
                for op, arg in plan:
                    if op in do:
                        do[op](arg)

            @block.gpsimd
            def _(pool):
                pool.memset(zero[:, :], 0.0).then_inc(gpsimd.done, gpsimd.step("zero"))
                pool.memset(raw[:, :, 0:3], 0.0).then_inc(gpsimd.done, gpsimd.step("pads"))
                for n, name in enumerate(UNITS):
                    if n == 3:
                        pool.memset(zeros[:, :], 0.0).then_inc(gpsimd.done, gpsimd.step("zeros"))
                        pool.memset(v_aug[:, :, :, HD:P], 1.0).then_inc(gpsimd.done, gpsimd.step("ones"))
                    slot, at = SLOTS.index(name.rstrip("01")), P if name[-1] == "1" else 0
                    pool.wait_ge(scalar.done, scalar.at(f"hi{n}"))
                    pool.tensor_tensor(w_lo[:, n % 2, :, :], ring[:, slot % 2, :, at:at + P], w_hi[:, n % 2, :, :].bitcast(F32), ALU.subtract)\
                        .then_inc(gpsimd.done, gpsimd.step(f"lo{n}"))
                    if name == UNITS[UNITS.index("cq1") + 2]:
                        pool.wait_ge(scalar.done, scalar.at("cq1"))
                        pool.wait_ge(tensor.done, tensor.at("ssd_s2"))
                        pool.tensor_tensor(cq_sq, cq, cq, ALU.mult).then_inc(gpsimd.done, gpsimd.step("cq_sq"))
                    if name == UNITS[UNITS.index("ckv") + 2]:
                        pool.wait_ge(scalar.done, scalar.at("ckv"))
                        pool.tensor_tensor(ckv_sq, ckv[:, :], ckv[:, :], ALU.mult).then_inc(gpsimd.done, gpsimd.step("ckv_sq"))
                pool.wait_ge(scalar.done, scalar.at("z1"))
                pool.wait_ge(vector.done, vector.at("ssd_y1"))
                pool.tensor_tensor(ssd_y, ssd_y, zs, ALU.mult).then_inc(gpsimd.done, gpsimd.step())
                pool.wait_ge(gpsimd.done, gpsimd.n)
                pool.wait_ge(scalar.done, scalar.at("sig_z"))
                pool.tensor_tensor(ssd_y, ssd_y, sig_z, ALU.mult).then_inc(gpsimd.done, gpsimd.step())
                pool.wait_ge(gpsimd.done, gpsimd.n)
                pool.wait_ge(tensor.done, tensor.at("ckv_ms"))
                pool.tensor_tensor(ssd_sq, ssd_y, ssd_y, ALU.mult).then_inc(gpsimd.done, gpsimd.step("ssd_sq"))
                pool.wait_ge(scalar.done, scalar.at("sig_o"))
                pool.wait_ge(vector.done, vector.at("ml_y3"))
                pool.tensor_tensor(ml_h, ml_h, os_, ALU.mult).then_inc(gpsimd.done, gpsimd.step())
                pool.wait_ge(gpsimd.done, gpsimd.n)
                pool.tensor_tensor(ml_sq, ml_h, ml_h, ALU.mult).then_inc(gpsimd.done, gpsimd.step("ml_sq"))
                for n in range(2):
                    pool.wait_ge(vector.done, vector.at(f"out_hi{n}"))
                    pool.tensor_tensor(out_lo[:, 2 * n:2 * n + 2, :], w_out_at[n].rearrange("p (k d) -> p k d", d=D),
                                       out_hi[:, 2 * n:2 * n + 2, :].bitcast(F32), ALU.subtract).then_inc(gpsimd.done, gpsimd.step(f"out_lo{n}"))
        clear(nc, steps, sems)
        record(seen, steps)


def moe(nc, A, known, seen, layer, bank, C, ccols, token_bf, par, pcol, x_tm, h_tm, ms, eps):
    with ExitStack() as ctx:
        def sb(name, shape, dt=F32):
            return ctx.enter_context(nc.sbuf_tensor(name, shape, dt))

        h2T = sb("h2T", [P, KD, T])
        wring = sb("wring", [P, 2, 3, 2048])
        xe = sb("xe", [P, 2, D])
        xeT = sb("xeT", [P, 2, KD, P])
        act_g = sb("act_g", [P, 2, DE])
        hid = sb("hid", [P, 2, DE])
        hidT = sb("hidT", [P, 2, 2, P])
        ye = sb("ye", [P, 2, D])
        w_rt = sb("w_rt", [P, KD, NR])
        logitsT = sb("logitsT", [P, T])
        lg = sb("lg", [P, NT, NR])
        sm = sb("sm", [P, 24, NT])
        oh_g = sb("oh_g", [P, NT, NG])
        oh_e = sb("oh_e", [P, 2, NT, EG])
        el = sb("el", [P, NT, EG])
        tmp4 = sb("tmp4", [P, NT, NG])
        tmp16 = sb("tmp16", [P, NT, NE])
        chosen = sb("chosen", [P, 3, NT, NE])
        place = sb("place", [P, NT, NE])
        match = sb("match", [P, 2, NT, P], BF16)
        idx1 = sb("idx1", [P, 2], U32)
        rows_of = sb("rows_of", [P, 2, NT], U32)
        counts = sb("counts", [P, 2 * NE + 1], I32)
        cf = sb("cf", [P, 4, NE])
        weight = lambda c: sm[:, 8 + c, :]

        route_and_experts(nc, A, known, seen, layer, bank, C, ccols, token_bf, par, pcol, locals())
        most = nc.values_load(counts[0:1, NE:NE + 1], min_val=0, max_val=T)
        with nc.If(most > CAP):
            with nc.Fori(1, T // CAP) as again:
                with nc.Fori(0, NE) as e:
                    n = nc.values_load(counts[0:1, bass.ds(e, 1)], min_val=0, max_val=T)
                    base = nc.values_load(counts[0:1, bass.ds(e + NE + 1, 1)], min_val=NE, max_val=NE + SPARE - T // CAP + 1)
                    with nc.If(n > again * CAP):
                        one_pass(nc, A, known, seen, layer, e, again, base, bank, C, token_bf, pcol, locals())
                    nc.all_engine_barrier()
            nc.all_engine_barrier()
        nc.all_engine_barrier()
        combine(nc, A, known, seen, rows_of, weight, xe, ye, h2T, x_tm, h_tm, ms, eps)


def route_and_experts(nc, A, known, seen, layer, bank, C, ccols, token_bf, par, pcol, B):
    h_tm, h2T, wring, xe, xeT, act_g, hid, hidT, ye = (B[n] for n in ("h_tm", "h2T", "wring", "xe", "xeT", "act_g", "hid", "hidT", "ye"))
    w_rt, lg, sm, oh_g, oh_e, el, tmp4, tmp16, chosen, place = (B[n] for n in ("w_rt", "lg", "sm", "oh_g", "oh_e", "el", "tmp4", "tmp16", "chosen", "place"))
    match, idx1, rows_of, counts, weight = (B[n] for n in ("match", "idx1", "rows_of", "counts", "weight"))
    cf, logitsT = B["cf"], B["logitsT"]
    rank = ccols[:, COLS["rank"][0]:COLS["rank"][0] + EG].rearrange("p (o e) -> p o e", o=1).to_broadcast([P, NT, EG])
    first_row1 = ccols[:, COLS["first_row"][0]:COLS["first_row"][0] + NE]
    first_row = first_row1.rearrange("p (o e) -> p o e", o=1).to_broadcast([P, NT, NE])
    S_ = lambda i: sm[:, i, :]
    places = bank[6][:, 0:(NT + 1) * NE]

    def each(v, n):
        return v.rearrange("p (i o) -> p i o", o=1).to_broadcast([P, NT, n])

    with ExitStack() as ctx:
        tensor, scalar, vector, gpsimd = steps = engine_steps(nc, ctx, known, "moe")
        names = ("router_in", "h_stored", "matched", "found", "turned", "turned_out", "gu", "gated", "hidden", "hid_turned", "hid_out",
                 "down", "y_low", "y_high", "idx_at", "xe_in0", "xe_in1", "y_stored0", "y_stored1",
                 "w_in00", "w_in01", "w_in02", "w_in10", "w_in11", "w_in12")
        Q = {n: ctx.enter_context(nc.semaphore(n)) for n in names}

        def wait(eng, name, n):
            if isinstance(n, int) and n <= 0:
                return
            eng.wait_ge(Q[name], n)

        with nc.allow_low_precision(reason="counts below 2 ** 24 are exact in float32 and as integers"), nc.Block() as block:
            @block.sync
            def _(sp):
                sp.dma_start(w_rt[:, :, :], A["w_router"][bass.ds(layer, 1), :, :, :].rearrange("o p k n -> (o p) k n")).then_inc(Q["router_in"], 16)

                def load(e, two, parts):
                    for part in parts:
                        src = A["w_moe"][bass.ds(layer * NE + e, 1), part, :, :].rearrange("o p n -> (o p) n")
                        sp.dma_start(wring[:, two, part, :], src).then_inc(Q[f"w_in{two}{part}"], 16)

                sp.dma_start(A["h2"].rearrange("(i p) d -> p i d", p=P), h_tm).then_inc(Q["h_stored"], 16)
                load(0, 0, (0, 1, 2))
                load(1, 1, (0, 1, 2))

                def step(e, two, before):
                    static_last = isinstance(e, int) and e + 2 >= NE
                    if not static_last:
                        wait(sp, "gu", e + 1)
                        load(e + 2, two, (0, 1))
                        wait(sp, "down", e + 1)
                        load(e + 2, two, (2,))
                    wait(sp, "y_low", e + 1)
                    wait(sp, "y_high", e + 1)
                    sp.dma_start(A["y"][bass.ds(e * CAP, CAP), :], ye[:, two, :]).then_inc(Q[f"y_stored{two}"], 16)

                step(0, 0, 0)
                with sp.Fori(0, NE // 2 - 2) as n:
                    step(2 * n + 1, 1, n)
                    step(2 * n + 2, 0, n + 1)
                step(NE - 3, 1, NE // 2 - 2)
                step(NE - 2, 0, NE // 2 - 1)
                step(NE - 1, 1, NE // 2 - 1)
                for two in range(2):
                    sp.wait_ge(Q[f"y_stored{two}"], 16 * (NE // 2))
                sp.wait_ge(Q["h_stored"], 16)

            @block.gpsimd
            def _(pool):
                pool.memset(cf[:, 3, :], 0.0).then_inc(gpsimd.done, gpsimd.step("zeros"))

                pool.wait_ge(Q["h_stored"], 16)
                for e in range(NE):
                    wait(pool, "idx_at", e + 1)
                    pool.indirect_dma_start(xe[:, e % 2, :], None, A["h2"], bass.IndirectOffsetOnAxis(ap=idx1[:, e % 2:e % 2 + 1], axis=0))\
                        .then_inc(Q[f"xe_in{e % 2}"], 16)
                for two in range(2):
                    pool.wait_ge(Q[f"xe_in{two}"], 16 * (NE // 2))
                forget(pool, Q["xe_in0"], Q["xe_in1"])

            @block.tensor
            def _(pe):

                def mm(out, lhsT, rhs, start, stop):
                    return pe.matmul(out, lhsT, rhs, start=start, stop=stop, skip_group_check=True)

                for k in range(KD):
                    for i in range(NT):
                        m = pe.transpose(bank[k][:, i * P:(i + 1) * P], h_tm[:, i, k * P:(k + 1) * P], C["ident"])
                    m.then_inc(tensor.done, tensor.step(f"hT{k}"))
                pe.wait_ge(Q["router_in"], 16)
                for k in range(KD):
                    engine = (scalar, vector)[k % 2]
                    pe.wait_ge(engine.done, engine.at(f"hT{k}"))
                    m = mm(bank[0][0:NR, :], w_rt[:, k, :], h2T[:, k, :], k == 0, k == KD - 1)
                m.then_inc(tensor.done, tensor.step("logitsT"))
                pe.wait_ge(scalar.done, scalar.at("logitsT"))
                for i in range(NT):
                    m = pe.transpose(bank[1][:, i * NR:(i + 1) * NR], logitsT[0:NR, i * P:(i + 1) * P], C["ident"][0:NR, 0:NR])
                m.then_inc(tensor.done, tensor.step("logits"))
                pe.wait_ge(vector.done, vector.at("chosen"))
                for i in range(NT):
                    for j in range(i + 1):
                        mm(places[:, i * NE:(i + 1) * NE], C["before"] if j == i else C["ones"], chosen[:, 2, j, :], j == 0, j == i)
                for j in range(NT):
                    m = mm(places[:, NT * NE:NT * NE + NE], C["ones"], chosen[:, 2, j, :], j == 0, j == NT - 1)
                m.then_inc(tensor.done, tensor.step("places"))

                def find(e, two):
                    wait(pe, "matched", e + 1)
                    wait(pe, "idx_at", e)
                    for i in range(NT):
                        m = mm(bank[7][:, 2 * two:2 * two + 2], match[:, two, i, :], token_bf[:, i, :], i == 0, i == NT - 1)
                    m.then_inc(Q["found"], 1)

                def turn(e, two, times):
                    pe.wait_ge(Q[f"xe_in{two}"], 16 * (times + 1))
                    wait(pe, "turned_out", e)
                    for k in range(KD):
                        m = pe.transpose(bank[k // 4][:, (k % 4) * P:(k % 4 + 1) * P], xe[:, two, k * P:(k + 1) * P], C["ident"])
                    m.then_inc(Q["turned"], 1)

                def gate_up(e, two, times):
                    wait(pe, "turned_out", e + 1)
                    wait(pe, "hidden", e - 1)
                    for part in range(2):
                        pe.wait_ge(Q[f"w_in{two}{part}"], 16 * (times + 1))
                        for j in range(4):
                            m = mm(bank[2 + two][:, :], xeT[:, two, 4 * part + j, :], wring[:, two, part, j * 512:(j + 1) * 512],
                                   part + j == 0, part * j == 3)
                    m.then_inc(Q["gu"], 1)

                def down(e, two, times):
                    wait(pe, "hid_out", e + 1)
                    pe.wait_ge(Q[f"w_in{two}2"], 16 * (times + 1))
                    wait(pe, "y_low", e)
                    wait(pe, "y_high", e)
                    for half in range(2):
                        for f in range(2):
                            m = mm(bank[5 + half][:, :], hidT[:, two, f, :], wring[:, two, 2, f * D + half * 512:f * D + half * 512 + 512], f == 0, f == 1)
                    m.then_inc(Q["down"], 1)

                def turn_hidden(e, two, times):
                    wait(pe, "hidden", e + 1)
                    wait(pe, "hid_out", e)
                    for f in range(2):
                        m = pe.transpose(bank[4][:, f * P:(f + 1) * P], hid[:, two, f * P:(f + 1) * P], C["ident"])
                    m.then_inc(Q["hid_turned"], 1)

                find(0, 0)
                find(1, 1)
                turn(0, 0, 0)
                gate_up(0, 0, 0)
                turn(1, 1, 0)
                turn_hidden(0, 0, 0)

                def step(e, two, times, last=False):
                    gate_up(e, two, times)
                    if not last:
                        turn(e + 1, 1 - two, times + two)
                    down(e - 1, 1 - two, times - (1 - two))
                    if not (isinstance(e, int) and e + 2 >= NE):
                        find(e + 2, two)
                    turn_hidden(e, two, times)

                find(2, 0)
                step(1, 1, 0)
                step(2, 0, 1)
                with pe.Fori(1, NE // 2 - 2) as n:
                    step(2 * n + 1, 1, n)
                    step(2 * n + 2, 0, n + 1)
                step(NE - 3, 1, NE // 2 - 2)
                step(NE - 2, 0, NE // 2 - 1)
                step(NE - 1, 1, NE // 2 - 1, True)
                down(NE - 1, 1, NE // 2 - 1)

            @block.scalar
            def _(act):
                for k in range(0, KD, 2):
                    act.wait_ge(tensor.done, tensor.at(f"hT{k}"))
                    act.activation(h2T[:, k, :], bank[k][:, :], ACT.Identity, scale=pcol("g_ffn", k)).then_inc(scalar.done, scalar.step(f"hT{k}"))
                act.wait_ge(tensor.done, tensor.at("logitsT"))
                act.activation(logitsT[0:NR, :], bank[0][0:NR, :], ACT.Copy).then_inc(scalar.done, scalar.step("logitsT"))
                act.wait_ge(vector.done, vector.at("group_less_max"))
                act.activation(tmp4[:, :, :], tmp4[:, :, :], ACT.Exp).then_inc(scalar.done, scalar.step("group_exp"))
                act.wait_ge(vector.done, vector.at("second_less_first"))
                act.activation(S_(4), S_(4), ACT.Exp).then_inc(scalar.done, scalar.step("second_exp"))

                def gate(e, two, times):
                    wait(act, "gu", e + 1)
                    wait(act, "hidden", e - 1)
                    act.activation(act_g[:, two, :], bank[2 + two][:, 0:DE], ACT.Silu).then_inc(Q["gated"], 1)

                def hidden_out(e, two, times):
                    wait(act, "hid_turned", e + 1)
                    wait(act, "down", e - 1)
                    act.activation(hidT[:, two, :, :], bank[4][:, 0:DE].rearrange("p (f s) -> p f s", f=2), ACT.Copy).then_inc(Q["hid_out"], 1)

                def y_out(e, two, times):
                    wait(act, "down", e + 1)
                    if not (isinstance(e, int) and e < 2):
                        act.wait_ge(Q[f"y_stored{two}"], 16 * times)
                    act.activation(ye[:, two, 0:512], bank[5][:, :], ACT.Copy).then_inc(Q["y_low"], 1)

                gate(0, 0, 0)
                hidden_out(0, 0, 0)
                gate(1, 1, 0)
                y_out(0, 0, 0)
                hidden_out(1, 1, 0)
                gate(2, 0, 1)
                y_out(1, 1, 0)
                hidden_out(2, 0, 1)

                def step(e, two, times):
                    gate(e, two, times)
                    y_out(e - 1, 1 - two, times - (1 - two))
                    hidden_out(e, two, times)
                with act.Fori(1, NE // 2 - 1) as n:
                    step(2 * n + 1, 1, n)
                    step(2 * n + 2, 0, n + 1)
                step(NE - 1, 1, NE // 2 - 1)
                y_out(NE - 1, 1, NE // 2 - 1)

            @block.vector
            def _(dve):
                tt, ts, stt = dve.tensor_tensor, dve.tensor_scalar, dve.scalar_tensor_tensor
                for k in range(1, KD, 2):
                    dve.wait_ge(tensor.done, tensor.at(f"hT{k}"))
                    ts(h2T[:, k, :], bank[k][:, :], pcol("g_ffn", k), None, ALU.mult).then_inc(vector.done, vector.step(f"hT{k}"))
                dve.wait_ge(tensor.done, tensor.at("logits"))
                bias = par[:, PARAMS["router_b"][0]:PARAMS["router_b"][0] + NR].rearrange("p (o n) -> p o n", o=1).to_broadcast([P, NT, NR])
                tt(lg[:, :, :], bank[1][:, 0:NT * NR].rearrange("p (i n) -> p i n", i=NT), bias, ALU.add).then_inc(vector.done, vector.step())
                dve.wait_ge(vector.done, vector.n)

                def first_max(values, best, onehot):
                    dve.tensor_reduce(best, values, AX.X, ALU.max).then_inc(vector.done, vector.step())
                    dve.wait_ge(vector.done, vector.n)
                    tt(onehot, values, each(best, EG), ALU.is_equal).then_inc(vector.done, vector.step())
                    dve.wait_ge(vector.done, vector.n)
                    tt(onehot, onehot, rank, ALU.mult).then_inc(vector.done, vector.step())
                    dve.wait_ge(vector.done, vector.n)
                    dve.tensor_reduce(S_(1), onehot, AX.X, ALU.max).then_inc(vector.done, vector.step())
                    dve.wait_ge(vector.done, vector.n)
                    tt(onehot, onehot, each(S_(1), EG), ALU.is_equal).then_inc(vector.done, vector.step())
                    dve.wait_ge(vector.done, vector.n)

                first_max(lg[:, :, 0:NG], S_(0), oh_g[:, :, :])
                tt(tmp4[:, :, :], lg[:, :, 0:NG], each(S_(0), NG), ALU.subtract).then_inc(vector.done, vector.step("group_less_max"))
                for g_ in range(NG):
                    lg_g = lg[:, :, NG + g_ * EG:NG + (g_ + 1) * EG]
                    one = oh_g[:, :, g_:g_ + 1].to_broadcast([P, NT, EG])
                    if g_ == 0:
                        tt(el[:, :, :], lg_g, one, ALU.mult).then_inc(vector.done, vector.step())
                        dve.wait_ge(vector.done, vector.n)
                    else:
                        tt(oh_e[:, 0, :, :], lg_g, one, ALU.mult).then_inc(vector.done, vector.step())
                        dve.wait_ge(vector.done, vector.n)
                        tt(el[:, :, :], el[:, :, :], oh_e[:, 0, :, :], ALU.add).then_inc(vector.done, vector.step())
                        dve.wait_ge(vector.done, vector.n)
                first_max(el[:, :, :], S_(2), oh_e[:, 0, :, :])
                stt(el[:, :, :], oh_e[:, 0, :, :], NEG, el[:, :, :], ALU.mult, ALU.add).then_inc(vector.done, vector.step())
                dve.wait_ge(vector.done, vector.n)
                first_max(el[:, :, :], S_(3), oh_e[:, 1, :, :])
                tt(S_(4), S_(3), S_(2), ALU.subtract).then_inc(vector.done, vector.step("second_less_first"))
                for c in range(2):
                    for g_ in range(NG):
                        m = tt(chosen[:, c, :, g_ * EG:(g_ + 1) * EG], oh_e[:, c, :, :], oh_g[:, :, g_:g_ + 1].to_broadcast([P, NT, EG]), ALU.mult)
                        m.then_inc(vector.done, vector.step())
                dve.wait_ge(vector.done, vector.n)
                tt(chosen[:, 2, :, :], chosen[:, 0, :, :], chosen[:, 1, :, :], ALU.add).then_inc(vector.done, vector.step("chosen"))
                dve.wait_ge(vector.done, vector.n)
                dve.wait_ge(tensor.done, tensor.at("places"))
                pos = places[:, 0:NT * NE].rearrange("p (i e) -> p i e", i=NT)
                stt(place[:, :, :], pos, 1.0, chosen[:, 2, :, :], ALU.add, ALU.mult).then_inc(vector.done, vector.step())
                dve.wait_ge(vector.done, vector.n)
                ts(place[:, :, :], place[:, :, :], -1.0, None, ALU.add).then_inc(vector.done, vector.step("place"))
                dve.wait_ge(vector.done, vector.n)
                def match_tokens(e, two):
                    wait(dve, "found", e - 1)
                    iota = C["iota"].rearrange("p (o s) -> p o s", o=1).to_broadcast([P, NT, P])
                    at = place[:, :, e:e + 1] if isinstance(e, int) else place[:, :, bass.ds(e, 1)]
                    tt(match[:, two, :, :], iota, at.to_broadcast([P, NT, P]), ALU.is_equal).then_inc(Q["matched"], 1)

                def index(e, two, times):
                    wait(dve, "found", e + 1)
                    if not (isinstance(e, int) and e < 2):
                        dve.wait_ge(Q[f"xe_in{two}"], 16 * times)
                    dve.tensor_reduce(idx1[:, two:two + 1], bank[7][:, 2 * two:2 * two + 2], AX.X, ALU.add).then_inc(Q["idx_at"], 1)

                match_tokens(0, 0)
                match_tokens(1, 1)
                index(0, 0, 0)
                index(1, 1, 0)
                dve.wait_ge(scalar.done, scalar.at("group_exp"))
                dve.reduce_sum(S_(5), tmp4[:, :, :], AX.X).then_inc(vector.done, vector.step())
                dve.wait_ge(vector.done, vector.n)
                dve.wait_ge(scalar.done, scalar.at("second_exp"))
                ts(S_(6), S_(4), 1.0, None, ALU.add).then_inc(vector.done, vector.step())
                dve.wait_ge(vector.done, vector.n)
                tt(S_(6), S_(6), S_(5), ALU.mult).then_inc(vector.done, vector.step())
                dve.wait_ge(vector.done, vector.n)
                dve.reciprocal(weight(0), S_(6)).then_inc(vector.done, vector.step())
                dve.wait_ge(vector.done, vector.n)
                tt(weight(1), weight(0), S_(4), ALU.mult).then_inc(vector.done, vector.step())
                dve.wait_ge(vector.done, vector.n)
                dve.tensor_copy(counts[:, 0:NE], places[:, NT * NE:NT * NE + NE]).then_inc(vector.done, vector.step())
                dve.reduce_max(counts[:, NE:NE + 1], places[:, NT * NE:NT * NE + NE], AX.X).then_inc(vector.done, vector.step())
                dve.wait_ge(vector.done, vector.n)
                dve.wait_ge(gpsimd.done, gpsimd.at("zeros"))
                dve.tensor_copy(cf[:, 0, :], counts[:, 0:NE]).then_inc(vector.done, vector.step())
                dve.wait_ge(vector.done, vector.n)
                ts(cf[:, 1, :], cf[:, 0, :], float(CAP), None, ALU.is_gt).then_inc(vector.done, vector.step())
                dve.wait_ge(vector.done, vector.n)
                for again in range(2, T // CAP):
                    stt(cf[:, 1, :], cf[:, 0, :], float(again * CAP), cf[:, 1, :], ALU.is_gt, ALU.add).then_inc(vector.done, vector.step())
                    dve.wait_ge(vector.done, vector.n)
                dve.tensor_tensor_scan(cf[:, 2, :], cf[:, 1, :], cf[:, 3, :], float(NE), ALU.add, ALU.add).then_inc(vector.done, vector.step())
                dve.wait_ge(vector.done, vector.n)
                tt(cf[:, 2, :], cf[:, 2, :], cf[:, 1, :], ALU.subtract).then_inc(vector.done, vector.step())
                dve.wait_ge(vector.done, vector.n)
                dve.tensor_copy(counts[:, NE + 1:2 * NE + 1], cf[:, 2, :]).then_inc(vector.done, vector.step())
                dve.wait_ge(vector.done, vector.n)
                ts(cf[:, 2, :], cf[:, 2, :], float(CAP), -float(CAP), ALU.mult, ALU.add).then_inc(vector.done, vector.step())
                dve.wait_ge(vector.done, vector.n)
                tt(cf[:, 2, :], cf[:, 2, :], first_row1, ALU.subtract).then_inc(vector.done, vector.step())
                dve.wait_ge(vector.done, vector.n)
                further = cf[:, 2, :].rearrange("p (o e) -> p o e", o=1).to_broadcast([P, NT, NE])
                stt(tmp16[:, :, :], place[:, :, :], float(CAP), further, ALU.is_ge, ALU.mult).then_inc(vector.done, vector.step())
                dve.wait_ge(vector.done, vector.n)
                tt(tmp16[:, :, :], tmp16[:, :, :], place[:, :, :], ALU.add).then_inc(vector.done, vector.step())
                dve.wait_ge(vector.done, vector.n)
                tt(tmp16[:, :, :], tmp16[:, :, :], first_row, ALU.add).then_inc(vector.done, vector.step())
                dve.wait_ge(vector.done, vector.n)
                for c in range(2):
                    tt(chosen[:, c, :, :], chosen[:, c, :, :], tmp16[:, :, :], ALU.mult).then_inc(vector.done, vector.step())
                    dve.wait_ge(vector.done, vector.n)
                    dve.tensor_reduce(rows_of[:, c, :], chosen[:, c, :, :], AX.X, ALU.add).then_inc(vector.done, vector.step())

                def turned_out(e, two, times):
                    wait(dve, "turned", e + 1)
                    wait(dve, "gu", e - 1)
                    for half in range(2):
                        gain = par[:, PARAMS["g_ffn"][0] + 4 * half:PARAMS["g_ffn"][0] + 4 * half + 4].rearrange("p (k o) -> p k o", o=1)
                        m = tt(xeT[:, two, 4 * half:4 * half + 4, :], bank[half][:, :].rearrange("p (k s) -> p k s", k=4),
                               gain.to_broadcast([P, 4, P]), ALU.mult)
                    m.then_inc(Q["turned_out"], 1)

                def hidden(e, two, times):
                    wait(dve, "gated", e + 1)
                    wait(dve, "hid_turned", e - 1)
                    tt(hid[:, two, :], bank[2 + two][:, DE:2 * DE], act_g[:, two, :], ALU.mult).then_inc(Q["hidden"], 1)

                def y_out(e, two, times):
                    wait(dve, "down", e + 1)
                    if not (isinstance(e, int) and e < 2):
                        dve.wait_ge(Q[f"y_stored{two}"], 16 * times)
                    dve.tensor_copy(ye[:, two, 512:D], bank[6][:, :]).then_inc(Q["y_high"], 1)

                def step(e, two, times, ahead=True):
                    if ahead:
                        turned_out(e + 1, 1 - two, times + two)
                    more = not (isinstance(e, int) and e + 2 >= NE)
                    if more:
                        match_tokens(e + 2, two)
                    hidden(e, two, times)
                    if more:
                        index(e + 2, two, times + 1)
                    if not (isinstance(e, int) and e == 0):
                        y_out(e - 1, 1 - two, times - (1 - two))

                turned_out(0, 0, 0)
                step(0, 0, 0)
                step(1, 1, 0)
                step(2, 0, 1)
                with dve.Fori(1, NE // 2 - 2) as n:
                    step(2 * n + 1, 1, n)
                    step(2 * n + 2, 0, n + 1)
                step(NE - 3, 1, NE // 2 - 2)
                step(NE - 2, 0, NE // 2 - 1)
                step(NE - 1, 1, NE // 2 - 1, False)
                y_out(NE - 1, 1, NE // 2 - 1)
        clear(nc, steps, Q.values())
        record(seen, steps)


def one_pass(nc, A, known, seen, layer, e, again, base, bank, C, token_bf, pcol, B):
    wring, xe, xeT, act_g, hid, hidT, ye, place, match, idx1, par = (
        B[n] for n in ("wring", "xe", "xeT", "act_g", "hid", "hidT", "ye", "place", "match", "idx1", "par"))
    with ExitStack() as ctx:
        tensor, scalar, vector, gpsimd = steps = engine_steps(nc, ctx, known, "pass")
        loaded, gathered, stored = (ctx.enter_context(nc.semaphore(n)) for n in ("pass_loaded", "pass_gathered", "pass_stored"))
        with nc.allow_low_precision(reason="token numbers are exact in float32 and as integers"), nc.Block() as block:
            @block.sync
            def _(sp):
                for part in range(3):
                    sp.dma_start(wring[:, 0, part, :], A["w_moe"][bass.ds(layer * NE + e, 1), part, :, :].rearrange("o p n -> (o p) n")).then_inc(loaded, 16)
                sp.wait_ge(vector.done, vector.at("y"))
                sp.dma_start(A["y"][bass.ds((base + again - 1) * CAP, CAP), :], ye[:, 0, :]).then_inc(stored, 16)
                sp.wait_ge(stored, 16)

            @block.gpsimd
            def _(pool):
                pool.wait_ge(vector.done, vector.at("idx"))
                pool.indirect_dma_start(xe[:, 0, :], None, A["h2"], bass.IndirectOffsetOnAxis(ap=idx1[:, 0:1], axis=0)).then_inc(gathered, 16)
                pool.wait_ge(gathered, 16)
                forget(pool, gathered)

            @block.tensor
            def _(pe):

                def mm(out, lhsT, rhs, start, stop):
                    return pe.matmul(out, lhsT, rhs, start=start, stop=stop, skip_group_check=True)
                pe.wait_ge(vector.done, vector.at("match"))
                for i in range(NT):
                    m = mm(bank[7][:, 0:2], match[:, 0, i, :], token_bf[:, i, :], i == 0, i == NT - 1)
                m.then_inc(tensor.done, tensor.step("idx"))
                pe.wait_ge(gathered, 16)
                for k in range(KD):
                    m = pe.transpose(bank[k // 4][:, (k % 4) * P:(k % 4 + 1) * P], xe[:, 0, k * P:(k + 1) * P], C["ident"])
                m.then_inc(tensor.done, tensor.step("turned"))
                pe.wait_ge(loaded, 48)
                pe.wait_ge(vector.done, vector.at("turned"))
                for k in range(KD):
                    m = mm(bank[2][:, :], xeT[:, 0, k, :], wring[:, 0, k // 4, (k % 4) * 512:(k % 4 + 1) * 512], k == 0, k == KD - 1)
                m.then_inc(tensor.done, tensor.step("gu"))
                pe.wait_ge(vector.done, vector.at("hid"))
                for f in range(2):
                    m = pe.transpose(bank[4][:, f * P:(f + 1) * P], hid[:, 0, f * P:(f + 1) * P], C["ident"])
                m.then_inc(tensor.done, tensor.step("hid"))
                pe.wait_ge(vector.done, vector.at("hidT"))
                for half in range(2):
                    for f in range(2):
                        m = mm(bank[5 + half][:, :], hidT[:, 0, f, :], wring[:, 0, 2, f * D + half * 512:f * D + half * 512 + 512], f == 0, f == 1)
                m.then_inc(tensor.done, tensor.step("down"))

            @block.scalar
            def _(act):
                act.wait_ge(tensor.done, tensor.at("gu"))
                act.activation(act_g[:, 0, :], bank[2][:, 0:DE], ACT.Silu).then_inc(scalar.done, scalar.step("gate"))

            @block.vector
            def _(dve):
                iota = C["iota"].rearrange("p (o s) -> p o s", o=1).to_broadcast([P, NT, P])
                dve.tensor_scalar(B["tmp16"][:, :, 0:1], place[:, :, bass.ds(e, 1)], -float(CAP), None, ALU.add).then_inc(vector.done, vector.step())
                dve.wait_ge(vector.done, vector.n)
                dve.tensor_copy(place[:, :, bass.ds(e, 1)], B["tmp16"][:, :, 0:1]).then_inc(vector.done, vector.step())
                dve.wait_ge(vector.done, vector.n)
                dve.tensor_tensor(match[:, 0, :, :], iota, B["tmp16"][:, :, 0:1].to_broadcast([P, NT, P]), ALU.is_equal).then_inc(vector.done, vector.step("match"))
                dve.wait_ge(tensor.done, tensor.at("idx"))
                dve.tensor_reduce(idx1[:, 0:1], bank[7][:, 0:2], AX.X, ALU.add).then_inc(vector.done, vector.step("idx"))
                dve.wait_ge(tensor.done, tensor.at("turned"))
                for half in range(2):
                    gain = par[:, PARAMS["g_ffn"][0] + 4 * half:PARAMS["g_ffn"][0] + 4 * half + 4].rearrange("p (k o) -> p k o", o=1)
                    m = dve.tensor_tensor(xeT[:, 0, 4 * half:4 * half + 4, :], bank[half][:, :].rearrange("p (k s) -> p k s", k=4),
                                          gain.to_broadcast([P, 4, P]), ALU.mult)
                m.then_inc(vector.done, vector.step("turned"))
                dve.wait_ge(scalar.done, scalar.at("gate"))
                dve.tensor_tensor(hid[:, 0, :], bank[2][:, DE:2 * DE], act_g[:, 0, :], ALU.mult).then_inc(vector.done, vector.step("hid"))
                dve.wait_ge(tensor.done, tensor.at("hid"))
                dve.tensor_copy(hidT[:, 0, :, :], bank[4][:, 0:DE].rearrange("p (f s) -> p f s", f=2)).then_inc(vector.done, vector.step("hidT"))
                dve.wait_ge(tensor.done, tensor.at("down"))
                dve.tensor_copy(ye[:, 0, 0:512], bank[5][:, :]).then_inc(vector.done, vector.step())
                dve.tensor_copy(ye[:, 0, 512:D], bank[6][:, :]).then_inc(vector.done, vector.step("y"))
        clear(nc, steps, [loaded, gathered, stored])
        record(seen, steps)


def combine(nc, A, known, seen, rows_of, weight, xe, ye, h2T, x_tm, h_tm, ms, eps):
    spare = h2T[:, :, :].rearrange("p k t -> p (k t)").rearrange("p (n d) -> p n d", d=D)
    bufs = [xe[:, 0, :], xe[:, 1, :], ye[:, 0, :], ye[:, 1, :], *(spare[:, i, :] for i in range(4))]
    with ExitStack() as ctx:
        tensor, scalar, vector, gpsimd = steps = engine_steps(nc, ctx, known, "combine")
        got = [ctx.enter_context(nc.semaphore(f"result_in{n}")) for n in range(2 * NT)]
        with nc.Block() as block:
            @block.gpsimd
            def _(pool):
                for i in range(NT):
                    for c in range(2):
                        n = 2 * i + c
                        pool.indirect_dma_start(bufs[n], None, A["y"], bass.IndirectOffsetOnAxis(ap=rows_of[:, c, i:i + 1], axis=0)).then_inc(got[n], 16)
                for n in range(2 * NT):
                    pool.wait_ge(got[n], 16)
                forget(pool, *got)

            @block.vector
            def _(dve):
                for i in range(NT):
                    dve.wait_ge(got[2 * i], 16)
                    dve.scalar_tensor_tensor(x_tm[:, i, :], bufs[2 * i], weight(0)[:, i:i + 1], x_tm[:, i, :], ALU.mult, ALU.add).then_inc(vector.done, vector.step())
                    dve.wait_ge(vector.done, vector.n)
                    dve.wait_ge(got[2 * i + 1], 16)
                    dve.scalar_tensor_tensor(x_tm[:, i, :], bufs[2 * i + 1], weight(1)[:, i:i + 1], x_tm[:, i, :], ALU.mult, ALU.add).then_inc(vector.done, vector.step(f"x{i}"))
                    if i:
                        normalise(dve, scalar, vector, x_tm[:, i - 1, :], h_tm[:, i - 1, :], ms, i - 1)
                normalise(dve, scalar, vector, x_tm[:, NT - 1, :], h_tm[:, NT - 1, :], ms, NT - 1)

            @block.scalar
            def _(act):
                for i in range(NT):
                    act.wait_ge(vector.done, vector.at(f"x{i}"))
                    root_mean_square(act, scalar, x_tm[:, i, :], h_tm[:, i, :], ms, eps, i)
        clear(nc, steps, got)
        record(seen, steps)


def final_norm(nc, A, known, seen, h_tm):
    with ExitStack() as ctx:
        sb = lambda name, shape: ctx.enter_context(nc.sbuf_tensor(name, shape, F32))
        g_row, o = sb("g_row", [P, D]), sb("o", [P, NT, D])
        tensor, scalar, vector, gpsimd = steps = engine_steps(nc, ctx, known, "final")
        loaded, stored = (ctx.enter_context(nc.semaphore(n)) for n in ("g_loaded", "out_stored"))
        with nc.Block() as block:
            @block.sync
            def _(sp):
                sp.dma_start(g_row[:, :], A["final_norm_g"].partition_broadcast(P)).then_inc(loaded, 16)
                for i in range(NT):
                    sp.wait_ge(vector.done, vector.at(f"o{i}"))
                    sp.dma_start(A["out"][i * P:(i + 1) * P, :], o[:, i, :]).then_inc(stored, 16)
                sp.wait_ge(stored, 16 * NT)

            @block.vector
            def _(dve):
                dve.wait_ge(loaded, 16)
                for i in range(NT):
                    dve.tensor_tensor(o[:, i, :], h_tm[:, i, :], g_row[:, :], ALU.mult).then_inc(vector.done, vector.step(f"o{i}"))
        record(seen, steps)


def constants():
    r = np.arange(P)
    m = {
        "ident": np.eye(P), "neg_row": np.where(r[None, :] <= r[:, None], 0, NEG),
        "neg_col": np.where(r[None, :] >= r[:, None], 0, NEG),
        "avg128": np.full((P, P), 1 / 128), "avg256": np.full((P, P), 1 / 256),
        "avg64": (r[:, None] // HD == r[None, :] // HD) / HD, "swap": np.eye(P)[r ^ 16],
        "before": (r[:, None] < r[None, :]), "ones": np.ones((P, P)), "iota": np.broadcast_to(r[None, :], (P, P)),
    }
    const = np.stack([np.asarray(m[n], np.float32) for n in CONSTS], 1)
    inv = np.float32(10000.0) ** (-(np.arange(16, dtype=np.float32) * 2) / np.float32(32))
    cols = np.zeros((P, NCOLS), np.float32)
    cols[:, 0], cols[:, 1] = inv[r % 16], np.where(r % 32 < 16, -1, 1)
    token = np.stack([np.broadcast_to(P * np.arange(NT), (P, NT)), np.broadcast_to(r[:, None], (P, NT))], -1)
    for name, v in (("token", token.reshape(P, -1)), ("rank", EG - np.arange(EG)), ("first_row", CAP * np.arange(NE))):
        cols[:, COLS[name][0]:sum(COLS[name])] = v
    return np.ascontiguousarray(const), cols


def layout(i):
    a = {n: np.asarray(v) for n, v in i.items()}

    def tiles(w):
        return w.reshape(w.shape[0], -1, P, w.shape[-1]).transpose(0, 2, 1, 3)

    w_in = a["w_in"]
    slots = np.zeros((L, len(SLOTS), P, KD, 256), np.float32)
    for n, name in enumerate(SLOTS):
        if name == "small":
            continue
        width = 128 if name == "ckv" else 256
        slots[:, n, :, :, :width] = tiles(w_in[:, :, W_IN_AT[name]:W_IN_AT[name] + width])
    small = np.zeros((L, D, P), np.float32)
    for at, src, n in ((Q_DT, W_DT, H), (Q_IG, W_IG, H), (Q_FG, W_FG, H), (Q_KR, W_KR, 32)):
        small[:, :, at:at + n] = w_in[:, :, src:src + n]
    slots[:, SLOTS.index("small"), :, :, :P] = tiles(small)
    uq = a["mla_w_uq"].reshape(L, GW, H, 96)
    uq = np.concatenate([uq[..., :HD].reshape(L, GW, GW), uq[..., HD:].reshape(L, GW, P)], -1)
    ukv = a["mla_w_ukv"].reshape(L, P, H, P)
    ukv = np.concatenate([ukv[..., :HD].reshape(L, P, GW), ukv[..., HD:].reshape(L, P, GW)], -1)
    w_out = a["w_out"].reshape(L, 4, 2, P, D).transpose(0, 1, 3, 2, 4).reshape(L, 4, P, 2 * D)

    par = np.zeros((L, P, NPAR), np.float32)

    def put(name, cols):
        par[:, :, PARAMS[name][0]:PARAMS[name][0] + cols.shape[-1]] = cols

    columns = lambda v: v.reshape(L, -1, P).transpose(0, 2, 1)
    put("g_mix", columns(a["norm_mix_g"]))
    put("g_ffn", columns(a["norm_ffn_g"]))
    cw = np.concatenate([a["ssm_conv_w"], a["ml_conv_w"]], -1)
    put("conv_w", cw.reshape(L, 4, 10, P).transpose(0, 3, 2, 1).reshape(L, P, 40))
    put("conv_b", columns(np.concatenate([a["ssm_conv_b"], a["ml_conv_b"]], -1)))
    gate = np.zeros((L, P, 1), np.float32)
    for at, name in ((Q_DT, "ssm_dt_bias"), (Q_IG, "ml_ig_bias"), (Q_FG, "ml_fg_bias")):
        gate[:, at:at + H, 0] = a[name]
    put("gate_b", gate)
    log = np.zeros((L, P, 1), np.float32)
    log[:, 0:H, 0] = a["ssm_a_log"]
    put("a_log", log)
    put("d_skip", columns(np.repeat(a["ssm_d"], HD, -1)))
    put("ssm_g", columns(a["ssm_norm_g"]))
    put("ml_g", columns(a["ml_norm_g"]))
    put("q_g", columns(a["mla_q_norm_g"]))
    put("kv_g", columns(a["mla_kv_norm_g"]))
    rb = np.concatenate([a["moe_b_group"], a["moe_b_router"]], -1)
    put("router_b", np.broadcast_to(rb[:, None, :], (L, P, NG + NE)))
    router = np.concatenate([a["moe_w_group"], a["moe_w_router"]], -1)
    gu = np.concatenate([a["moe_w_gate"], a["moe_w_up"]], -1).reshape(L * NE, 2, 4, P, 2 * DE).transpose(0, 1, 3, 2, 4).reshape(L * NE, 2, P, 2048)
    dn = a["moe_w_down"].reshape(L * NE, 1, 2, P, D).transpose(0, 1, 3, 2, 4).reshape(L * NE, 1, P, 2048)
    const, ccols = constants()
    arrays = {"x": a["x"].reshape(T, D), "positions": a["positions"], "const": const, "ccols": ccols, "params": par,
              "w_router": tiles(router), "w_moe": np.concatenate([gu, dn], 1), "final_norm_g": a["final_norm_g"],
              "w_in": slots, "w_uq": tiles(uq), "w_ukv": ukv, "w_out": w_out}
    return {n: np.ascontiguousarray(v) for n, v in arrays.items()}


def program(nc, arrays, known):
    A = {n: nc.dram_tensor(f"in_{n}", v.shape, mybir.dt.from_np(v.dtype), kind="ExternalInput").ap() for n, v in arrays.items()}
    for name, rows in (("residual", T), ("h2", T), ("y", (NE + SPARE) * CAP)):
        A[name] = nc.dram_tensor(name, (rows, D), F32, kind="Internal").ap()
    A["out"] = nc.dram_tensor("out_0_dram", (T, D), F32, kind="ExternalOutput").ap()
    return build(nc, A, known)


def kernel(**inputs):
    import concourse.bacc as bacc
    from concourse.bass_utils import run_bass_kernel_spmd

    arrays = layout(inputs)
    known = program(bacc.Bacc("TRN2", target_bir_lowering=False, num_devices=1), arrays, None)
    nc = bacc.Bacc("TRN2", target_bir_lowering=False, num_devices=1)
    program(nc, arrays, known)
    r = run_bass_kernel_spmd(nc, [{f"in_{n}": v for n, v in arrays.items()}], core_ids=[0])
    return r.results[0]["out_0_dram"].reshape(1, T, D)
```
